# Optimizing a Trainium2 kernel written in Bass

```python
import functools
import jax, jax.numpy as jnp
from jax import lax
import numpy as np

D_MODEL = 2048
BATCH = 1
SEQ = 256
DEPTH = 1
DEC_BATCH = 8
DEC_SEQ = 8
PAST_LEN = 2048
PAGE_SIZE = 128

HEAD_DIM = 128
N_HEADS = D_MODEL // HEAD_DIM
N_KV_HEADS = 4
GROUP = N_HEADS // N_KV_HEADS
KV_W = N_KV_HEADS * HEAD_DIM
CMP_LEN = 32
CMP_STRIDE = 16
CMP_SUB = CMP_LEN // CMP_STRIDE
CMP_HID = HEAD_DIM
SLC_LEN = 64
SLC_TOP = 16
N_LOCAL_BLOCKS = 2
WINDOW = 512
WIN_BLK = 128
SLC_Q_CHUNK = 64
CONV_DIM = D_MODEL
CONV_W = 3
D_FF = 4 * D_MODEL
N_KV_KINDS = 4
RMS_EPS = 1e-6
NEG = -1e30
SCALE = HEAD_DIM ** -0.5
W_IN_SPLITS = (N_HEADS * HEAD_DIM,) + (KV_W,) * 6 + (3 * N_HEADS,) + (CONV_DIM,) * 3 + (D_MODEL,) * 2
W_IN_COLS = sum(W_IN_SPLITS)

kernel_name = "nsa_shortconv_gated_hybrid_step"

def rmsnorm(x, g):
    xf = x.astype(jnp.float32)
    y = xf * lax.rsqrt(jnp.mean(xf * xf, axis=-1, keepdims=True) + RMS_EPS)
    return (y * g.astype(jnp.float32)).astype(x.dtype)

def compress(k, w1, w2, pe):
    B, T = k.shape[:2]
    n_chunk = T // CMP_STRIDE
    chunks = k[:, :n_chunk * CMP_STRIDE].reshape(B, n_chunk, CMP_STRIDE, N_KV_HEADS, HEAD_DIM)
    w1s = w1.reshape(CMP_SUB, CMP_STRIDE, HEAD_DIM, CMP_HID)
    part = jnp.einsum('bcrkd,srdf->bcskf', chunks, w1s)
    nc = n_chunk - CMP_SUB + 1
    h = part[:, 0:nc, 0]
    for s in range(1, CMP_SUB):
        h = h + part[:, s:s + nc, s]
    h = h + jnp.einsum('srd,srdf->f', pe.reshape(CMP_SUB, CMP_STRIDE, HEAD_DIM), w1s)
    return jax.nn.gelu(h) @ w2

def cmp_attend(q, kc, vc, q_pos):
    nc = kc.shape[1]
    blk_end = jnp.arange(nc) * CMP_STRIDE + CMP_LEN - 1
    mask = blk_end[None, :] <= q_pos[:, None]
    s = jnp.einsum('bskgd,bckd->bkgsc', q, kc).astype(jnp.float32) * SCALE
    s = jnp.where(mask, s, NEG)
    p = jax.nn.softmax(s, axis=-1) * mask
    o = jnp.einsum('bkgsc,bckd->bskgd', p.astype(vc.dtype), vc)
    return o, p

def select_blocks(p_cmp, q_pos, n_blocks):
    pg = jnp.sum(p_cmp, axis=2)
    nc = pg.shape[-1]
    cs = jnp.arange(nc) * CMP_STRIDE
    sb = jnp.arange(n_blocks) * SLC_LEN
    ov = jnp.clip(jnp.minimum(cs[:, None] + CMP_LEN, sb[None, :] + SLC_LEN)
                  - jnp.maximum(cs[:, None], sb[None, :]), 0, None)
    m = (ov / CMP_STRIDE).astype(jnp.float32)
    score = jnp.einsum('bksc,cn->bksn', pg, m)
    cur = q_pos // SLC_LEN
    j = jnp.arange(n_blocks)
    valid = j[None, :] <= cur[:, None]
    forced = (j[None, :] == 0) | (j[None, :] > cur[:, None] - N_LOCAL_BLOCKS)
    score = jnp.where(valid, jnp.where(forced, jnp.inf, score), -jnp.inf)
    n_top = min(SLC_TOP, n_blocks)
    vals, idx = lax.top_k(score, n_top)
    return idx, vals > -jnp.inf

def slc_attend(q, kb, vb, idx, valid, q_pos):
    gather = jax.vmap(jax.vmap(lambda blocks, ix: blocks[ix]))
    kg = gather(kb, idx)
    vg = gather(vb, idx)
    kpos = idx[..., None] * SLC_LEN + jnp.arange(SLC_LEN)
    mask = valid[..., None] & (kpos <= q_pos[None, None, :, None, None])
    s = jnp.einsum('bskgd,bksnld->bksgnl', q, kg).astype(jnp.float32) * SCALE
    s = jnp.where(mask[:, :, :, None], s, NEG)
    p = jax.nn.softmax(s, axis=(-2, -1))
    return jnp.einsum('bksgnl,bksnld->bskgd', p.astype(vg.dtype), vg)

def nsa_global(q, k_cmp, v_cmp, k_slc, v_slc, q_pos, cw, chunked):
    kc = compress(k_cmp, cw[0], cw[1], cw[2])
    vc = compress(v_cmp, cw[3], cw[4], cw[5])
    o_cmp, p_cmp = cmp_attend(q, kc, vc, q_pos)
    B, T = k_slc.shape[:2]
    ns = -(-T // SLC_LEN)
    idx, valid = select_blocks(p_cmp, q_pos, ns)
    padw = ((0, 0), (0, ns * SLC_LEN - T), (0, 0), (0, 0))
    kb = jnp.pad(k_slc, padw).reshape(B, ns, SLC_LEN, N_KV_HEADS, HEAD_DIM).transpose(0, 3, 1, 2, 4)
    vb = jnp.pad(v_slc, padw).reshape(B, ns, SLC_LEN, N_KV_HEADS, HEAD_DIM).transpose(0, 3, 1, 2, 4)
    if chunked:
        S = q.shape[1]
        qc = min(SLC_Q_CHUNK, S)
        nq = S // qc
        n_top = idx.shape[-1]
        qs = q.reshape(B, nq, qc, N_KV_HEADS, GROUP, HEAD_DIM).swapaxes(0, 1)
        ids = idx.reshape(B, N_KV_HEADS, nq, qc, n_top).transpose(2, 0, 1, 3, 4)
        vls = valid.reshape(B, N_KV_HEADS, nq, qc, n_top).transpose(2, 0, 1, 3, 4)
        ps = q_pos.reshape(nq, qc)
        o = lax.map(lambda a: slc_attend(a[0], kb, vb, a[1], a[2], a[3]), (qs, ids, vls, ps))
        o_slc = o.swapaxes(0, 1).reshape(B, S, N_KV_HEADS, GROUP, HEAD_DIM)
    else:
        o_slc = slc_attend(q, kb, vb, idx, valid, q_pos)
    return o_cmp, o_slc

def window_prompt(q, k, v):
    B, S = k.shape[:2]
    blk = min(WIN_BLK, S)
    nb = S // blk
    nprev = -(-WINDOW // blk)
    span = (nprev + 1) * blk
    padw = ((0, 0), (nprev * blk, 0), (0, 0), (0, 0))
    kp = jnp.pad(k, padw).reshape(B, nb + nprev, blk, N_KV_HEADS, HEAD_DIM)
    vp = jnp.pad(v, padw).reshape(B, nb + nprev, blk, N_KV_HEADS, HEAD_DIM)
    kband = jnp.concatenate([kp[:, j:j + nb] for j in range(nprev + 1)], axis=2)
    vband = jnp.concatenate([vp[:, j:j + nb] for j in range(nprev + 1)], axis=2)
    qb = q.reshape(B, nb, blk, N_KV_HEADS, GROUP, HEAD_DIM)
    qpos = jnp.arange(S).reshape(nb, blk)
    kpos = (jnp.arange(nb) * blk - nprev * blk)[:, None] + jnp.arange(span)[None, :]
    diff = qpos[:, :, None] - kpos[:, None, :]
    mask = (kpos[:, None, :] >= 0) & (diff >= 0) & (diff < WINDOW)
    s = jnp.einsum('bnqkgd,bnckd->bnkgqc', qb, kband).astype(jnp.float32) * SCALE
    s = jnp.where(mask[None, :, None, None], s, NEG)
    p = jax.nn.softmax(s, axis=-1)
    o = jnp.einsum('bnkgqc,bnckd->bnqkgd', p.astype(vband.dtype), vband)
    return o.reshape(B, S, N_KV_HEADS, GROUP, HEAD_DIM)

def local_attend(q, k, v, mask):
    s = jnp.einsum('bskgd,btkd->bkgst', q, k).astype(jnp.float32) * SCALE
    s = jnp.where(mask, s, NEG)
    p = jax.nn.softmax(s, axis=-1)
    return jnp.einsum('bkgst,btkd->bskgd', p.astype(v.dtype), v)

def nsa_prompt(q, kv, cw):
    k_cmp, v_cmp, k_slc, v_slc, k_win, v_win = kv
    S = q.shape[1]
    q_pos = jnp.arange(S)
    o_cmp, o_slc = nsa_global(q, k_cmp, v_cmp, k_slc, v_slc, q_pos, cw, True)
    o_win = window_prompt(q, k_win, v_win)
    kv_rows = jnp.stack([k_cmp, v_cmp, k_slc, v_slc], axis=2)
    wb = min(WINDOW, S)
    win_state = jnp.stack([k_win, v_win], axis=2)[:, S - wb:]
    return o_cmp, o_slc, o_win, kv_rows, win_state

def nsa_sample(q, kv, cw, cache, page_table, win):
    k_cmp, v_cmp, k_slc, v_slc, k_win, v_win = kv
    DB, DS = q.shape[:2]
    past_len = page_table.shape[1] * cache.shape[1]
    kv_rows = jnp.stack([k_cmp, v_cmp, k_slc, v_slc], axis=2)
    past = cache[page_table].reshape(DB, past_len, N_KV_KINDS, N_KV_HEADS, HEAD_DIM)
    full = jnp.concatenate([past, kv_rows.astype(past.dtype)], axis=1)
    q_pos = past_len + jnp.arange(DS)
    o_cmp, o_slc = nsa_global(q, full[:, :, 0], full[:, :, 1], full[:, :, 2], full[:, :, 3], q_pos, cw, False)
    wb = win.shape[1]
    wk = jnp.concatenate([win, jnp.stack([k_win, v_win], axis=2).astype(win.dtype)], axis=1)
    kpos = past_len - wb + jnp.arange(wb + DS)
    diff = q_pos[:, None] - kpos[None, :]
    o_win = local_attend(q, wk[:, :, 0], wk[:, :, 1], (diff >= 0) & (diff < WINDOW))
    win_state = wk[:, DS:]
    return o_cmp, o_slc, o_win, kv_rows, win_state

def short_conv(u, prev, w, b):
    S = u.shape[1]
    up = jnp.concatenate([prev.astype(u.dtype), u], axis=1)
    y = b
    for j in range(CONV_W):
        y = y + up[:, j:j + S] * w[j]
    return y, up[:, S:]

def layer_forward(x, c, lw, cw, nsa_fn, conv_prev):
    B, S = x.shape[:2]
    ada = jax.nn.silu(c) @ lw['w_ada'] + lw['b_ada']
    sh1, sc1, g1, sh2, sc2, g2 = jnp.split(ada[:, None, :], 6, axis=-1)
    h = rmsnorm(x, lw['norm1_g']) * (1 + sc1) + sh1
    parts = jnp.split(h @ lw['w_in'], list(np.cumsum(W_IN_SPLITS)[:-1]), axis=-1)
    q, k_cmp, v_cmp, k_slc, v_slc, k_win, v_win, g_nsa, u_in, b_gate, c_gate, m_attn, m_conv = parts
    q = q.reshape(B, S, N_KV_HEADS, GROUP, HEAD_DIM)
    kv = tuple(t.reshape(B, S, N_KV_HEADS, HEAD_DIM) for t in (k_cmp, v_cmp, k_slc, v_slc, k_win, v_win))
    o_cmp, o_slc, o_win, kv_rows, win_state = nsa_fn(q, kv, cw)
    g = jax.nn.sigmoid(g_nsa).reshape(B, S, 3, N_KV_HEADS, GROUP, 1)
    o_attn = (g[:, :, 0] * o_cmp + g[:, :, 1] * o_slc + g[:, :, 2] * o_win).reshape(B, S, N_HEADS * HEAD_DIM)
    conv_y, conv_state = short_conv(c_gate * u_in, conv_prev, lw['conv_w'], lw['conv_b'])
    z = b_gate * conv_y
    mixed = (jax.nn.sigmoid(m_attn) * (o_attn @ lw['w_attn_proj'])
             + jax.nn.sigmoid(m_conv) * (z @ lw['w_conv_proj']))
    x = x + g1 * (mixed @ lw['w_out'])
    h2 = rmsnorm(x, lw['norm2_g']) * (1 + sc2) + sh2
    x = x + g2 * (jnp.square(jax.nn.relu(h2 @ lw['w_mlp1'])) @ lw['w_mlp2'])
    return x, kv_rows, win_state, conv_state

def setup_inputs(seed: int = 0) -> dict:
    key = jax.random.key(seed)
    ks = jax.random.split(key, 32)
    f32 = jnp.float32
    n_pages = PAST_LEN // PAGE_SIZE
    n_used = DEC_BATCH * n_pages
    n_pool = n_used + max(1, n_used // 4)
    win_buf = min(WINDOW, PAST_LEN)

    def nrm(k, shape, scale):
        return jax.random.normal(k, shape, f32) * scale

    page_table = jax.random.permutation(ks[0], n_pool)[:n_used].reshape(DEC_BATCH, n_pages).astype(jnp.int32)
    return {
        'x_prompt': nrm(ks[1], (BATCH, SEQ, D_MODEL), 1.0),
        'x_sample': nrm(ks[2], (DEC_BATCH, DEC_SEQ, D_MODEL), 1.0),
        'c_prompt': nrm(ks[3], (BATCH, D_MODEL), 1.0),
        'c_sample': nrm(ks[4], (DEC_BATCH, D_MODEL), 1.0),
        'cache_nsa_kv': nrm(ks[5], (DEPTH, n_pool, PAGE_SIZE, N_KV_KINDS, N_KV_HEADS, HEAD_DIM), 1.0),
        'page_table': page_table,
        'state_win_kv': nrm(ks[6], (DEPTH, DEC_BATCH, win_buf, 2, N_KV_HEADS, HEAD_DIM), 1.0),
        'state_conv': nrm(ks[7], (DEPTH, DEC_BATCH, CONV_W - 1, CONV_DIM), 1.0),
        'w_ada': nrm(ks[8], (DEPTH, D_MODEL, 6 * D_MODEL), 0.5 * D_MODEL ** -0.5),
        'b_ada': nrm(ks[9], (DEPTH, 6 * D_MODEL), 0.02),
        'norm1_g': 1.0 + nrm(ks[10], (DEPTH, D_MODEL), 0.05),
        'norm2_g': 1.0 + nrm(ks[11], (DEPTH, D_MODEL), 0.05),
        'w_in': nrm(ks[12], (DEPTH, D_MODEL, W_IN_COLS), D_MODEL ** -0.5),
        'w_cmp_k1': nrm(ks[13], (DEPTH, CMP_LEN * HEAD_DIM, CMP_HID), (CMP_LEN * HEAD_DIM) ** -0.5),
        'w_cmp_k2': nrm(ks[14], (DEPTH, CMP_HID, HEAD_DIM), 1.5 * CMP_HID ** -0.5),
        'pe_cmp_k': nrm(ks[15], (DEPTH, CMP_LEN, HEAD_DIM), 0.1),
        'w_cmp_v1': nrm(ks[16], (DEPTH, CMP_LEN * HEAD_DIM, CMP_HID), (CMP_LEN * HEAD_DIM) ** -0.5),
        'w_cmp_v2': nrm(ks[17], (DEPTH, CMP_HID, HEAD_DIM), 1.5 * CMP_HID ** -0.5),
        'pe_cmp_v': nrm(ks[18], (DEPTH, CMP_LEN, HEAD_DIM), 0.1),
        'conv_w': nrm(ks[19], (DEPTH, CONV_W, CONV_DIM), CONV_W ** -0.5),
        'conv_b': nrm(ks[20], (DEPTH, CONV_DIM), 0.02),
        'w_attn_proj': nrm(ks[21], (DEPTH, N_HEADS * HEAD_DIM, D_MODEL), (N_HEADS * HEAD_DIM) ** -0.5),
        'w_conv_proj': nrm(ks[22], (DEPTH, CONV_DIM, D_MODEL), CONV_DIM ** -0.5),
        'w_out': nrm(ks[23], (DEPTH, D_MODEL, D_MODEL), D_MODEL ** -0.5),
        'w_mlp1': nrm(ks[24], (DEPTH, D_MODEL, D_FF), D_MODEL ** -0.5),
        'w_mlp2': nrm(ks[25], (DEPTH, D_FF, D_MODEL), D_FF ** -0.5),
        'normf_g': 1.0 + nrm(ks[26], (D_MODEL,), 0.05),
    }

def reference(x_prompt, x_sample, c_prompt, c_sample, cache_nsa_kv, page_table, state_win_kv, state_conv,
              w_ada, b_ada, norm1_g, norm2_g, w_in, w_cmp_k1, w_cmp_k2, pe_cmp_k, w_cmp_v1, w_cmp_v2, pe_cmp_v,
              conv_w, conv_b, w_attn_proj, w_conv_proj, w_out, w_mlp1, w_mlp2, normf_g):
    yp, ys = x_prompt, x_sample
    kv_p, kv_s, win_p, win_s, conv_p, conv_s = [], [], [], [], [], []
    for l in range(DEPTH):
        lw = {'w_ada': w_ada[l], 'b_ada': b_ada[l], 'norm1_g': norm1_g[l], 'norm2_g': norm2_g[l],
              'w_in': w_in[l], 'conv_w': conv_w[l], 'conv_b': conv_b[l], 'w_attn_proj': w_attn_proj[l],
              'w_conv_proj': w_conv_proj[l], 'w_out': w_out[l], 'w_mlp1': w_mlp1[l], 'w_mlp2': w_mlp2[l]}
        cw = (w_cmp_k1[l], w_cmp_k2[l], pe_cmp_k[l], w_cmp_v1[l], w_cmp_v2[l], pe_cmp_v[l])
        conv0 = jnp.zeros((yp.shape[0], CONV_W - 1, CONV_DIM), yp.dtype)
        yp, a, b, c = layer_forward(yp, c_prompt, lw, cw, nsa_prompt, conv0)
        kv_p.append(a); win_p.append(b); conv_p.append(c)
        sample_fn = functools.partial(nsa_sample, cache=cache_nsa_kv[l], page_table=page_table, win=state_win_kv[l])
        ys, a, b, c = layer_forward(ys, c_sample, lw, cw, sample_fn, state_conv[l])
        kv_s.append(a); win_s.append(b); conv_s.append(c)
    y_prompt = rmsnorm(yp, normf_g)
    y_sample = rmsnorm(ys, normf_g)
    return (y_prompt, y_sample, jnp.stack(kv_p), jnp.stack(kv_s), jnp.stack(win_p), jnp.stack(win_s),
            jnp.stack(conv_p), jnp.stack(conv_s))


_drawn_inputs = setup_inputs


def setup_inputs(seed=0):
    import zlib

    import numpy as np

    out = dict(_drawn_inputs(seed))
    spreads = {}
    factors = {'cache_nsa_kv': 4.619, 'pe_cmp_k': 8.0, 'pe_cmp_v': 7.03, 'conv_b': 8.0, 'norm2_g': 2.784}
    for name, (base, spread) in spreads.items():
        noise = np.random.default_rng([zlib.crc32(name.encode()), seed]).standard_normal(out[name].shape)
        drawn = base * np.exp(spread * noise) if base else spread * noise
        out[name] = __import__('jax').numpy.asarray(drawn.astype(out[name].dtype))
    for name, factor in factors.items():
        out[name] = (out[name] * factor).astype(out[name].dtype)
    return out
```

```python
import concourse.bass as bass
from concourse import mybir
from contextlib import ExitStack

F32 = mybir.dt.float32
F32R = mybir.dt.float32r
I32 = mybir.dt.int32
ALU = mybir.AluOpType
ACT = mybir.ActivationFunctionType
AX = mybir.AxisListType
ds = bass.ds

P = 128
D = 2048
KT = D // P
NPR = 256
NB, NSTEP = 8, 8
NSM = NB * NSTEP
NT = NPR + NSM
NSEQ = 1 + NB
NH, NKV, GRP, HD = 16, 4, 4, 128
KVW = NKV * HD
PAST = 2048
PAGE = 128
NPAGE = PAST // PAGE
WIN = 512
CLEN, CSTR = 32, 16
NC_S = PAST // CSTR - 1
NC_P = NPR // CSTR - 1
SLC = 64
NSB = PAST // SLC + 1
FF = 4 * D
EPS = 1e-6
NEG = -1e30
SCALE = HD ** -0.5

COL_Q, COL_KV, COL_G = 0, D, D + 6 * KVW
COL_U = COL_G + 3 * NH
COL_B, COL_C = COL_U + D, COL_U + 2 * D
COL_MA, COL_MC = COL_U + 3 * D, COL_U + 4 * D

T_CONV, T_MC, T_WC, T_MA, T_Q, T_KV = 0, 48, 64, 80, 96, 112
T_WA, T_WO, T_MLP, T_END = 136, 152, 168, 296
CH = KT // 2
POOL_STEPS = 18
CREDIT = 8


class Steps:

    def __init__(self, eng, sem, first=0):
        self.eng, self.sem, self.base, self.k, self.regs = eng, sem, first, 0, []

    def did(self, ins):
        ins.then_inc(self.sem, 1)
        self.k += 1
        return self

    def value(self):
        v = self.base + self.k
        for reg, per, k in self.regs:
            v = reg * per + v + k
        return v

    def wait(self):
        self.eng.wait_ge(self.sem, self.value())

    def enter(self, reg, per):
        self.regs.append((reg, per, self.k))
        self.k = 0

    def leave(self, times):
        reg, per, before = self.regs.pop()
        assert self.k == per, f"{self.sem}: {self.k} steps in an iteration, {per} stated"
        self.k = before + per * times


def build_step(nc, A):
    ctx = ExitStack()
    with ctx:
        def at(name, shape, offset, dt=F32):
            return nc.alloc_sbuf_tensor_at("sb_" + name, shape, dt, offset=offset)

        def sem(name):
            return ctx.enter_context(nc.semaphore(name))

        def dram(name, shape):
            return nc.dram_tensor("scratch_" + name, shape, F32, kind="Internal").ap()

        TOK = KT * NT * 4
        A_SMALL = 16512
        A_HI = A_SMALL + 11776
        A_LO = A_HI + TOK
        A_Q = A_LO + TOK
        A_KV = A_Q + TOK
        A_GA = A_KV + 24 * NT * 4
        A_MX = A_GA + TOK
        A_RING = A_MX + TOK + 256
        A_END = 229344

        used = [A_SMALL]

        def small(name, shape, dt=F32):
            n = 4
            for s in shape[1:]:
                n *= s
            o = used[0]
            used[0] = o + (n + 31) // 32 * 32
            assert used[0] <= A_HI
            return at(name, shape, o, dt)

        ident = small("ident", [P, P])
        ones = small("ones", [P, P])
        params = small("params", [P, 112])
        b_ada = small("b_ada", [P, 96])
        ada = small("ada", [P, 96, NSEQ])
        cT = small("cT", [P, KT, NSEQ])
        page_ids = small("page_ids", [1, NB * NPAGE], I32)
        A_CS = used[0]
        cs = at("cs", [P, KT, 32], A_CS)
        a_mul = small("a_mul", [P, KT, NSEQ])
        tmp_s = small("tmp_s", [P, NSM])
        gate_p = small("gate_p", [P, 2, 48])
        gate_s = small("gate_s", [P, 3, NB])
        cstate = small("cstate", [P, KT, 2 * NSEQ])
        assert used[0] >= A_CS + KT * 32 * 4
        sel9 = small("sel9", [P, NSEQ])
        ada_row = at("ada_row", [P, 256], used[0])
        rbc = small("rbc", [P, NT])
        pe_col = small("pe_col", [P, 2])
        peT = small("peT", [P, 2, 32])
        prevT = small("prevT", [P, 2 * NB, KT])
        g1n, g2n, gfn, cvb = (params[:, 16 * i:16 * i + 16] for i in range(4))
        cvw = [params[:, 64 + 16 * j:80 + 16 * j] for j in range(3)]

        act_hi = at("act_hi", [P, KT, NT], A_HI, F32R)
        act_lo = at("act_lo", [P, KT, NT], A_LO, F32R)
        z_hi = at("z_hi", [P, KT, NT], A_Q, F32R)
        z_lo = at("z_lo", [P, KT, NT], A_GA, F32R)
        hid_hi = at("hid_hi", [P, KT, NT], A_Q, F32R)
        hid_lo = at("hid_lo", [P, KT, NT], A_MX, F32R)
        qo = at("qo", [P, NH, NT], A_Q)
        kv = at("kv", [P, 24, NT], A_KV)
        ga = at("ga", [P, KT, NT], A_GA)
        mx = at("mx", [P, KT, NT], A_MX)
        x0 = at("x0", [P, KT, NT], A_KV)
        x1 = at("x1", [P, KT, NT], A_GA)
        sq = at("sq", [P, KT, NT], A_Q)
        raw = at("raw", [P, 2, KT, 256], A_RING)
        w_hi = at("w_hi", [P, 4, CH, P], A_RING + 32768, F32R)
        w_lo = at("w_lo", [P, 4, CH, P], A_RING + 32768 + 16384, F32R)
        ada_raw = at("ada_raw", [P, 2, KT, 256], A_RING + 32768)
        A_CV = A_KV + TOK
        up_p = at("up_p", [P, 2, NPR + 2], A_CV)
        up_s = at("up_s", [P, 2, NB, NSTEP + 2], A_CV + 2080)
        u_sb = at("u_sb", [P, 2, NT], A_CV + 2080 + 640)
        y_sb = at("y_sb", [P, 2, NT], A_CV + 2080 + 640 + 2560)
        z_sb = at("z_sb", [P, 2, NT], A_MX)
        gw_hi = at("gw_hi", [P, KT, P], A_Q, F32R)
        gw_lo = at("gw_lo", [P, KT, P], A_Q + 8192, F32R)
        gw = at("gw", [P, KT, P], A_KV)
        gT = at("gT", [48, NT], A_KV + 8192)
        gTs = at("gTs", [48, NSTEP, NB], A_KV + 8192 + 1280)
        x_rows = at("x_rows", [P, 3, D], A_HI)
        rows = at("rows", [P, 8, P], A_HI + 3 * D * 4)
        w1_hi = at("w1_hi", [P, 2, 32, P], A_HI, F32R)
        w1_lo = at("w1_lo", [P, 2, 32, P], A_HI + 32768, F32R)
        w1 = at("w1", [P, 2, 32, P], A_HI + 65536)
        KEYS = 2 * PAST + CSTR
        keyT_hi = at("keyT_hi", [P, 2, KEYS], A_HI + 65536, F32R)
        keyT_lo = at("keyT_lo", [P, 2, KEYS], A_HI + 65536 + 8 * KEYS, F32R)
        pages = at("pages", [P, 2, NPAGE, 2 * HD], A_RING)
        A_T = A_HI + 65536 + 16 * KEYS
        gelu = at("gelu", [P, 2 * NC_S], A_T)
        kc_out = at("kc_out", [P, 2, NC_S], A_T + 1024)
        assert A_T + 2048 <= A_RING
        A_T2 = A_RING + 65536
        vc_out = at("vc_out", [NC_S, 2, P], A_T2)
        w2 = at("w2", [P, 2, P], A_T2 + 1024)
        A_P = A_RING
        w1p = at("w1p", [P, 2, 32, P], A_HI)
        w2p = at("w2p", [P, 2, P], A_HI + 32768)
        gelu_p = at("gelu_p", [P, 2, NKV, NC_P], A_HI + 33792)
        kc_p = at("kc_p", [P, NKV, NC_P], A_HI + 34304)
        vc_p = at("vc_p", [NC_P, NKV, P], A_HI + 34560)
        mask_p = at("mask_p", [P, 2, NPR], A_HI + 36608)
        mask_c = at("mask_c", [P, 2, NC_P], A_HI + 38656)
        vis = at("vis", [P, 2], A_HI + 38784)
        q_b = at("q_b", [P, GRP, NPR], A_P)
        kv_b = at("kv_b", [P, 6, NT], A_P + 4096)
        gate_b = at("gate_b", [P, 3, GRP, 2], A_P + 11776)
        rowsb = at("rowsb", [P, 3, 6, P], A_P + 11904)
        S_p = at("S_p", [P, 8, 2, NPR], A_P + 21120)
        S_c = at("S_c", [P, 8, NC_P], A_P + 37504)
        mxp = at("mxp", [P, 8, 3], A_P + 38016)
        nmp = at("nmp", [P, 8, 3], A_P + 38112)
        den = at("den_p", [P, 8, 3], A_P + 38208)
        rr = at("rr_p", [P, 8, 3], A_P + 38304)
        PT = at("PT_p", [P, 2, 4, P], A_P + 38400)
        PTc = at("PTc_p", [NC_P, 8, P], A_P + 42496)
        o_row = at("o_row", [P, 2, P], A_P + 46592)
        kc_b = at("kc_b", [P, NC_P], A_P + 48128)
        vc_b = at("vc_b", [NC_P, P], A_P + 48192)
        assert A_P + 48704 <= A_END
        A_S = A_HI
        krow = at("krow", [P, 3, 4, KVW], A_S)
        kT = at("kT", [P, 2, NKV, 512], A_S + 24576)
        vrow = at("vrow", [P, 3, 4, KVW], A_RING)
        S_s = at("S_s", [P, PAST + NSTEP], A_RING + 24576)
        W_s = at("W_s", [P, WIN + NSTEP], A_RING + 24576 + 8224)
        C_s = at("C_s", [P, P], A_RING + 24576 + 8224 + 2080)
        PTs = at("PTs", [P, 20, P], A_RING + 35392)
        PTn = at("PTn", [NSTEP, 2, P], A_RING + 45632)
        PTcs = at("PTcs", [NC_S, P], A_RING + 46656)
        kc_s = at("kc_s", [P, 2, NKV, NC_S], A_RING + 47168)
        vc_s = at("vc_s", [NC_S, 2, NKV, P], A_RING + 51232)
        A_M = A_RING + 55328
        q_s = at("q_s", [P, P], A_M)
        knew = at("knew", [P, 16, NSTEP], A_M + 512)
        vnew = at("vnew", [NSTEP, 2, KVW], A_M + 1024)
        mask_w = at("mask_w", [P, WIN + NSTEP], A_M + 5120)
        mask_n = at("mask_n", [P, NSTEP], A_M + 7200)
        selw = at("selw", [P, NSB], A_M + 7232)
        grp = at("grp", [P, P], A_M + 7392)
        z_s = at("z_s", [P, NSB], A_M + 7904)
        sc1 = at("sc1", [P, NSB], A_M + 8064)
        sc2 = at("sc2", [P, NSB], A_M + 8224)
        selb = at("selb", [P, NSB], A_M + 8384)
        top8 = at("top8", [P, 8], A_M + 8544)
        st = at("st", [P, 12], A_M + 8576)
        os_row = at("os_row", [P, P], A_M + 8640)
        os_tmp = at("os_tmp", [P, P], A_M + 9152)
        rowi = at("rowi", [P, 4], A_M + 9664, I32)
        rowf = at("rowf", [P, 4], A_M + 9696)
        coli = at("coli", [P, WIN + NSTEP], A_S, I32)
        colf = at("colf", [P, WIN + NSTEP], A_S + 2080)
        grpf = at("grpf", [P, P], A_S + 4160)
        assert A_M + 9728 <= A_END, (A_M + 9728, A_END)
        y_rows = at("y_rows", [P, 2, D], A_HI)
        cs_rows = at("cs_rows", [2 * NSEQ, KT, P], A_KV)
        rl = at("rl", [P, 4, NT], A_KV + 10240)
        rl2 = at("rl2", [P, 4, NT], A_KV + 10240 + 5120)

        bank = [ctx.enter_context(nc.psum_tensor(f"bank{i}", [P, 512], F32)) for i in range(8)]

        w_ada = A["w_ada"][0].rearrange("(t p) n -> p t n", p=P)
        w_in = A["w_in"][0].rearrange("(t p) n -> p t n", p=P)
        w_attn = A["w_attn_proj"][0].rearrange("(t p) n -> p t n", p=P)
        w_conv = A["w_conv_proj"][0].rearrange("(t p) n -> p t n", p=P)
        w_out = A["w_out"][0].rearrange("(t p) n -> p t n", p=P)
        w_mlp1 = A["w_mlp1"][0].rearrange("(t p) n -> p t n", p=P)
        w_mlp2 = A["w_mlp2"][0].rearrange("(f t p) n -> f p t n", p=P, t=KT)
        cache = A["cache_nsa_kv"][0].rearrange("g p k h d -> g p k (h d)")
        win = A["state_win_kv"][0].rearrange("b (c p) k h d -> b p c k (h d)", p=P)
        kc_d = dram("kc", [NB, P, NKV, NC_S])
        vc_d = dram("vc", [NB, NC_S, NKV, P])
        x_d = dram("x", [P, KT, NT])
        g_d = dram("gates", [48, NSTEP, NB])

        s_rows = sem("start_rows_loaded")
        s_w1 = sem("compress_weights_loaded")
        s_const = sem("constants_made")
        s_tr = sem("start_transposes_done")
        s_prm = sem("start_rows_turned")
        s_x0 = sem("x_feature_major")
        s_ids = sem("page_ids_loaded")
        s_page = [sem("pair0_pages_loaded"), sem("pair1_pages_loaded")]
        s_w1_hi = sem("compress_weights_hi")
        s_w1_lo = sem("compress_weights_lo")
        s_kt_bank = sem("key_bank_filled")
        s_kt_hi = sem("key_bank_hi_copied")
        s_kt_ev = sem("key_bank_split")
        s_cmp_h = sem("compress_hidden_done")
        s_gelu = sem("compress_gelu_done")
        s_cmp_o = sem("compress_out_done")
        s_cmp_ev = sem("compress_out_copied")
        s_cmp_st = [sem("kc_stored"), sem("vc_stored")]
        s_cmp_free = [sem("kc_out_free"), sem("vc_out_free")]
        s_pe_b = sem("pe_bias_summed")
        s_ada = [sem(f"ada_panel_loaded{i}") for i in range(2)]
        s_ada_pe = sem("ada_panel_multiplied")
        s_ada_row = sem("ada_rows_copied")
        s_ada_t = sem("ada_rows_turned")
        s_ada_ev = sem("ada_panel_copied")
        s_silu = sem("silu_of_c_done")
        s_sq = sem("squares_done")
        s_nsum = sem("square_sums_done")
        s_h = sem("operand_split_done")
        s_raw = [sem(f"weight_panel_loaded{i}") for i in range(2)]
        s_hi = sem("weight_hi_ready")
        s_lo = sem("weight_lo_ready")
        s_chunk = sem("chunk_multiplied")
        s_ev = sem("tile_taken_out")
        s_z = sem("z_split_done")
        s_zl = sem("z_lo_ready")
        s_zt = sem("scaled_group_ready")
        s_cpp = sem("prompt_compressed_copied")
        s_m = sem("merge_done")
        s_gate = sem("gate_step")
        s_gld = sem("gate_weights_loaded")
        s_gdma = sem("gates_moved")
        s_pe = sem("tensor_misc")
        s_av = sem("act_chain")
        s_dv = sem("dve_chain")
        s_xsp = sem("x_spilled")
        s_xadd = sem("x_tile_updated")
        s_xld = sem("x_back")
        s_xld1 = sem("x_back_after_attention")
        s_pool = sem("pool_chain")
        s_out = sem("outputs_written")
        s_win = sem("window_rows_written")
        s_rowdma = sem("kv_rows_written")
        s_rowfree = sem("kv_rows_free")
        s_bun = sem("head_bundle_copied")
        s_rtr = sem("kv_rows_turned")
        s_rev = sem("kv_rows_copied")
        s_sc = sem("scores_done")
        s_scev = sem("scores_copied")
        s_exp = sem("exps_done")
        s_pt = sem("probs_turned")
        s_ptev = sem("probs_turned_copied")
        s_pv = sem("values_summed")
        s_orow = sem("head_out_mixed")
        s_otr = sem("head_out_turned")
        s_oev = sem("head_out_stored")
        s_kd = [sem(f"sample_keys_loaded{i}") for i in range(3)]
        s_vd = [sem(f"sample_values_loaded{i}") for i in range(3)]
        s_cd = sem("sample_compressed_loaded")
        s_ktr = sem("sample_keys_turned")
        s_ktev = [sem("sample_bank_copied_act"), sem("sample_bank_copied_dve")]
        s_hidh = sem("hidden_hi_ready")
        s_ssc = sem("sample_scores_done")
        s_sev = sem("sample_scores_copied")
        s_spt = sem("sample_probs_turned")
        s_spte = sem("sample_probs_copied")
        s_spv = sem("sample_values_summed")
        s_sel = sem("selection_step")
        s_selp = sem("selection_products")
        s_sexp = sem("sample_exps_done")
        s_new = sem("new_rows_copied")
        s_vnt = sem("new_values_turned")
        s_vne = sem("new_values_copied")
        s_so = sem("sample_out_stored")
        s_sm = sem("sample_out_mixed")
        s_sot = sem("sample_out_turned")
        s_hid = sem("hidden_ready")
        s_fin = sem("final_step")
        s_ftr = sem("final_turned")
        s_fev = sem("final_copied")
        s_pass = [sem("passed_dve"), sem("passed_pe"), sem("passed_pool")]

        block = ctx.enter_context(nc.Block())

        @block.sync
        def _(sp):
            row_src = [
                (rows[0:16, 0, :], A["norm1_g"][0].rearrange("(t p) -> t p", p=P)),
                (rows[16:32, 0, :], A["norm2_g"][0].rearrange("(t p) -> t p", p=P)),
                (rows[32:48, 0, :], A["normf_g"].rearrange("(t p) -> t p", p=P)),
                (rows[48:64, 0, :], A["conv_b"][0].rearrange("(t p) -> t p", p=P)),
                (rows[64:112, 0, :], A["conv_w"][0].rearrange("j (t p) -> (j t) p", p=P)),
                (rows[0:96, 1, :], A["b_ada"][0].rearrange("(t p) -> t p", p=P)),
                (rows[0:16, 2, :], A["c_prompt"].rearrange("b (t p) -> (b t) p", p=P)),
                (rows[:, 3, :], A["c_sample"].rearrange("b (t p) -> (b t) p", p=P)),
                (rows[:, 4, :], A["state_conv"][0, 0:4].rearrange("b j (t p) -> (b j t) p", p=P)),
                (rows[:, 5, :], A["state_conv"][0, 4:8].rearrange("b j (t p) -> (b j t) p", p=P)),
                (rows[0:32, 6, :], A["pe_cmp_k"][0]),
                (rows[0:32, 7, :], A["pe_cmp_v"][0]),
            ]
            sp.dma_start(page_ids[:, :], A["page_table"].rearrange("(a b) n -> a (b n)", a=1)).then_inc(s_ids, 16)
            for dst, src in row_src:
                sp.dma_start(dst, src).then_inc(s_rows, 16)
            sp.dma_start(x_rows[:, 0:2, :], A["x_prompt"][0].rearrange("(t p) n -> p t n", p=P)).then_inc(s_rows, 16)
            sp.dma_start(x_rows[0:NSM, 2, :], A["x_sample"].rearrange("b s n -> (b s) n")).then_inc(s_rows, 16)
            sp.dma_start(w1[:, 0], A["w_cmp_k1"][0].rearrange("(r d) f -> d r f", d=P)).then_inc(s_w1, 16)
            sp.dma_start(w1[:, 1], A["w_cmp_v1"][0].rearrange("(r d) f -> d r f", d=P)).then_inc(s_w1, 16)
            sp.dma_start(w2[:, 0, :], A["w_cmp_k2"][0]).then_inc(s_w1, 16)
            sp.dma_start(w2[:, 1, :], A["w_cmp_v2"][0]).then_inc(s_w1, 16)
            def load_pages(b):
                return [sp.value_load(page_ids[0:1, ds(b * NPAGE + pg, 1)], min_val=0, max_val=A["cache_nsa_kv"].shape[1] - 1)
                        for pg in range(NPAGE)]

            def unit_pages(b, u, page):
                kind, pair = u % 4 // 2, u % 2
                sp.wait_ge(s_kt_bank, b * 32 + 8 * u - 8 + 2 * CREDIT)
                for pg in range(NPAGE):
                    sp.dma_start(pages[:, pair, pg, :],
                                 cache[ds(page[pg], 1), :, kind, 256 * pair:256 * pair + 256].rearrange("a p n -> p (a n)")).then_inc(s_page[pair], 16)

            def ada_panel(b, p):
                sp.wait_ge(s_ada_pe, b * 6 + p - 1 + CREDIT)
                sp.dma_start(ada_raw[:, p % 2, :, :], w_ada[:, :, ds(b * 1536 + 256 * p, 256)]).then_inc(s_ada[p % 2], 16)

            def compress_loads(b, last):
                page = load_pages(b)
                for u in range(4):
                    if u == 2 and not last:
                        page = load_pages(b + 1)
                    if u < 2 or not last:
                        unit_pages(b, u + 2, page)
                    for p in ((2 * u + 2, 2 * u + 3) if u < (2 if last else 3) else ()):
                        ada_panel(b, p)

            sp.wait_ge(s_ids, 16)
            first = load_pages(0)
            unit_pages(0, 0, first)
            unit_pages(0, 1, first)
            ada_panel(0, 0)
            ada_panel(0, 1)
            with sp.Fori(0, NB - 1) as b:
                compress_loads(b, False)
            compress_loads(NB - 1, True)
            sp.wait_ge(s_cmp_ev, 4 * NB + CREDIT)
            sp.dma_start(x0[:, :, :], x_d).then_inc(s_xld, 16)

            def panel(t, src):
                slot = (t // 2) % 2 if isinstance(t, int) else t[1] // 2 % 2
                sp.wait_ge(s_lo, (2 * t if isinstance(t, int) else 2 * t[0] + 2 * t[1]) - 4 + CREDIT)
                sp.dma_start(raw[:, slot, :, :], src).then_inc(s_raw[slot], 16)

            def dense(t0, n, src):
                with sp.Fori(0, n // 4) as i:
                    for j in range(2):
                        panel((i * 4 + t0, 2 * j), src(i * 512 + 256 * j))

            with sp.Fori(0, 4) as i:
                for half in range(2):
                    for k, col in enumerate((COL_U, COL_C, COL_B)):
                        panel((i * 12 + T_CONV, 6 * half + 2 * k), w_in[:, :, ds(i * 512 + col + 256 * half, 256)])
            dense(T_MC, 16, lambda c: w_in[:, :, ds(c + COL_MC, 256)])
            dense(T_WC, 16, lambda c: w_conv[:, :, ds(c, 256)])
            dense(T_MA, 16, lambda c: w_in[:, :, ds(c + COL_MA, 256)])
            sp.wait_ge(s_h, 4)
            sp.dma_start(gw[:, :, :], w_in[:, :, COL_G:COL_G + P]).then_inc(s_gld, 16)
            dense(T_Q, 16, lambda c: w_in[:, :, ds(c + COL_Q, 256)])
            dense(T_KV, 24, lambda c: w_in[:, :, ds(c + COL_KV, 256)])

            sp.wait_ge(s_ev, T_WA + CREDIT)
            sp.dma_start(w1p[:, 0], A["w_cmp_k1"][0].rearrange("(r d) f -> d r f", d=P)).then_inc(s_w1, 16)
            sp.dma_start(w1p[:, 1], A["w_cmp_v1"][0].rearrange("(r d) f -> d r f", d=P)).then_inc(s_w1, 16)
            sp.dma_start(w2p[:, 0, :], A["w_cmp_k2"][0]).then_inc(s_w1, 16)
            sp.dma_start(w2p[:, 1, :], A["w_cmp_v2"][0]).then_inc(s_w1, 16)
            with sp.Fori(0, NKV) as h:
                for tt in range(3):
                    sp.wait_ge(s_rev, h * 6 + 2 * tt + 2 + CREDIT)
                    n = P if tt < 2 else NSM
                    kvo = A["out_kv_prompt"][0, 0, P * tt:P * tt + P] if tt < 2 else A["out_kv_sample"][0].rearrange("b s k h d -> (b s) k h d")
                    sp.dma_start(kvo[:, :, ds(h, 1), :].rearrange("t k a d -> t k (a d)"), rowsb[0:n, tt, 0:4, :]).then_inc(s_rowdma, 16)
                    if tt < 2:
                        wo = A["out_win_prompt"][0, 0, P * tt:P * tt + P]
                        sp.dma_start(wo[:, :, ds(h, 1), :].rearrange("t k a d -> t k (a d)"), rowsb[0:n, tt, 4:6, :]).then_inc(s_rowdma, 16)
                    else:
                        for b in range(NB):
                            wo = A["out_win_sample"][0, b, WIN - NSTEP:WIN]
                            sp.dma_start(wo[:, :, ds(h, 1), :].rearrange("t k a d -> t k (a d)"),
                                         rowsb[NSTEP * b:NSTEP * b + NSTEP, tt, 4:6, :]).then_inc(s_rowdma, 16)
                sp.wait_ge(s_rowdma, h * (16 * (5 + NB)) + 16 * (5 + NB))
                sp.sem_inc(s_rowfree, 1)
            sp.wait_ge(s_sel, 1)
            with sp.Fori(0, NB) as b:
                sp.wait_ge(s_ktr, b * 26 - 6 + 2 * CREDIT)
                sp.dma_start(krow[:, 2, :, :], win[ds(b, 1), :, :, 0, :].rearrange("a p c n -> p (a c) n")).then_inc(s_kd[2], 16)
                for c in range(4):
                    for pg in range(4):
                        page = sp.value_load(page_ids[0:1, ds(b * NPAGE + 4 * c + pg, 1)], min_val=0, max_val=A["cache_nsa_kv"].shape[1] - 1)
                        if pg == 0:
                            sp.wait_ge(s_ktr, b * 26 + (-14, -10, 4, 8)[c] + 2 * CREDIT)
                        sp.dma_start(krow[:, c % 2, pg, :],
                                     cache[ds(page, 1), :, 2, :].rearrange("a p n -> p (a n)")).then_inc(s_kd[c % 2], 16)
            sp.wait_ge(s_oev, 32 + CREDIT)
            sp.wait_ge(s_so, NB + CREDIT)

            dense(T_WA, 16, lambda c: w_attn[:, :, ds(c, 256)])
            dense(T_WO, 16, lambda c: w_out[:, :, ds(c, 256)])
            with sp.Fori(0, 4) as f:
                with sp.Fori(0, 4) as i:
                    for j in range(2):
                        panel((f * 32 + i * 4 + T_MLP, 2 * j), w_mlp1[:, :, ds(f * D + i * 512 + 256 * j, 256)])
                with sp.Fori(0, 4) as i:
                    for j in range(2):
                        panel((f * 32 + i * 4 + T_MLP + 16, 2 * j),
                              w_mlp2[ds(f, 1), :, :, ds(i * 512 + 256 * j, 256)].rearrange("a p t n -> p (a t) n"))
            for tt in range(3):
                sp.wait_ge(s_fev, 4 * (tt + 1))
                if tt < 2:
                    sp.dma_start(A["out_y_prompt"][0, P * tt:P * tt + P, :], y_rows[:, tt % 2, :]).then_inc(s_out, 16)
                else:
                    sp.dma_start(A["out_y_sample"].rearrange("b s n -> (b s) n"), y_rows[0:NSM, 0, :]).then_inc(s_out, 16)
            sp.wait_ge(s_out, 16 * 3)
            sp.wait_ge(s_rowdma, 16 * NKV * (5 + NB))
            sp.wait_ge(s_win, 16 * (NB + 2))

        @block.gpsimd
        def _(pool):
            chain = Steps(pool, s_pool)
            chain.did(pool.memset(ident[:, :], 0.0))
            pool.memset(ones[:, :], 1.0).then_inc(s_const, 1)
            chain.wait()
            pool.affine_select(out=ident[:, :], in_=ident[:, :], compare_op=ALU.not_equal, fill=1.0, base=0,
                               pattern=[[-1, P]], channel_multiplier=1).then_inc(s_const, 1)
            pool.wait_ge(s_x0, 16)
            pool.dma_start(x_d, mx[:, :, :]).then_inc(s_xsp, 16)
            for b in range(NB):
                pool.dma_start(A["out_win_sample"][0, b, 0:WIN - NSTEP].rearrange("t k h d -> t (k h d)"),
                               A["state_win_kv"][0, b, NSTEP:WIN].rearrange("t k h d -> t (k h d)")).then_inc(s_win, 16)
            with pool.Fori(0, NB) as b:
                for kind in range(2):
                    for pair in range(2):
                        pool.wait_ge(s_cmp_ev, b * 4 + 2 * kind + pair + 1 + CREDIT)
                        pool.sem_inc(s_pass[2], 1)
                        if kind == 0:
                            pool.dma_start(kc_d[ds(b, 1), :, 2 * pair:2 * pair + 2, :].rearrange("a p h c -> p (a h) c"),
                                           kc_out[:, :, :]).then_inc(s_cmp_st[0], 16)
                        else:
                            pool.dma_start(vc_d[ds(b, 1), :, 2 * pair:2 * pair + 2, :].rearrange("a p h c -> p (a h) c"),
                                           vc_out[:, :, :]).then_inc(s_cmp_st[1], 16)
                        pool.wait_ge(s_cmp_st[kind], b * 32 + 16 * pair + 16)
                        pool.sem_inc(s_cmp_free[kind], 1)
            pool.wait_ge(s_gate, 5)
            pool.dma_start(g_d, gTs[:, :, :]).then_inc(s_gdma, 16)
            pool.wait_ge(s_gdma, 16)
            pool.dma_start(gate_s[:, :, :], g_d.rearrange("(r h) s b -> (h s) r b", r=3)).then_inc(s_gdma, 16)
            pool.wait_ge(s_ev, T_WA + CREDIT)
            m = Steps(pool, s_pool, chain.value())
            m.did(pool.memset(mask_p[:, :, :], 0.0))
            m.did(pool.memset(mask_c[:, :, :], 0.0))
            m.did(pool.memset(vis[:, :], 1.0))
            m.wait()
            for qt in range(2):
                m.did(pool.affine_select(out=mask_p[:, qt, :], in_=mask_p[:, qt, :], compare_op=ALU.is_ge, fill=NEG,
                                         base=P * qt, pattern=[[-1, NPR]], channel_multiplier=1))
                m.did(pool.affine_select(out=mask_c[:, qt, :], in_=mask_c[:, qt, :], compare_op=ALU.is_ge, fill=NEG,
                                         base=P * qt - CLEN + 1, pattern=[[-CSTR, NC_P]], channel_multiplier=1))
                m.did(pool.affine_select(out=vis[:, qt:qt + 1], in_=vis[:, qt:qt + 1], compare_op=ALU.is_ge, fill=0.0,
                                         base=P * qt - CLEN + 1, pattern=[[0, 1]], channel_multiplier=1))
            pool.wait_ge(s_oev, 32 + CREDIT)
            m.did(pool.iota(coli[:, :], pattern=[[1, WIN + NSTEP]], base=0, channel_multiplier=0))
            m.did(pool.iota(rowi[:, 0:1], pattern=[[0, 1]], base=0, channel_multiplier=1))
            m.did(pool.memset(selw[:, :], 1.0))
            m.did(pool.memset(sc1[:, :], 1.0))
            m.wait()
            for off, tile in ((0, selw), (1, sc1)):
                m.did(pool.affine_select(out=tile[:, :], in_=tile[:, :], compare_op=ALU.is_ge, fill=0.0, base=off,
                                         pattern=[[-4, NSB]], channel_multiplier=1))
                m.wait()
                m.did(pool.affine_select(out=tile[:, :], in_=tile[:, :], compare_op=ALU.is_ge, fill=0.0, base=3 - off,
                                         pattern=[[4, NSB]], channel_multiplier=-1))
                m.wait()
            assert m.value() == POOL_STEPS, m.value()
            pool.wait_ge(s_ids, 16)
            pool.wait_ge(s_rowdma, 16 * NKV * (5 + NB))
            with pool.Fori(0, NB) as b:
                pool.wait_ge(s_spv, b * 2 + CREDIT)
                pool.sem_inc(s_pass[2], 1)
                pool.wait_ge(s_cmp_st[0], 16 * 2 * NB)
                pool.wait_ge(s_cmp_st[1], 16 * 2 * NB)
                pool.dma_start(kc_s[:, 0], kc_d[ds(b, 1)].rearrange("a p h c -> p (a h) c")).then_inc(s_cd, 16)
                pool.dma_start(vc_s[:, 0], vc_d[ds(b, 1)].rearrange("a p h c -> p (a h) c")).then_inc(s_cd, 16)
                pool.dma_start(vrow[:, 2, :, :], win[ds(b, 1), :, :, 1, :].rearrange("a p c n -> p (a c) n")).then_inc(s_vd[2], 16)
                for c in range(4):
                    for pg in range(4):
                        page = pool.value_load(page_ids[0:1, ds(b * NPAGE + 4 * c + pg, 1)], min_val=0, max_val=A["cache_nsa_kv"].shape[1] - 1)
                        if pg == 0 and c == 2:
                            pool.wait_ge(s_spv, b * 2 + 1 + CREDIT)
                            pool.sem_inc(s_pass[2], 1)
                        pool.dma_start(vrow[:, c % 2, pg, :],
                                       cache[ds(page, 1), :, 3, :].rearrange("a p n -> p (a n)")).then_inc(s_vd[c % 2], 16)
            pool.wait_ge(s_m, 16)
            pool.dma_start(x1[:, :, :], x_d).then_inc(s_xld1, 16)
            pool.wait_ge(s_fin, 4)
            pool.dma_start(A["out_conv_prompt"][0, 0].rearrange("j (t p) -> j t p", p=P), cs_rows[0:2]).then_inc(s_win, 16)
            pool.dma_start(A["out_conv_sample"][0].rearrange("b j (t p) -> (b j) t p", p=P), cs_rows[2:18]).then_inc(s_win, 16)

        @block.scalar
        def _(act):
            fence = lambda: act.wait_ge(s_const, 1)
            act.sem_inc(s_gelu, CREDIT)
            act.sem_inc(s_cmp_o, CREDIT)
            act.sem_inc(s_rowfree, CREDIT)
            act.sem_inc(s_rev, CREDIT)
            act.sem_inc(s_ptev, CREDIT)
            act.sem_inc(s_ktev[0], CREDIT)
            for k in range(KT):
                act.wait_ge(s_tr, 3 + k)
                act.activation(mx[:, k, :], bank[2 + k % 4][:, 0:NT], ACT.Copy).then_inc(s_x0, 1)
            act.wait_ge(s_prm, 10)
            act.activation(cs[:, :, 0:NSEQ], cT[:, :, :], ACT.Silu).then_inc(s_silu, 1)
            act.wait_ge(s_w1, 64)
            act.wait_ge(s_tr, 18)
            for kind in range(2):
                act.activation(w1_hi[:, kind], w1[:, kind], ACT.Copy).then_inc(s_w1_hi, 1)
            act.wait_ge(s_w1_lo, 2)
            act.wait_ge(s_pe_b, 2)
            act.wait_ge(s_xsp, 16)
            act.activation(keyT_hi[:, :, 2 * PAST:KEYS], ident[:, 0:2 * CSTR].rearrange("p (a c) -> p a c", a=2), ACT.Copy).then_inc(s_w1_hi, 1)

            def keys_hi(b, u, f):
                act.wait_ge(s_kt_bank, b * 32 + 8 * u + f + 1 + 2 * CREDIT)
                act.wait_ge(s_cmp_h, b * 4 + u - 1 + CREDIT)
                act.activation(keyT_hi[:, u % 2, 512 * f:512 * f + 512], bank[f % 4][:, :], ACT.Copy).then_inc(s_kt_hi, 1)

            def compress_act(b, last):
                for u in range(4):
                    kind, pair = u // 2, u % 2

                    def ada_row_out(p):
                        act.wait_ge(s_ada_pe, b * 6 + p + 1 + CREDIT)
                        act.activation(ada_row[:, :], bank[7][:, 0:256], ACT.Copy).then_inc(s_ada_row, 1)

                    for f in range(8):
                        if f in (0, 4) and u < 3:
                            ada_row_out(2 * u + f // 4)
                        if f == 5:
                            act.wait_ge(s_cmp_h, b * 4 + u + 1 + CREDIT)
                            act.wait_ge(s_cmp_o, b * 4 + u + CREDIT)
                            act.activation(gelu[:, :].rearrange("p (h c) -> p h c", h=2),
                                           bank[4 + pair][:, 0:2 * P].rearrange("p (h c) -> p h c", h=2)[:, :, 0:NC_S], ACT.Gelu_apprx_tanh,
                                           bias=pe_col[:, kind:kind + 1]).then_inc(s_gelu, 1)
                        if not (last and u == 3):
                            keys_hi(b, u + 1, f)

            for f in range(8):
                keys_hi(0, 0, f)
            with act.Fori(0, NB - 1) as b:
                compress_act(b, False)
            compress_act(NB - 1, True)

            nrm = [0]

            def norm_act(x, ready, later):
                n = nrm[0]
                nrm[0] += 1
                ready()
                for g in range(4):
                    act.activation(sq[:, 4 * g:4 * g + 4, :], x[:, 4 * g:4 * g + 4, :], ACT.Square).then_inc(s_sq, 1)
                act.wait_ge(s_nsum, 3 * n + 2)
                act.activation(rbc[:, :], rbc[:, :], ACT.Sqrt).then_inc(s_nsum, 1)
                if later:
                    for g in range(4):
                        act.wait_ge(s_zt, 4 * n + g + 1)
                        act.activation(act_hi[:, 4 * g:4 * g + 4, :], sq[:, 4 * g:4 * g + 4, :], ACT.Copy).then_inc(s_z, 1)

            norm_act(x0, lambda: act.wait_ge(s_xld, 16), True)

            def hi(i, per, t, ch):
                act.wait_ge(s_raw[(t // 2) % 2], i * (4 * per) + 16 * (t // 4 + 1))
                act.wait_ge(s_chunk, i * (2 * per) + 2 * t + ch - 3 + CREDIT)
                act.activation(w_hi[:, (2 * t + ch) % 4], raw[:, (t // 2) % 2, CH * ch:CH * ch + CH, P * (t % 2):P * (t % 2) + P],
                               ACT.Copy).then_inc(s_hi, 1)

            def dense_act(t0, n, evac, per=4, last=False, outer=None):
                def body(i, stop):
                    for j in range(per):
                        t = t0 + j
                        ahead = not (stop and j >= per - 2)
                        step = i if outer is None else outer * 8 + i
                        if ahead:
                            hi(step, 4 if outer is not None else per, t + 2, 0)
                        evac(i, j)
                        if ahead:
                            hi(step, 4 if outer is not None else per, t + 2, 1)
                times = n // per
                with act.Fori(0, times - 1 if last else times) as i:
                    body(i, False)
                if last:
                    body(times - 1, True)

            def tile_done(i, t, per=4):
                act.wait_ge(s_chunk, i * (2 * per) + 2 * t + 2 + CREDIT)

            for c in range(4):
                hi(0, 4, c // 2, c % 2)

            def ev_conv(i, j):
                if j % 6 >= 4:
                    m = 2 * (j // 6) + j % 2
                    act.wait_ge(s_ev, i * 12 + T_CONV + j + 1 + CREDIT)
                    fence()
                    act.activation(z_hi[:, ds(i * 4 + m, 1), :], z_sb[:, j % 2, :].unsqueeze(1), ACT.Copy).then_inc(s_z, 1)

            dense_act(T_CONV, 48, ev_conv, per=12)
            act.wait_ge(s_cmp_st[0], 16 * 2 * NB)
            act.wait_ge(s_cmp_st[1], 16 * 2 * NB)

            def ev_to(dst, t0, func):
                def ev(i, j):
                    tile_done(i, t0 + j)
                    fence()
                    act.activation(dst[:, ds(i * 4 + j, 1), :], bank[j % 4][:, 0:NT].unsqueeze(1), func).then_inc(s_ev, 1)
                return ev

            act.wait_ge(s_zl, 16)
            dense_act(T_MC, 16, ev_to(mx, T_MC, ACT.Sigmoid))
            dense_act(T_WC, 16, lambda i, j: None)
            dense_act(T_MA, 16, ev_to(ga, T_MA, ACT.Sigmoid))
            act.wait_ge(s_gld, 16)
            act.wait_ge(s_ev, T_MA + CREDIT)
            act.activation(gw_hi[:, :, :], gw[:, :, :], ACT.Copy).then_inc(s_gate, 1)
            act.wait_ge(s_gate, 3)
            act.activation(gT[:, :], bank[7][0:48, 0:NT], ACT.Sigmoid).then_inc(s_gate, 1)
            act.wait_ge(s_gate, 4)
            dense_act(T_Q, 16, ev_to(qo, T_Q, ACT.Copy))
            act.wait_ge(s_gate, 7)
            act.wait_ge(s_gdma, 32)
            dense_act(T_KV, 24, ev_to(kv, T_KV, ACT.Copy), last=True)

            for kind in range(2):
                act.wait_ge(s_pe, 1 + kind)
                act.activation(gelu_p[:, kind], bank[6 + kind][:, 0:NKV * NC_P].rearrange("p (h c) -> p h c", h=NKV),
                               ACT.Gelu_apprx_tanh, bias=pe_col[:, kind:kind + 1]).then_inc(s_gelu, 1)
            with act.Fori(0, NKV) as h:
                for n in range(6):
                    tt, kg = n // 2, n % 2
                    act.wait_ge(s_rtr, h * 6 + n + 1)
                    act.wait_ge(s_rowfree, h + CREDIT)
                    act.wait_ge(s_pv, h * 8 + CREDIT)
                    rows_n = P if tt < 2 else NSM
                    k0, kn = (0, 4) if kg == 0 else (4, 2)
                    act.activation(rowsb[0:rows_n, tt, k0:k0 + kn, :],
                                   bank[n % 2][0:rows_n, 0:kn * P].rearrange("p (k d) -> p k d", d=P), ACT.Copy).then_inc(s_rev, 1)
                act.wait_ge(s_scev, h * 10 + 10 + CREDIT)
                for u in range(8):
                    nk = P * (u % 2 + 1)
                    for br in range(2):
                        act.activation(S_p[:, u, br, 0:nk], S_p[:, u, br, 0:nk], ACT.Exp, scale=SCALE,
                                       bias=nmp[:, u, 1 + br:2 + br], accum_out=den[:, u, 1 + br:2 + br]).then_inc(s_exp, 1)
                    act.activation(S_c[:, u, :], S_c[:, u, :], ACT.Exp, scale=SCALE,
                                   bias=nmp[:, u, 0:1], accum_out=den[:, u, 0:1]).then_inc(s_exp, 1)
                for f in range(10):
                    act.wait_ge(s_pt, h * 10 + f + 1)
                    act.wait_ge(s_pv, h * 8 + (f - 3 if f >= 2 else 0) + CREDIT)
                    if f < 2:
                        act.activation(PTc[:, 4 * f:4 * f + 4, :], bank[6][0:NC_P, :].rearrange("p (u q) -> p u q", q=P),
                                       ACT.Copy).then_inc(s_ptev, 1)
                    else:
                        u = f - 2
                        tiles = (0, 2) if u % 2 == 0 else (0, 1, 2, 3)
                        if u % 2 == 0:
                            act.activation(PT[:, u % 2, 0:4:2, :], bank[f % 2][:, :].rearrange("p (k q) -> p k q", q=P)[:, 0:4:2, :],
                                           ACT.Copy).then_inc(s_ptev, 1)
                        else:
                            act.activation(PT[:, u % 2, :, :], bank[f % 2][:, :].rearrange("p (k q) -> p k q", q=P),
                                           ACT.Copy).then_inc(s_ptev, 1)

            with act.Fori(0, NB) as b:
                act.wait_ge(s_sel, b * 12 + 3)
                act.activation(C_s[:, 0:NC_S], bank[4][:, 0:NC_S], ACT.Exp, scale=SCALE, bias=st[:, 3:4],
                               accum_out=st[:, 6:7]).then_inc(s_sexp, 1)
                for pc in range(5):
                    if pc == 1:
                        act.wait_ge(s_selp, b * 3 + 1)
                        act.activation(PTcs[:, :], bank[7][0:NC_S, 0:P], ACT.Copy).then_inc(s_sexp, 1)
                    for hd in range(0, NKV, 2):
                        act.wait_ge(s_ktr, b * 26 + 4 * pc + hd + 1 + 2 * CREDIT)
                        act.wait_ge(s_ssc, b * 6 + (pc if pc >= 2 else 0) + CREDIT)
                        act.activation(kT[:, pc % 2, hd, :], bank[0][:, :], ACT.Copy).then_inc(s_ktev[0], 1)
                for br in range(2):
                    act.wait_ge(s_sm, b * 5 + 1 + br)
                    w = S_s if br == 0 else W_s
                    act.activation(w[:, :], w[:, :], ACT.Exp, scale=SCALE, bias=st[:, 4 + br:5 + br],
                                   accum_out=st[:, 7 + br:8 + br]).then_inc(s_sexp, 1)
                for f in range(0, 6, 2):
                    act.wait_ge(s_ktr, b * 26 + 20 + f + 1 + 2 * CREDIT)
                    act.activation(PTs[:, 4 * f:4 * f + 4, :], bank[0][:, :].rearrange("p (k q) -> p k q", q=P),
                                   ACT.Copy).then_inc(s_ktev[0], 1)

            def split_act(src, wait_for):
                wait_for()
                for g in range(4):
                    act.activation(act_hi[:, 4 * g:4 * g + 4, :], src[:, 4 * g:4 * g + 4, :], ACT.Copy).then_inc(s_z, 1)

            split_act(qo, lambda: (act.wait_ge(s_so, NB + CREDIT), act.wait_ge(s_oev, 32 + CREDIT)))
            for c in range(4):
                hi(0, 4, T_WA + c // 2, c % 2)
            dense_act(T_WA, 16, lambda i, j: None)
            split_act(mx, lambda: act.wait_ge(s_m, 16))
            dense_act(T_WO, 16, lambda i, j: None)
            norm_act(x1, lambda: act.wait_ge(s_xadd, 16), True)

            def mlp(f, last):
                def ev_hidden(i, j):
                    n = f * 32 + i * 4
                    act.wait_ge(s_chunk, n * 2 + 2 * (T_MLP + j) + 2 + CREDIT)
                    act.wait_ge(s_hid, f * 16 + i * 4 + j - 3 + CREDIT)
                    act.activation(rl[:, j, :], bank[j][:, 0:NT], ACT.Relu).then_inc(s_ev, 1)
                    act.wait_ge(s_ev, n + T_MLP + j + 1 + CREDIT)
                    fence()
                    act.activation(hid_hi[:, ds(i * 4 + j, 1), :], rl[:, j, :].unsqueeze(1), ACT.Square).then_inc(s_hidh, 1)
                dense_act(T_MLP, 16, ev_hidden, outer=f)
                dense_act(T_MLP + 16, 16, lambda i, j: None, outer=f, last=last)

            with act.Fori(0, 3) as f:
                mlp(f, False)
            mlp(3, True)
            norm_act(x1, lambda: act.wait_ge(s_xadd, 80), False)
            for g in range(4):
                act.wait_ge(s_ftr, g + 1)
                act.activation(cs_rows[:, 4 * g:4 * g + 4, :], bank[g % 4][0:2 * NSEQ, :].rearrange("p (k q) -> p k q", q=P),
                               ACT.Copy).then_inc(s_fin, 1)
            for f in range(12):
                tt, g = f // 4, f % 4
                n = P if tt < 2 else NSM
                act.wait_ge(s_ftr, 4 + f + 1)
                if tt == 2:
                    act.wait_ge(s_out, 32)
                act.activation(y_rows[0:n, tt % 2, 512 * g:512 * g + 512], bank[f % 4][0:n, :], ACT.Copy).then_inc(s_fev, 1)

        @block.tensor
        def _(pe):
            mm, tr = nc.tensor.matmul, nc.tensor.transpose
            pe.sem_inc(s_chunk, CREDIT)
            pe.sem_inc(s_kt_bank, 2 * CREDIT)
            pe.sem_inc(s_cmp_h, CREDIT)
            pe.sem_inc(s_ada_pe, CREDIT)
            pe.sem_inc(s_pv, CREDIT)
            pe.sem_inc(s_ktr, 2 * CREDIT)
            pe.sem_inc(s_ssc, CREDIT)
            pe.sem_inc(s_spv, CREDIT)
            pe.wait_ge(s_const, 2)
            pe.wait_ge(s_rows, 16 * 14)
            tr(bank[0][:, 0:112], rows[0:112, 0, :], ident[0:112, 0:112])
            tr(bank[0][:, 128:224], rows[0:96, 1, :], ident[0:96, 0:96])
            tr(bank[0][:, 256:272], rows[0:16, 2, :], ident[0:16, 0:16])
            tr(bank[0][:, 288:320], rows[0:32, 6, :], ident[0:32, 0:32])
            tr(bank[0][:, 320:352], rows[0:32, 7, :], ident[0:32, 0:32]).then_inc(s_tr, 1)
            for k in range(3):
                last = tr(bank[1][:, P * k:P * k + P], rows[:, 3 + k, :], ident[:, :])
            last.then_inc(s_tr, 1)
            for k in range(KT):
                if k >= 4:
                    pe.wait_ge(s_x0, k - 3)
                for tt in range(3):
                    n = P if tt < 2 else NSM
                    last = tr(bank[2 + k % 4][:, P * tt:P * tt + n], x_rows[0:n, tt, P * k:P * k + P], ident[0:n, 0:n])
                last.then_inc(s_tr, 1)
            pe.wait_ge(s_w1, 64)
            pe.wait_ge(s_prm, 8)
            for kind in range(2):
                for r in range(CLEN):
                    last = mm(bank[7][:, kind:kind + 1], w1[:, kind, r, :], peT[:, kind, r:r + 1], start=(r == 0), stop=(r == CLEN - 1))
            last.then_inc(s_pe_b, 1)
            pe.wait_ge(s_x0, 16)
            pe.wait_ge(s_silu, 1)
            pe.wait_ge(s_pe_b, 2)
            pe.wait_ge(s_w1_lo, 3)

            def keys_bank(b, u, f):
                kind, pair = u // 2, u % 2
                if f == 0:
                    pe.wait_ge(s_page[pair], b * (32 * NPAGE) + 16 * NPAGE * (kind + 1))
                pe.wait_ge(s_kt_ev, b * 32 + 8 * u + f - 3 + CREDIT)
                for pg in range(4):
                    last = tr(bank[f % 4][:, P * pg:P * pg + P], pages[:, pair, 4 * (f % 4) + pg, P * (f // 4):P * (f // 4) + P], ident[:, :])
                last.then_inc(s_kt_bank, 1)

            def compress_pe(b, last_one):

                def ada_prod(p):
                    pe.wait_ge(s_ada[p % 2], b * 48 + 16 * (p // 2) + 16)
                    pe.wait_ge(s_ada_ev, b * 6 + p + CREDIT)
                    for kk in range(4):
                        for g in range(4):
                            last = mm(bank[7][32 * g:32 * g + 32, 0:256], cs[:, 4 * kk + g, :], ada_raw[:, p % 2, 4 * kk + g, :],
                                      start=(kk == 0), stop=(kk == 3))
                    last.then_inc(s_ada_pe, 1)

                def ada_turn(p):
                    pe.wait_ge(s_ada_row, b * 6 + p + 1)
                    for half in range(2):
                        last = mm(bank[7][:, 16 * half:16 * half + NSEQ], ada_row[:, P * half:P * half + P], sel9[:, :], start=True, stop=True)
                    last.then_inc(s_ada_t, 1)

                for u in range(4):
                    kind, pair = u // 2, u % 2
                    if u < 3:
                        ada_prod(2 * u)
                    pe.wait_ge(s_kt_ev, b * 32 + 8 * u + 8 + CREDIT)
                    pe.wait_ge(s_gelu, b * 4 + u - 1 + CREDIT)
                    hout = bank[4 + pair][:, 0:2 * P]
                    for f in range(8):
                        for r in range(6 * f, min(6 * f + 6, CLEN)):
                            k_hi, k_lo = (k[:, pair, r:r + CSTR * (2 * P - 1) + 1:CSTR] for k in (keyT_hi, keyT_lo))
                            mm(hout, w1_hi[:, kind, r, :], k_hi, start=(r == 0), stop=False)
                            mm(hout, w1_lo[:, kind, r, :], k_hi, start=False, stop=False)
                            last = mm(hout, w1_hi[:, kind, r, :], k_lo, start=False, stop=(r == CLEN - 1))
                            if r == CLEN - 1:
                                last.then_inc(s_cmp_h, 1)
                        if not (last_one and u == 3):
                            keys_bank(b, u + 1, f)
                        if u < 3:
                            if f in (1, 5):
                                ada_turn(2 * u + f // 4)
                            elif f == 3:
                                ada_prod(2 * u + 1)
                    pe.wait_ge(s_gelu, b * 4 + u + 1 + CREDIT)
                    pe.wait_ge(s_cmp_ev, b * 4 + u + CREDIT)
                    if kind == 0:
                        last = mm(bank[6][:, 0:2 * NC_S], w2[:, 0, :], gelu[:, :], start=True, stop=True)
                    else:
                        for hh in range(2):
                            last = mm(bank[6][0:NC_S, P * hh:P * hh + P], gelu[:, NC_S * hh:NC_S * hh + NC_S], w2[:, 1, :],
                                      start=True, stop=True)
                    last.then_inc(s_cmp_o, 1)

            for f in range(8):
                keys_bank(0, 0, f)
            with pe.Fori(0, NB - 1) as b:
                compress_pe(b, False)
            compress_pe(NB - 1, True)

            nrm = [0]

            def norm_pe():
                n = nrm[0]
                nrm[0] += 1
                for k in range(KT):
                    if k % 4 == 0:
                        pe.wait_ge(s_sq, 4 * n + k // 4 + 1)
                    last = mm(bank[7][:, 0:NT], ones[:, :], sq[:, k, :], start=(k == 0), stop=(k == KT - 1))
                last.then_inc(s_nsum, 1)

            norm_pe()

            def dense_pe(t0, n, x_hi, x_lo, per=4, outer=None, first=None):
                times = n // per
                if first is not None:
                    first()
                with pe.Fori(0, times) as i:
                    for j in range(per):
                        t = t0 + j
                        step = i * per if outer is None else outer * 32 + i * 4
                        pe.wait_ge(s_ev, step + t + 1 - 4 + CREDIT)
                        for ch in range(2):
                            pe.wait_ge(s_lo, step * 2 + 2 * t + ch + 1 + CREDIT)
                            buf = (2 * t + ch) % 4
                            for k in range(CH):
                                kk = CH * ch + k
                                out = bank[t % 4][:, 0:NT]
                                mm(out, w_hi[:, buf, k, :], x_hi[:, kk, :], start=(kk == 0), stop=False)
                                mm(out, w_lo[:, buf, k, :], x_hi[:, kk, :], start=False, stop=False)
                                last = mm(out, w_hi[:, buf, k, :], x_lo[:, kk, :], start=False, stop=(kk == KT - 1))
                            last.then_inc(s_chunk, 1)

            pe.wait_ge(s_h, 4)
            dense_pe(T_CONV, 48, act_hi, act_lo, per=12)
            dense_pe(T_MC, 16, act_hi, act_lo, first=lambda: pe.wait_ge(s_ev, T_MC + CREDIT))
            dense_pe(T_WC, 16, z_hi, z_lo, first=lambda: (pe.wait_ge(s_ev, T_WC + CREDIT), pe.wait_ge(s_zl, 16)))
            dense_pe(T_MA, 16, act_hi, act_lo, first=lambda: pe.wait_ge(s_ev, T_MA + CREDIT))
            pe.wait_ge(s_gate, 2)
            for k in range(KT):
                mm(bank[7][:, 0:NT], gw_hi[:, k, :], act_hi[:, k, :], start=(k == 0), stop=False)
                mm(bank[7][:, 0:NT], gw_lo[:, k, :], act_hi[:, k, :], start=False, stop=False)
                last = mm(bank[7][:, 0:NT], gw_hi[:, k, :], act_lo[:, k, :], start=False, stop=(k == KT - 1))
            last.then_inc(s_gate, 1)
            pe.wait_ge(s_gate, 5)
            for qt in range(2):
                last = tr(bank[6][:, 64 * qt:64 * qt + 48], gT[:, P * qt:P * qt + P], ident[0:48, 0:48])
            last.then_inc(s_gate, 1)
            dense_pe(T_Q, 16, act_hi, act_lo, first=lambda: pe.wait_ge(s_ev, T_Q + CREDIT))
            dense_pe(T_KV, 24, act_hi, act_lo, first=lambda: pe.wait_ge(s_ev, T_KV + CREDIT))

            pe.wait_ge(s_ev, T_WA + CREDIT)
            pe.wait_ge(s_gate, 7)
            pe.wait_ge(s_w1, 128)
            for kind in range(2):
                hout = bank[6 + kind][:, 0:NKV * NC_P].rearrange("p (h c) -> p h c", h=NKV)
                for r in range(CLEN):
                    last = mm(hout, w1p[:, kind, r, :], kv[:, 4 * kind:4 * kind + 4, r:r + CSTR * (NC_P - 1) + 1:CSTR],
                              start=(r == 0), stop=(r == CLEN - 1))
                last.then_inc(s_pe, 1)
            pe.wait_ge(s_gelu, 4 * NB + 1 + CREDIT)
            mm(bank[4][:, 0:NKV * NC_P], w2p[:, 0, :], gelu_p[:, 0].rearrange("p h c -> p (h c)"), start=True, stop=True).then_inc(s_pe, 1)
            pe.wait_ge(s_gelu, 4 * NB + 2 + CREDIT)
            for h in range(NKV):
                last = mm(bank[5][0:NC_P, P * h:P * h + P], gelu_p[:, 1, h, :], w2p[:, 1, :], start=True, stop=True)
            last.then_inc(s_pe, 1)
            pe.wait_ge(s_cpp, 2)
            with pe.Fori(0, NKV) as h:
                pe.wait_ge(s_bun, h * 5 + 5)
                for n in range(6):
                    tt, kg = n // 2, n % 2
                    if n >= 2:
                        pe.wait_ge(s_rev, h * 6 + n - 1 + CREDIT)
                    else:
                        pe.wait_ge(s_ptev, h * 10 + CREDIT)
                    pe.sem_inc(s_pass[1], 1)
                    rows_n = P if tt < 2 else NSM
                    k0, kn = (0, 4) if kg == 0 else (4, 2)
                    for k in range(kn):
                        last = tr(bank[n % 2][0:rows_n, P * k:P * k + P], kv_b[:, k0 + k, P * tt:P * tt + rows_n], ident[:, :])
                    last.then_inc(s_rtr, 1)
                pe.wait_ge(s_oev, h * 8 + CREDIT)
                for u in range(8):
                    g, qt = u // 2, u % 2
                    last = mm(bank[7][:, 16 * u:16 * u + NC_P], q_b[:, g, P * qt:P * qt + P], kc_b[:, :], start=True, stop=True)
                last.then_inc(s_sc, 1)
                for u in range(8):
                    g, qt = u // 2, u % 2
                    nk = P * (qt + 1)
                    if u >= 4:
                        pe.wait_ge(s_scev, h * 10 + 1 + (u - 4) + 1 + CREDIT)
                    mm(bank[2 + u % 4][:, 0:nk], q_b[:, g, P * qt:P * qt + P], kv_b[:, 2, 0:nk], start=True, stop=True)
                    mm(bank[2 + u % 4][:, NPR:NPR + nk], q_b[:, g, P * qt:P * qt + P], kv_b[:, 4, 0:nk],
                       start=True, stop=True).then_inc(s_sc, 1)
                pe.wait_ge(s_rev, h * 6 + 6 + CREDIT)
                for f in range(2):
                    pe.wait_ge(s_exp, h * 24 + 12 * f + 12)
                    if f == 1:
                        pe.wait_ge(s_ptev, h * 10 + 1 + CREDIT)
                    for k in range(4):
                        last = tr(bank[6][0:NC_P, P * k:P * k + P], S_c[:, 4 * f + k, :], ident[:, :])
                    last.then_inc(s_pt, 1)

                def turn(u):
                    pe.wait_ge(s_exp, h * 24 + 3 * u + 3)
                    if u >= 2:
                        pe.wait_ge(s_ptev, h * 10 + u + 1 + CREDIT)
                    for k in ((0, 2) if u % 2 == 0 else (0, 1, 2, 3)):
                        last = tr(bank[u % 2][:, P * k:P * k + P], S_p[:, u, k // 2, P * (k % 2):P * (k % 2) + P], ident[:, :])
                    last.then_inc(s_pt, 1)

                turn(0)
                for u in range(8):
                    if u < 7:
                        turn(u + 1)
                    o = bank[2 + u % 4]
                    if u >= 4:
                        pe.wait_ge(s_orow, h * 8 + u - 3)
                    pe.wait_ge(s_ptev, h * 10 + 2 + u + 1 + CREDIT)
                    mm(o[:, 0:P], PTc[:, u, :], vc_b[:, :], start=True, stop=True)
                    for br, kind in ((1, 3), (2, 5)):
                        for t in range(u % 2 + 1):
                            last = mm(o[:, P * br:P * br + P], PT[:, u % 2, 2 * (br - 1) + t, :], rowsb[:, t, kind, :],
                                      start=(t == 0), stop=(t == u % 2))
                    last.then_inc(s_pv, 1)
                    for w in ([u - 1] if u else []) + ([7] if u == 7 else []):
                        pe.wait_ge(s_orow, h * 8 + w + 1)
                        pe.wait_ge(s_oev, h * 8 + w - 1 + CREDIT)
                        tr(bank[7 - w % 2][:, 0:P], o_row[:, w % 2, :], ident[:, :]).then_inc(s_otr, 1)

            pe.wait_ge(s_oev, 32 + CREDIT)
            pe.wait_ge(s_sel, 1)
            with pe.Fori(0, NB) as b:
                pe.wait_ge(s_new, b * 2 + 2)
                pe.wait_ge(s_cd, b * 32 + 32)
                pe.wait_ge(s_so, b + CREDIT)
                for h in range(NKV):
                    qh = q_s[:, 32 * h:32 * h + 32]
                    mm(bank[4][32 * h:32 * h + 32, 0:NC_S], qh, kc_s[:, 0, h, :], start=True, stop=True)
                for h in range(NKV):
                    qh = q_s[:, 32 * h:32 * h + 32]
                    mm(bank[4][32 * h:32 * h + 32, P:P + NSTEP], qh, knew[:, h, :], start=True, stop=True)
                for h in range(NKV):
                    qh = q_s[:, 32 * h:32 * h + 32]
                    last = mm(bank[4][32 * h:32 * h + 32, P + NSTEP:P + 2 * NSTEP], qh, knew[:, 8 + h, :], start=True, stop=True)
                last.then_inc(s_ssc, 1)
                for br in range(2):
                    for h in range(NKV):
                        last = tr(bank[5 + br][0:NSTEP, P * h:P * h + P], knew[:, 8 * br + 4 + h, :], ident[:, :])
                last.then_inc(s_vnt, 1)

                def keys(pc):
                    slot = pc % 2 if pc < 4 else 2
                    if pc < 4:
                        pe.wait_ge(s_kd[slot], b * 128 + 64 * (pc // 2 + 1))
                    else:
                        pe.wait_ge(s_kd[2], b * 16 + 16)
                    for h in range(NKV):
                        pe.wait_ge(s_ktev[h % 2], b * 13 + 2 * pc + h // 2 + CREDIT)
                        for k in range(4):
                            last = tr(bank[h % 2][:, P * k:P * k + P], krow[:, slot, k, P * h:P * h + P], ident[:, :])
                        last.then_inc(s_ktr, 1)

                def scores(pc):
                    for par in range(2):
                        pe.wait_ge(s_ktev[par], b * 13 + 2 * pc + 2 + CREDIT)
                    if pc >= 2:
                        pe.wait_ge(s_sev, b * 5 + pc - 1 + CREDIT)
                    for h in range(NKV):
                        last = mm(bank[2 + pc % 2][32 * h:32 * h + 32, :], q_s[:, 32 * h:32 * h + 32], kT[:, pc % 2, h, :],
                                  start=True, stop=True)
                    last.then_inc(s_ssc, 1)

                keys(0)
                pe.wait_ge(s_sexp, b * 4 + 1)
                tr(bank[7][0:NC_S, 0:P], C_s[:, 0:NC_S], ident[:, :]).then_inc(s_selp, 1)
                keys(1)
                pe.wait_ge(s_sexp, b * 4 + 2)
                mm(bank[7][:, P:P + NSB], PTcs[:, :], selw[0:NC_S, :], start=True, stop=True).then_inc(s_selp, 1)
                scores(0)
                pe.wait_ge(s_sel, b * 12 + 5)
                mm(bank[7][:, 192:192 + NSB], grp[:, :], z_s[:, :], start=True, stop=True).then_inc(s_selp, 1)
                keys(2)
                scores(1)
                keys(3)
                scores(2)
                keys(4)
                scores(3)
                scores(4)
                for f in range(6):
                    pe.wait_ge(s_ktev[f % 2], b * 13 + 10 + f // 2 + CREDIT)
                    pe.wait_ge(s_sexp, b * 4 + (3 if f < 4 else 4))
                    for k in range(4 if f < 5 else 0):
                        src = S_s[:, 512 * f + P * k:512 * f + P * k + P] if f < 4 else W_s[:, P * k:P * k + P]
                        last = tr(bank[f % 2][:, P * k:P * k + P], src, ident[:, :])
                    if f == 5:
                        tr(bank[1][0:NSTEP, 0:P], S_s[:, PAST:PAST + NSTEP], ident[:, :])
                        last = tr(bank[1][0:NSTEP, P:2 * P], W_s[:, WIN:WIN + NSTEP], ident[:, :])
                    last.then_inc(s_ktr, 1)
                for par in range(2):
                    pe.wait_ge(s_ktev[par], b * 13 + 13 + CREDIT)
                pe.wait_ge(s_vne, b * 2 + 2)
                pe.wait_ge(s_sev, b * 5 + 5 + CREDIT)

                def weigh(acc, probs, values, start, stop):
                    for h in range(NKV):
                        last = mm(bank[acc][32 * h:32 * h + 32, 0:P], probs[:, 32 * h:32 * h + 32], values[:, P * h:P * h + P],
                                  start=start, stop=stop)
                    return last

                pe.wait_ge(s_vd[2], b * 16 + 16)
                for k in range(4):
                    weigh(3, PTs[:, 16 + k, :], vrow[:, 2, k, :], k == 0, False)
                weigh(3, PTn[:, 1, :], vnew[:, 1, :], False, True)
                weigh(4, PTcs[:, :], vc_s[:, 0].rearrange("p h d -> p (h d)"), True, True)
                weigh(2, PTn[:, 0, :], vnew[:, 0, :], True, False)
                for c in range(4):
                    pe.wait_ge(s_vd[c % 2], b * 128 + 64 * (c // 2 + 1))
                    for k in range(4):
                        last = weigh(2, PTs[:, 4 * c + k, :], vrow[:, c % 2, k, :], False, c == 3 and k == 3)
                    if c % 2 == 1:
                        last.then_inc(s_spv, 1)
                pe.wait_ge(s_sm, b * 5 + 5)
                tr(bank[6][:, 0:P], os_row[:, :], ident[:, :]).then_inc(s_sot, 1)

            pe.wait_ge(s_h, 8)
            dense_pe(T_WA, 16, act_hi, act_lo)
            dense_pe(T_WO, 16, act_hi, act_lo, first=lambda: (pe.wait_ge(s_ev, T_WO + CREDIT), pe.wait_ge(s_h, 12)))
            norm_pe()
            pe.wait_ge(s_h, 16)

            def outer_first(taken, hidden=None):
                pe.wait_ge(s_ev, taken)
                if hidden is not None:
                    pe.wait_ge(s_hid, hidden)
                pe.sem_inc(s_pass[1], 1)

            with pe.Fori(0, 4) as f:
                dense_pe(T_MLP, 16, act_hi, act_lo, outer=f, first=lambda: outer_first(f * 32 + T_MLP + CREDIT))
                dense_pe(T_MLP + 16, 16, hid_hi, hid_lo, outer=f,
                         first=lambda: outer_first(f * 32 + T_MLP + 16 + CREDIT, f * 16 + 16 + CREDIT))
            norm_pe()
            for g in range(4):
                for k in range(4):
                    last = tr(bank[g][0:2 * NSEQ, P * k:P * k + P], cstate[:, 4 * g + k, :], ident[:, :])
                last.then_inc(s_ftr, 1)
            for f in range(12):
                tt, g = f // 4, f % 4
                n = P if tt < 2 else NSM
                if f < 4:
                    pe.wait_ge(s_fin, f + 1)
                    pe.wait_ge(s_zt, 8 + f + 1)
                else:
                    pe.wait_ge(s_fev, f - 3)
                for k in range(4):
                    last = tr(bank[f % 4][0:n, P * k:P * k + P], sq[:, 4 * g + k, P * tt:P * tt + n], ident[:, :])
                last.then_inc(s_ftr, 1)

        @block.vector
        def _(dve):
            for c in (s_kt_ev, s_cmp_free[0], s_cmp_free[1], s_cmp_ev, s_ada_ev, s_lo, s_ev, s_scev, s_oev, s_ktev[1], s_sev, s_so, s_hid):
                dve.sem_inc(c, CREDIT)
            step = Steps(dve, s_dv)
            V = nc.vector

            def seq(ins):
                step.did(ins)
                step.wait()

            dve.wait_ge(s_tr, 2)
            V.tensor_copy(params[:, :], bank[0][:, 0:112]).then_inc(s_prm, 1)
            V.tensor_copy(b_ada[:, :], bank[0][:, 128:224]).then_inc(s_prm, 1)
            V.tensor_copy(cT[:, :, 0], bank[0][:, 256:272]).then_inc(s_prm, 1)
            V.tensor_copy(peT[:, 0, :], bank[0][:, 288:320]).then_inc(s_prm, 1)
            V.tensor_copy(peT[:, 1, :], bank[0][:, 320:352]).then_inc(s_prm, 1)
            V.tensor_copy(cT[:, :, 1:NSEQ], bank[1][:, 0:P].rearrange("p (b t) -> p t b", b=NB)).then_inc(s_prm, 1)
            for k in range(2):
                V.tensor_copy(prevT[:, 8 * k:8 * k + 8, :],
                              bank[1][:, P + P * k:2 * P + P * k].rearrange("p (r t) -> p r t", r=8)).then_inc(s_prm, 1)

            V.memset(cs[:, :, :], 0.0).then_inc(s_prm, 1)
            V.tensor_reduce(sel9[:, :], ident[:, :].rearrange("p (g s) -> p s g", g=4)[:, 0:NSEQ, :], AX.X, ALU.add).then_inc(s_prm, 1)
            dve.wait_ge(s_pe_b, 1)
            V.tensor_copy(pe_col[:, :], bank[7][:, 0:2]).then_inc(s_pe_b, 1)
            for kind in range(2):
                dve.wait_ge(s_w1_hi, kind + 1)
                V.tensor_tensor(w1_lo[:, kind], w1[:, kind], w1_hi[:, kind].bitcast(F32), ALU.subtract).then_inc(s_w1_lo, 1)

            dve.wait_ge(s_w1_hi, 3)
            V.tensor_tensor(keyT_lo[:, :, 2 * PAST:KEYS], keyT_hi[:, :, 2 * PAST:KEYS].bitcast(F32), keyT_hi[:, :, 2 * PAST:KEYS].bitcast(F32),
                            ALU.subtract).then_inc(s_w1_lo, 1)

            def keys_lo(b, u, f):
                dve.wait_ge(s_kt_hi, b * 32 + 8 * u + f + 1)
                part = (slice(None), u % 2, slice(512 * f, 512 * f + 512))
                V.tensor_tensor(keyT_lo[part], bank[f % 4][:, :], keyT_hi[part].bitcast(F32), ALU.subtract).then_inc(s_kt_ev, 1)

            def compress_dve(b, last):
                for u in range(4):
                    kind, pair = u // 2, u % 2

                    def ada_out(p):
                        dve.wait_ge(s_ada_t, b * 6 + p + 1)
                        V.tensor_tensor(ada[:, ds(b * 12 + 2 * p, 2), :],
                                        bank[7][:, 0:32].rearrange("p (a c) -> p a c", a=2)[:, :, 0:NSEQ],
                                        b_ada[:, ds(b * 12 + 2 * p, 2)].unsqueeze(2).to_broadcast([P, 2, NSEQ]), ALU.add).then_inc(s_ada_ev, 1)

                    for f in range(8):
                        if not (last and u == 3):
                            keys_lo(b, u + 1, f)
                        if f in (2, 5) and u < 3:
                            ada_out(2 * u + f // 4)
                    dve.wait_ge(s_cmp_free[kind], b * 2 + pair + CREDIT)
                    dve.wait_ge(s_cmp_o, b * 4 + u + 1 + CREDIT)
                    if kind == 0:
                        V.tensor_copy(kc_out[:, :, :], bank[6][:, 0:2 * NC_S].rearrange("p (h c) -> p h c", h=2)).then_inc(s_cmp_ev, 1)
                    else:
                        V.tensor_copy(vc_out[:, :, :], bank[6][0:NC_S, 0:2 * P].rearrange("p (h d) -> p h d", h=2)).then_inc(s_cmp_ev, 1)

            for f in range(8):
                keys_lo(0, 0, f)
            with dve.Fori(0, NB - 1) as b:
                compress_dve(b, False)
            compress_dve(NB - 1, True)
            dve.wait_ge(s_ada_ev, 48 + CREDIT)
            dve.wait_ge(s_cmp_o, 4 * NB + CREDIT)
            sh1, sc1v, gt1, sh2, sc2v, gt2 = (ada[:, 16 * k:16 * k + 16, :] for k in range(6))

            nrm = [0]

            def rstd():
                n = nrm[0]
                nrm[0] += 1
                dve.wait_ge(s_nsum, 3 * n + 1)
                V.tensor_scalar(rbc[:, :], bank[7][:, 0:NT], 1.0 / D, EPS, ALU.mult, ALU.add).then_inc(s_nsum, 1)
                dve.wait_ge(s_nsum, 3 * n + 3)
                seq(V.reciprocal(rbc[:, :], rbc[:, :]))
                return n

            def per_seq(v, k0, kn):
                return v[:, k0:k0 + kn, 1:NSEQ].unsqueeze(3).to_broadcast([P, kn, NB, NSTEP])

            def by_seq(x):
                return x.rearrange("p k (b s) -> p k b s", b=NB)

            def lo(i, per, t, ch):
                dve.wait_ge(s_hi, i * (2 * per) + 2 * t + ch + 1)
                buf = (2 * t + ch) % 4
                V.tensor_tensor(w_lo[:, buf], raw[:, (t // 2) % 2, CH * ch:CH * ch + CH, P * (t % 2):P * (t % 2) + P],
                                w_hi[:, buf].bitcast(F32), ALU.subtract).then_inc(s_lo, 1)

            def modulate(x, gain, shift, scale, z0):
                seq(V.scalar_tensor_tensor(out=a_mul[:, :, :], in0=scale, scalar=1.0,
                                           in1=gain.unsqueeze(2).to_broadcast([P, KT, NSEQ]), op0=ALU.add, op1=ALU.mult))
                n = rstd()
                for g in range(4):
                    k4 = slice(4 * g, 4 * g + 4)
                    seq(V.tensor_tensor(sq[:, k4, :], x[:, k4, :], rbc[:, :].unsqueeze(1).to_broadcast([P, 4, NT]), ALU.mult))
                    seq(V.tensor_tensor(sq[:, k4, 0:NPR], sq[:, k4, 0:NPR],
                                        a_mul[:, k4, 0:1].to_broadcast([P, 4, NPR]), ALU.mult))
                    seq(V.tensor_tensor(by_seq(sq[:, k4, NPR:NT]), by_seq(sq[:, k4, NPR:NT]), per_seq(a_mul, 4 * g, 4), ALU.mult))
                    seq(V.tensor_tensor(sq[:, k4, 0:NPR], sq[:, k4, 0:NPR],
                                        shift[:, k4, 0:1].to_broadcast([P, 4, NPR]), ALU.add))
                    V.tensor_tensor(by_seq(sq[:, k4, NPR:NT]), by_seq(sq[:, k4, NPR:NT]), per_seq(shift, 4 * g, 4), ALU.add).then_inc(s_zt, 1)
                    dve.wait_ge(s_zt, 4 * n + g + 1)
                for g in range(4):
                    k4 = slice(4 * g, 4 * g + 4)
                    dve.wait_ge(s_z, z0 + g + 1)
                    V.tensor_tensor(act_lo[:, k4, :], sq[:, k4, :], act_hi[:, k4, :].bitcast(F32), ALU.subtract).then_inc(s_h, 1)

            modulate(x0, g1n, sh1, sc1v, 0)

            def dense_dve(t0, n, evac, per=4, last=False, outer=None, chain=0):
                def body(i, stop):
                    for j in range(per):
                        t = t0 + j
                        ahead = not (stop and j >= per - 2)
                        base = i if outer is None else outer * 8 + i
                        if ahead:
                            lo(base, 4 if outer is not None else per, t + 2, 0)
                        evac(i, j)
                        if ahead:
                            lo(base, 4 if outer is not None else per, t + 2, 1)
                times = n // per
                loops = times - 1 if last else times
                with dve.Fori(0, loops) as i:
                    step.enter(i, chain)
                    body(i, False)
                    step.leave(loops)
                if last:
                    body(times - 1, True)

            def tile_done(i, t, per=4):
                dve.wait_ge(s_chunk, i * (2 * per) + 2 * t + 2 + CREDIT)

            for c in range(4):
                lo(0, 4, c // 2, c % 2)
            seq(V.memset(up_p[:, :, 0:2], 0.0))

            def ev_conv(i, j):
                kind, m = (j % 6) // 2, j % 2
                kt = i * 4 + 2 * (j // 6) + m
                ps = bank[j % 4]
                dve.wait_ge(s_ev, i * 12 + T_CONV + j + CREDIT)
                if kind == 0:
                    tile_done(i, T_CONV + j, 12)
                    V.tensor_copy(u_sb[:, m, :], ps[:, 0:NT]).then_inc(s_ev, 1)
                elif kind == 1:
                    seq(V.tensor_scalar(up_s[:, m, :, 0:2], prevT[:, :, ds(kt, 1)].rearrange("p (b j) a -> p b (j a)", j=2), 1.0, None, ALU.mult))
                    tile_done(i, T_CONV + j, 12)
                    seq(V.tensor_tensor(up_p[:, m, 2:NPR + 2], ps[:, 0:NPR], u_sb[:, m, 0:NPR], ALU.mult))
                    V.tensor_tensor(up_s[:, m, :, 2:NSTEP + 2], ps[:, NPR:NT].rearrange("p (b s) -> p b s", b=NB),
                                    u_sb[:, m, NPR:NT].rearrange("p (b s) -> p b s", b=NB), ALU.mult).then_inc(s_ev, 1)
                    dve.wait_ge(s_ev, i * 12 + T_CONV + j + 1 + CREDIT)
                    seq(V.tensor_scalar(cstate[:, ds(kt, 1), 0:2], up_p[:, m, NPR:NPR + 2].unsqueeze(1), 1.0, None, ALU.mult))
                    seq(V.tensor_scalar(cstate[:, ds(kt, 1), 2:2 * NSEQ].rearrange("p a (b j) -> p (a b) j", j=2),
                                        up_s[:, m, :, NSTEP:NSTEP + 2], 1.0, None, ALU.mult))
                else:
                    y_p = y_sb[:, m, 0:NPR]
                    y_s = y_sb[:, m, NPR:NT].rearrange("p (b s) -> p b s", b=NB)
                    w = [v[:, ds(kt, 1)] for v in cvw]
                    seq(V.tensor_scalar(y_p, up_p[:, m, 0:NPR], w[0], cvb[:, ds(kt, 1)], ALU.mult, ALU.add))
                    seq(V.tensor_scalar(y_s, up_s[:, m, :, 0:NSTEP], w[0], cvb[:, ds(kt, 1)], ALU.mult, ALU.add))
                    for r in (1, 2):
                        seq(V.scalar_tensor_tensor(out=y_p, in0=up_p[:, m, r:NPR + r], scalar=w[r], in1=y_p, op0=ALU.mult, op1=ALU.add))
                        seq(V.scalar_tensor_tensor(out=y_s, in0=up_s[:, m, :, r:NSTEP + r], scalar=w[r], in1=y_s, op0=ALU.mult, op1=ALU.add))
                    dve.wait_ge(s_z, i * 4 + 4 + 2 * (j // 6))
                    tile_done(i, T_CONV + j, 12)
                    V.tensor_tensor(z_sb[:, m, :], y_sb[:, m, :], ps[:, 0:NT], ALU.mult).then_inc(s_ev, 1)
                    dve.wait_ge(s_z, i * 4 + 4 + 2 * (j // 6) + m + 1)
                    V.tensor_tensor(z_lo[:, ds(kt, 1), :], z_sb[:, m, :].unsqueeze(1), z_hi[:, ds(kt, 1), :].bitcast(F32), ALU.subtract).then_inc(s_zl, 1)

            dense_dve(T_CONV, 48, ev_conv, per=12, chain=40)
            dense_dve(T_MC, 16, lambda i, j: None)

            def ev_wc(i, j):
                tile_done(i, T_WC + j)
                kt = ds(i * 4 + j, 1)
                V.tensor_tensor(mx[:, kt, :], mx[:, kt, :], bank[j][:, 0:NT].unsqueeze(1), ALU.mult).then_inc(s_ev, 1)

            dve.wait_ge(s_ev, T_WC + CREDIT)
            dense_dve(T_WC, 16, ev_wc)
            dense_dve(T_MA, 16, lambda i, j: None)
            dve.wait_ge(s_gate, 1)
            V.tensor_tensor(gw_lo[:, :, :], gw[:, :, :], gw_hi[:, :, :].bitcast(F32), ALU.subtract).then_inc(s_gate, 1)
            dve.wait_ge(s_gate, 4)
            V.tensor_copy(gTs[:, :, :], gT[:, NPR:NT].rearrange("p (b s) -> p s b", b=NB)).then_inc(s_gate, 1)
            dve.wait_ge(s_gate, 6)
            V.tensor_copy(gate_p[:, :, :], bank[6][:, 0:P].rearrange("p (q c) -> p q c", q=2)[:, :, 0:48]).then_inc(s_gate, 1)
            dense_dve(T_Q, 16, lambda i, j: None)
            dense_dve(T_KV, 24, lambda i, j: None, last=True)

            dve.wait_ge(s_pe, 3)
            V.tensor_copy(kc_p[:, :, :], bank[4][:, 0:NKV * NC_P].rearrange("p (h c) -> p h c", h=NKV)).then_inc(s_cpp, 1)
            dve.wait_ge(s_pe, 4)
            V.tensor_copy(vc_p[:, :, :], bank[5][0:NC_P, :].rearrange("p (h d) -> p h d", h=NKV)).then_inc(s_cpp, 1)
            dve.wait_ge(s_cpp, 2)
            dve.wait_ge(s_pool, 10)
            with dve.Fori(0, NKV) as h:
                step.enter(h, 24)
                dve.wait_ge(s_oev, h * 8 + CREDIT)
                V.tensor_scalar(q_b[:, :, :], qo[:, ds(h * GRP, GRP), 0:NPR], 1.0, None, ALU.mult).then_inc(s_bun, 1)
                V.tensor_scalar(kv_b[:, :, :], kv[:, :, :].rearrange("p (k h) t -> p k h t", h=NKV)[:, :, ds(h, 1), :].rearrange("p k a t -> p k (a t)"),
                                1.0, None, ALU.mult).then_inc(s_bun, 1)
                for qt in range(2):
                    last = V.tensor_scalar(gate_b[:, :, :, qt], gate_p[:, qt, :].rearrange("p (r h) -> p r h", r=3)[:, :, ds(h * GRP, GRP)],
                                           1.0, None, ALU.mult)
                    if qt == 0:
                        seq(last)
                    else:
                        last.then_inc(s_bun, 1)
                V.tensor_scalar(kc_b[:, :], kc_p[:, ds(h, 1), :].rearrange("p a c -> p (a c)"), 1.0, None, ALU.mult).then_inc(s_bun, 1)
                V.tensor_scalar(vc_b[:, :], vc_p[:, ds(h, 1), :].rearrange("p a c -> p (a c)"), 1.0, None, ALU.mult).then_inc(s_bun, 1)
                dve.wait_ge(s_bun, h * 5 + 5)
                dve.wait_ge(s_sc, h * 9 + 1)
                V.tensor_tensor(S_c[:, :, :].rearrange("p (g q) c -> p g q c", q=2),
                                bank[7][:, 0:P].rearrange("p (g q c) -> p g q c", g=GRP, q=2)[:, :, :, 0:NC_P],
                                mask_c[:, :, :].unsqueeze(1).to_broadcast([P, GRP, 2, NC_P]), ALU.add).then_inc(s_scev, 1)
                for u in range(8):
                    qt = u % 2
                    nk = P * (qt + 1)
                    dve.wait_ge(s_sc, h * 9 + 1 + u + 1)
                    V.tensor_tensor(S_p[:, u, :, 0:nk], bank[2 + u % 4][:, :].rearrange("p (r k) -> p r k", r=2)[:, :, 0:nk],
                                    mask_p[:, qt:qt + 1, 0:nk].to_broadcast([P, 2, nk]), ALU.add).then_inc(s_scev, 1)
                dve.wait_ge(s_scev, h * 10 + 9 + CREDIT)
                seq(V.tensor_reduce(mxp[:, :, 0], S_c[:, :, :], AX.X, ALU.max))
                S4 = S_p[:, :, :, :].rearrange("p (g q) r k -> p g q r k", q=2)
                M4 = mxp[:, :, :].rearrange("p (g q) r -> p g q r", q=2)
                for qt in range(2):
                    seq(V.tensor_reduce(M4[:, :, qt, 1:3], S4[:, :, qt, :, 0:P * (qt + 1)], AX.X, ALU.max))
                V.tensor_scalar(nmp[:, :, :], mxp[:, :, :], -SCALE, -0.01 * NEG, ALU.mult, ALU.min).then_inc(s_scev, 1)
                dve.wait_ge(s_exp, h * 24 + 24)
                seq(V.tensor_scalar(den[:, :, :], den[:, :, :], 1e-30, None, ALU.max))
                seq(V.reciprocal(rr[:, :, :], den[:, :, :]))
                seq(V.tensor_tensor(rr[:, :, :].rearrange("p (g q) r -> p g q r", q=2), rr[:, :, :].rearrange("p (g q) r -> p g q r", q=2),
                                    gate_b[:, :, :, :].rearrange("p r g q -> p g q r"), ALU.mult))
                seq(V.tensor_tensor(rr[:, :, 0].rearrange("p (g q) -> p g q", q=2), rr[:, :, 0].rearrange("p (g q) -> p g q", q=2),
                                    vis[:, :].unsqueeze(1).to_broadcast([P, GRP, 2]), ALU.mult))

                def store(w):
                    dve.wait_ge(s_otr, h * 8 + w + 1)
                    V.tensor_scalar(qo[:, ds(h * GRP + w // 2, 1), P * (w % 2):P * (w % 2) + P],
                                    bank[7 - w % 2][:, 0:P].unsqueeze(1), 1.0, None, ALU.mult).then_inc(s_oev, 1)

                for u in range(8):
                    o = bank[2 + u % 4]
                    dve.wait_ge(s_pv, h * 8 + u + 1 + CREDIT)
                    if u >= 2:
                        dve.wait_ge(s_otr, h * 8 + u - 1)
                    seq(V.tensor_scalar(o_row[:, u % 2, :], o[:, 0:P], rr[:, u, 0:1], None, ALU.mult))
                    seq(V.scalar_tensor_tensor(out=o_row[:, u % 2, :], in0=o[:, P:2 * P], scalar=rr[:, u, 1:2], in1=o_row[:, u % 2, :],
                                               op0=ALU.mult, op1=ALU.add))
                    V.scalar_tensor_tensor(out=o_row[:, u % 2, :], in0=o[:, 2 * P:3 * P], scalar=rr[:, u, 2:3], in1=o_row[:, u % 2, :],
                                           op0=ALU.mult, op1=ALU.add).then_inc(s_orow, 1)
                    if u >= 1:
                        store(u - 1)
                store(7)
                step.leave(NKV)

            dve.wait_ge(s_pool, POOL_STEPS)
            seq(V.tensor_tensor(selw[:, :], selw[:, :], sc1[:, :], ALU.add))
            seq(V.tensor_copy(colf[:, :], coli[:, :]))
            seq(V.tensor_scalar(rowi[:, 1:2], rowi[:, 0:1], 7, None, ALU.bitwise_and))
            seq(V.tensor_scalar(rowi[:, 2:3], rowi[:, 0:1], 5, 3, ALU.logical_shift_right, ALU.logical_shift_left))
            seq(V.tensor_copy(rowf[:, 0:3], rowi[:, 0:3]))
            seq(V.tensor_tensor(rowf[:, 3:4], rowf[:, 1:2], rowf[:, 2:3], ALU.add))
            seq(V.tensor_scalar(rowf[:, 2:3], rowf[:, 1:2], float(WIN), None, ALU.add))
            seq(V.tensor_scalar(mask_w[:, :], colf[:, :], rowf[:, 1:2], NEG, ALU.is_le, ALU.mult))
            seq(V.tensor_scalar(mask_n[:, :], colf[:, 0:NSTEP], rowf[:, 1:2], NEG, ALU.is_gt, ALU.mult))
            seq(V.tensor_scalar(coli[:, P:2 * P], coli[:, 0:P], 5, 3, ALU.logical_shift_right, ALU.logical_shift_left))
            seq(V.tensor_scalar(coli[:, 0:P], coli[:, 0:P], 7, None, ALU.bitwise_and))
            seq(V.tensor_copy(grpf[:, :], coli[:, 0:P]))
            seq(V.tensor_copy(grp[:, :], coli[:, P:2 * P]))
            seq(V.tensor_tensor(grpf[:, :], grpf[:, :], grp[:, :], ALU.add))
            seq(V.tensor_scalar(grp[:, :], grpf[:, :], rowf[:, 3:4], None, ALU.is_equal))
            seq(V.tensor_copy(mask_w[:, WIN:WIN + NSTEP], mask_n[:, :]))
            dve.wait_ge(s_gdma, 32)
            V.tensor_copy(rowf[:, 0:1], rowf[:, 1:2]).then_inc(s_sel, 1)
            with dve.Fori(0, NB) as b:
                step.enter(b, 6)
                dve.wait_ge(s_sel, b * 12 + 1)
                dve.wait_ge(s_so, b + CREDIT)
                V.tensor_scalar(q_s[:, :].rearrange("p (h s) -> p h s", h=NH), qo[:, :, ds(b * NSTEP + NPR, NSTEP)], 1.0, None, ALU.mult).then_inc(s_new, 1)
                V.tensor_scalar(knew[:, :, :], kv[:, 8:24, ds(b * NSTEP + NPR, NSTEP)], 1.0, None, ALU.mult).then_inc(s_new, 1)
                dve.wait_ge(s_ssc, b * 6 + 1 + CREDIT)
                seq(V.tensor_tensor(S_s[:, PAST:PAST + NSTEP], bank[4][:, P:P + NSTEP], mask_n[:, :], ALU.add))
                seq(V.tensor_tensor(W_s[:, WIN:WIN + NSTEP], bank[4][:, P + NSTEP:P + 2 * NSTEP], mask_n[:, :], ALU.add))
                V.tensor_reduce(st[:, 0:1], bank[4][:, 0:NC_S], AX.X, ALU.max).then_inc(s_sel, 1)
                dve.wait_ge(s_sel, b * 12 + 2)
                V.tensor_scalar(st[:, 3:4], st[:, 0:1], -SCALE, None, ALU.mult).then_inc(s_sel, 1)
                dve.wait_ge(s_vnt, b + 1)
                for br in range(2):
                    V.tensor_copy(vnew[:, br, :], bank[5 + br][0:NSTEP, :]).then_inc(s_vne, 1)

                def keys_out(pc):
                    for hd in range(1, NKV, 2):
                        dve.wait_ge(s_ktr, b * 26 + 4 * pc + hd + 1 + 2 * CREDIT)
                        dve.wait_ge(s_ssc, b * 6 + (pc if pc >= 2 else 0) + CREDIT)
                        V.tensor_copy(kT[:, pc % 2, hd, :], bank[1][:, :]).then_inc(s_ktev[1], 1)

                def scores_out(pc):
                    dve.wait_ge(s_ssc, b * 6 + 1 + pc + 1 + CREDIT)
                    if pc < 4:
                        V.tensor_tensor(S_s[:, 512 * pc:512 * pc + 512].rearrange("p (n k) -> p n k", k=SLC),
                                        bank[2 + pc % 2][:, :].rearrange("p (n k) -> p n k", k=SLC),
                                        selb[:, 8 * pc:8 * pc + 8].unsqueeze(2).to_broadcast([P, 8, SLC]), ALU.add).then_inc(s_sev, 1)
                    else:
                        V.tensor_tensor(W_s[:, 0:WIN], bank[2][:, :], mask_w[:, 0:WIN], ALU.add).then_inc(s_sev, 1)

                keys_out(0)
                dve.wait_ge(s_sexp, b * 4 + 1)
                V.reciprocal(st[:, 9:10], st[:, 6:7]).then_inc(s_sel, 1)
                dve.wait_ge(s_sel, b * 12 + 4)
                keys_out(1)
                dve.wait_ge(s_selp, b * 3 + 2)
                V.tensor_scalar(z_s[:, :], bank[7][:, P:P + NSB], st[:, 9:10], None, ALU.mult).then_inc(s_sel, 1)
                dve.wait_ge(s_selp, b * 3 + 3)
                picks = [
                    lambda: V.tensor_copy(sc1[:, :], bank[7][:, 192:192 + NSB]),
                    lambda: V.memset(sc1[:, 0:1], -NEG),
                    lambda: V.memset(sc1[:, NSB - 2:NSB], -NEG),
                    lambda: V.max(top8[:, :], sc1[:, :]),
                    lambda: V.match_replace(sc2[:, :], top8[:, :], sc1[:, :], NEG),
                    lambda: V.max(top8[:, :], sc2[:, :]),
                    lambda: V.match_replace(sc1[:, :], top8[:, :], sc2[:, :], NEG),
                    lambda: V.tensor_scalar(selb[:, :], sc1[:, :], 0.5 * NEG, NEG, ALU.is_gt, ALU.mult),
                ]
                for k, pick in enumerate(picks):
                    dve.wait_ge(s_sel, b * 12 + 5 + k)
                    dve.sem_inc(s_pass[0], 1)
                    pick().then_inc(s_sel, 1)
                dve.wait_ge(s_sel, b * 12 + 13)
                keys_out(2)
                scores_out(0)
                keys_out(3)
                scores_out(1)
                keys_out(4)
                scores_out(2)
                scores_out(3)
                scores_out(4)
                dve.wait_ge(s_sev, b * 5 + 5 + CREDIT)
                seq(V.tensor_reduce(st[:, 1:2], S_s[:, :], AX.X, ALU.max))
                V.tensor_scalar(st[:, 4:5], st[:, 1:2], -SCALE, None, ALU.mult).then_inc(s_sm, 1)
                seq(V.tensor_reduce(st[:, 2:3], W_s[:, :], AX.X, ALU.max))
                V.tensor_scalar(st[:, 5:6], st[:, 2:3], -SCALE, None, ALU.mult).then_inc(s_sm, 1)
                for f in range(1, 6, 2):
                    dve.wait_ge(s_ktr, b * 26 + 20 + f + 1 + 2 * CREDIT)
                    if f < 5:
                        V.tensor_copy(PTs[:, 4 * f:4 * f + 4, :], bank[1][:, :].rearrange("p (k q) -> p k q", q=P)).then_inc(s_ktev[1], 1)
                    else:
                        V.tensor_copy(PTn[:, :, :], bank[1][0:NSTEP, 0:2 * P].rearrange("p (k q) -> p k q", q=P)).then_inc(s_ktev[1], 1)
                dve.wait_ge(s_sexp, b * 4 + 4)
                seq(V.reciprocal(st[:, 9:12], st[:, 6:9]))
                seq(V.tensor_tensor(st[:, 9:12], st[:, 9:12], gate_s[:, :, ds(b, 1)].rearrange("p r a -> p (r a)"), ALU.mult))
                dve.wait_ge(s_spv, b * 2 + 2 + CREDIT)
                V.tensor_scalar(os_row[:, :], bank[4][:, 0:P], st[:, 9:10], None, ALU.mult).then_inc(s_sm, 1)
                for br, acc in ((1, 2), (2, 3)):
                    dve.wait_ge(s_sm, b * 5 + 2 + br)
                    V.scalar_tensor_tensor(out=os_row[:, :], in0=bank[acc][:, 0:P], scalar=st[:, 9 + br:10 + br], in1=os_row[:, :],
                                           op0=ALU.mult, op1=ALU.add).then_inc(s_sm, 1)
                dve.wait_ge(s_sot, b + 1)
                V.tensor_scalar(qo[:, :, ds(b * NSTEP + NPR, NSTEP)], bank[6][:, 0:P].rearrange("p (h s) -> p h s", h=NH), 1.0, None,
                                ALU.mult).then_inc(s_so, 1)
                step.leave(NB)

            def split_dve(src, z0):
                for g in range(4):
                    dve.wait_ge(s_z, z0 + g + 1)
                    k4 = slice(4 * g, 4 * g + 4)
                    V.tensor_tensor(act_lo[:, k4, :], src[:, k4, :], act_hi[:, k4, :].bitcast(F32), ALU.subtract).then_inc(s_h, 1)

            split_dve(qo, 20)
            for c in range(4):
                lo(0, 4, T_WA + c // 2, c % 2)

            def ev_wa(i, j):
                kt = ds(i * 4 + j, 1)
                tile_done(i, T_WA + j)
                V.tensor_tensor(ga[:, kt, :], ga[:, kt, :], bank[j][:, 0:NT].unsqueeze(1), ALU.mult).then_inc(s_ev, 1)
                dve.wait_ge(s_ev, i * 4 + T_WA + j + 1 + CREDIT)
                V.tensor_tensor(mx[:, kt, :], mx[:, kt, :], ga[:, kt, :], ALU.add).then_inc(s_m, 1)

            dense_dve(T_WA, 16, ev_wa)
            dve.wait_ge(s_m, 16)
            split_dve(mx, 24)
            dve.wait_ge(s_xld1, 16)

            def ev_add(gate, t0, outer=None):
                def ev(i, j):
                    kt = ds(i * 4 + j, 1)
                    if outer is None:
                        tile_done(i, t0 + j)
                    else:
                        dve.wait_ge(s_chunk, outer * 64 + i * 8 + 2 * (t0 + j) + 2 + CREDIT)
                    seq(V.scalar_tensor_tensor(out=x1[:, kt, 0:NPR], in0=bank[j][:, 0:NPR].unsqueeze(1), scalar=gate[:, kt, 0:1].rearrange("p a c -> p (a c)"),
                                               in1=x1[:, kt, 0:NPR], op0=ALU.mult, op1=ALU.add))
                    V.tensor_tensor(tmp_s[:, :].rearrange("p (b s) -> p b s", b=NB), bank[j][:, NPR:NT].rearrange("p (b s) -> p b s", b=NB),
                                    gate[:, kt, 1:NSEQ].rearrange("p a b -> p (a b)").unsqueeze(2).to_broadcast([P, NB, NSTEP]), ALU.mult).then_inc(s_ev, 1)
                    step0 = i * 4 if outer is None else outer * 32 + i * 4
                    dve.wait_ge(s_ev, step0 + t0 + j + 1 + CREDIT)
                    V.tensor_tensor(x1[:, kt, NPR:NT], x1[:, kt, NPR:NT], tmp_s[:, :].unsqueeze(1), ALU.add).then_inc(s_xadd, 1)
                    dve.wait_ge(s_xadd, (i * 4 if outer is None else outer * 16 + i * 4 + 16) + j + 1)
                return ev

            dense_dve(T_WO, 16, ev_add(gt1, T_WO), chain=4)
            modulate(x1, g2n, sh2, sc2v, 28)

            def mlp(f, last):
                def ev_hidden(i, j):
                    n = f * 16 + i * 4 + j + 1
                    dve.wait_ge(s_hidh, n)
                    seq(V.tensor_tensor(rl2[:, j, :], rl[:, j, :], rl[:, j, :], ALU.mult))
                    V.tensor_tensor(hid_lo[:, ds(i * 4 + j, 1), :], rl2[:, j, :].unsqueeze(1), hid_hi[:, ds(i * 4 + j, 1), :].bitcast(F32),
                                    ALU.subtract).then_inc(s_hid, 1)
                dense_dve(T_MLP, 16, ev_hidden, outer=f, chain=4)
                dense_dve(T_MLP + 16, 16, ev_add(gt2, T_MLP + 16, outer=f), outer=f, last=last, chain=4)

            with dve.Fori(0, 3) as f:
                step.enter(f, 32)
                mlp(f, False)
                step.leave(3)
            mlp(3, True)
            rstd()
            for g in range(4):
                k4 = slice(4 * g, 4 * g + 4)
                seq(V.tensor_tensor(sq[:, k4, :], x1[:, k4, :], rbc[:, :].unsqueeze(1).to_broadcast([P, 4, NT]), ALU.mult))
                V.tensor_tensor(sq[:, k4, :], sq[:, k4, :], gfn[:, k4].unsqueeze(2).to_broadcast([P, 4, NT]), ALU.mult).then_inc(s_zt, 1)


_INS = ["x_prompt", "x_sample", "c_prompt", "c_sample", "cache_nsa_kv", "page_table", "state_win_kv", "state_conv",
        "w_ada", "b_ada", "norm1_g", "norm2_g", "w_in", "w_cmp_k1", "w_cmp_k2", "pe_cmp_k", "w_cmp_v1", "w_cmp_v2", "pe_cmp_v",
        "conv_w", "conv_b", "w_attn_proj", "w_conv_proj", "w_out", "w_mlp1", "w_mlp2", "normf_g"]
_OUTS = [("y_prompt", (1, 256, 2048)), ("y_sample", (8, 8, 2048)), ("kv_prompt", (1, 1, 256, 4, 4, 128)),
         ("kv_sample", (1, 8, 8, 4, 4, 128)), ("win_prompt", (1, 1, 256, 2, 4, 128)), ("win_sample", (1, 8, 512, 2, 4, 128)),
         ("conv_prompt", (1, 1, 2, 2048)), ("conv_sample", (1, 8, 2, 2048))]


def kernel(**inputs):
    import numpy as _np
    import concourse.bacc as _bacc
    from concourse import mybir as _mybir
    from concourse.bass_utils import run_bass_kernel_spmd as _run

    nc = _bacc.Bacc("TRN2", target_bir_lowering=False, num_devices=1)
    arrays, A = {}, {}
    for name in _INS:
        a = _np.ascontiguousarray(inputs[name])
        arrays[f"in_{name}"] = a
        A[name] = nc.dram_tensor(f"in_{name}", a.shape, _mybir.dt.from_np(a.dtype), kind="ExternalInput").ap()
    for name, shape in _OUTS:
        A[f"out_{name}"] = nc.dram_tensor(f"res_{name}", shape, _mybir.dt.float32, kind="ExternalOutput").ap()
    build_step(nc, A)
    r = _run(nc, [arrays], core_ids=[0])
    return tuple(r.results[0][f"res_{name}"] for name, _ in _OUTS)
```

```python
import concourse.bass as bass
from concourse import mybir
from contextlib import ExitStack

F32 = mybir.dt.float32
F32R = mybir.dt.float32r
I32 = mybir.dt.int32
ALU = mybir.AluOpType
ACT = mybir.ActivationFunctionType
AX = mybir.AxisListType
ds = bass.ds

P = 128
D = 2048
KT = D // P
NPR = 256
NB, NSTEP = 8, 8
NSM = NB * NSTEP
NT = NPR + NSM
NSEQ = 1 + NB
NH, NKV, GRP, HD = 16, 4, 4, 128
KVW = NKV * HD
PAST = 2048
PAGE = 128
NPAGE = PAST // PAGE
WIN = 512
CLEN, CSTR = 32, 16
NC_S = PAST // CSTR - 1
NC_P = NPR // CSTR - 1
SLC = 64
NSB = PAST // SLC + 1
FF = 4 * D
EPS = 1e-6
NEG = -1e30
SCALE = HD ** -0.5

COL_Q, COL_KV, COL_G = 0, D, D + 6 * KVW
COL_U = COL_G + 3 * NH
COL_B, COL_C = COL_U + D, COL_U + 2 * D
COL_MA, COL_MC = COL_U + 3 * D, COL_U + 4 * D

T_CONV, T_MC, T_WC, T_MA, T_Q, T_KV = 0, 48, 64, 80, 96, 112
T_WA, T_WO, T_MLP, T_END = 136, 152, 168, 296
CH = KT // 2
POOL_STEPS = 18
CREDIT = 8


class Steps:

    def __init__(self, eng, sem, first=0):
        self.eng, self.sem, self.base, self.k, self.regs = eng, sem, first, 0, []

    def did(self, ins):
        ins.then_inc(self.sem, 1)
        self.k += 1
        return self

    def value(self):
        v = self.base + self.k
        for reg, per, k in self.regs:
            v = reg * per + v + k
        return v

    def wait(self):
        self.eng.wait_ge(self.sem, self.value())

    def enter(self, reg, per):
        self.regs.append((reg, per, self.k))
        self.k = 0

    def leave(self, times):
        reg, per, before = self.regs.pop()
        assert self.k == per, f"{self.sem}: {self.k} steps in an iteration, {per} stated"
        self.k = before + per * times


def build_step(nc, A):
    ctx = ExitStack()
    with ctx:
        def at(name, shape, offset, dt=F32):
            return nc.alloc_sbuf_tensor_at("sb_" + name, shape, dt, offset=offset)

        def sem(name):
            return ctx.enter_context(nc.semaphore(name))

        def dram(name, shape):
            return nc.dram_tensor("scratch_" + name, shape, F32, kind="Internal").ap()

        TOK = KT * NT * 4
        A_SMALL = 16512
        A_HI = A_SMALL + 11776
        A_LO = A_HI + TOK
        A_Q = A_LO + TOK
        A_KV = A_Q + TOK
        A_GA = A_KV + 24 * NT * 4
        A_MX = A_GA + TOK
        A_RING = A_MX + TOK + 256
        A_END = 229344

        used = [A_SMALL]

        def small(name, shape, dt=F32):
            n = 4
            for s in shape[1:]:
                n *= s
            o = used[0]
            used[0] = o + (n + 31) // 32 * 32
            assert used[0] <= A_HI, (name, used[0], A_HI)
            return at(name, shape, o, dt)

        ident = small("ident", [P, P])
        ones = small("ones", [P, P])
        params = small("params", [P, 112])
        b_ada = small("b_ada", [P, 96])
        ada = small("ada", [P, 96, NSEQ])
        page_ids = small("page_ids", [1, NB * NPAGE], I32)
        A_CS = used[0]
        cs = at("cs", [P, KT, 32], A_CS)
        a_mul = small("a_mul", [P, KT, NSEQ])
        tmp_s = small("tmp_s", [P, NSM])
        gate_p = small("gate_p", [P, 2, 48])
        gate_s = small("gate_s", [P, 3, NB])
        cstate = small("cstate", [P, KT, 2 * NSEQ])
        assert used[0] >= A_CS + KT * 32 * 4
        sel9 = small("sel9", [P, NSEQ])
        rbc = small("rbc", [P, NT])
        pe_col = small("pe_col", [P, 2])
        prevT = small("prevT", [P, 2 * NB, KT])
        ada_row = small("ada_row", [P, 256])
        A_ROW = used[0] - 1024
        peT = at("peT", [P, 96], used[0] - 1024)
        cT = at("cT", [P, KT, NSEQ], used[0] - 640)
        g1n, g2n, gfn, cvb = (params[:, 16 * i:16 * i + 16] for i in range(4))
        cvw = [params[:, 64 + 16 * j:80 + 16 * j] for j in range(3)]

        act_hi = at("act_hi", [P, KT, NT], A_HI, F32R)
        act_lo = at("act_lo", [P, KT, NT], A_LO, F32R)
        z_hi = at("z_hi", [P, KT, NT], A_Q, F32R)
        z_lo = at("z_lo", [P, KT, NT], A_GA, F32R)
        mx_hi = at("mx_hi", [P, KT, NT], A_Q, F32R)
        mx_lo = at("mx_lo", [P, KT, NT], A_KV, F32R)
        hid_hi = at("hid_hi", [P, KT, NT], A_Q, F32R)
        hid_lo = at("hid_lo", [P, KT, NT], A_MX, F32R)
        qo = at("qo", [P, NH, NT], A_Q)
        kv = at("kv", [P, 24, NT], A_KV)
        ga = at("ga", [P, KT, NT], A_GA)
        mx = at("mx", [P, KT, NT], A_MX)
        x0_a = at("x0_a", [P, 12, NT], A_RING + 16384)
        x0_b = at("x0_b", [P, 4, NT], A_RING + 32768 + 16384 + 8192)
        x1 = at("x1", [P, KT, NT], A_GA)
        sq = at("sq", [P, KT, NT], A_Q)
        raw = at("raw", [P, 2, KT, 256], A_RING)
        w_hi = at("w_hi", [P, 4, CH, P], A_RING + 32768, F32R)
        w_lo = at("w_lo", [P, 4, CH, P], A_RING + 32768 + 16384, F32R)
        ada_raw = at("ada_raw", [P, 2, KT, 256], A_RING + 32768)
        sqt = at("sqt", [P, 4, NT], A_KV + 20480)
        A_CV = A_KV + TOK
        up_p = at("up_p", [P, 2, NPR + 2], A_CV)
        up_s = at("up_s", [P, 2, NB, NSTEP + 2], A_CV + 2080)
        u_sb = at("u_sb", [P, 2, NT], A_CV + 2080 + 640)
        y_sb = at("y_sb", [P, 2, NT], A_CV + 2080 + 640 + 2560)
        z_sb = at("z_sb", [P, 2, NT], A_MX)
        gw_hi = at("gw_hi", [P, KT, P], A_Q, F32R)
        gw_lo = at("gw_lo", [P, KT, P], A_Q + 8192, F32R)
        gw = at("gw", [P, KT, P], A_KV)
        gT = at("gT", [48, NT], A_KV + 8192)
        gTs = at("gTs", [48, NSTEP, NB], A_KV + 8192 + 1280)
        x_rows = at("x_rows", [P, 3, D], A_RING + 32768)
        rows = at("rows", [P, 8, P], A_RING + 32768 + 3 * D * 4)
        sq_start = at("sq_start", [P, 4, NT], A_HI + 98304)
        pe_rows = at("pe_rows", [P, 256], A_HI + 98304 + 5120)
        w1_hi = at("w1_hi", [P, 2, 32, P], A_HI, F32R)
        w1_lo = at("w1_lo", [P, 2, 32, P], A_HI + 32768, F32R)
        w1 = at("w1", [P, 2, 32, P], A_HI + 65536)
        KEYS = 2 * PAST + CSTR
        keyT_hi = at("keyT_hi", [P, 2, KEYS], A_HI + 65536, F32R)
        keyT_lo = at("keyT_lo", [P, 2, KEYS], A_HI + 65536 + 8 * KEYS, F32R)
        pages = at("pages", [P, 2, NPAGE, 2 * HD], A_RING)
        A_T = A_HI + 65536 + 16 * KEYS
        gelu = at("gelu", [P, 2 * NC_S], A_T)
        kc_out = at("kc_out", [P, 2, NC_S], A_T + 1024)
        assert A_T + 2048 <= A_RING
        A_T2 = A_RING + 65536
        vc_out = at("vc_out", [NC_S, 2, P], A_T2)
        w2 = at("w2", [P, 2, P], A_T2 + 1024)
        A_P = A_RING + 32768
        w1p = at("w1p", [P, 2, 32, P], A_RING)
        w2p = at("w2p", [P, 2, P], A_HI + 16384)
        gelu_p = at("gelu_p", [P, 2, NKV, NC_P], A_HI + 17408)
        kc_p = at("kc_p", [P, NKV, NC_P], A_HI + 17920)
        vc_p = at("vc_p", [NC_P, NKV, P], A_HI + 18176)
        mask_p = at("mask_p", [P, 2, NPR], A_HI + 20224)
        mask_c = at("mask_c", [P, 2, NC_P], A_HI + 22272)
        vis = at("vis", [P, 2], A_HI + 22400)
        q_b = at("q_b", [P, GRP, NPR], A_P)
        kv_b = at("kv_b", [P, 6, NT], A_P + 4096)
        gate_b = at("gate_b", [P, 3, GRP, 2], A_P + 11776)
        rowsb = at("rowsb", [P, 3, 6, P], A_P + 11904)
        S_p = at("S_p", [P, 8, 2, NPR], A_HI + 24576)
        S_c = at("S_c", [P, 8, NC_P], A_P + 21120)
        mxp = at("mxp", [P, 8, 3], A_P + 21632)
        nmp = at("nmp", [P, 8, 3], A_P + 21728)
        den = at("den_p", [P, 8, 3], A_P + 21824)
        rr = at("rr_p", [P, 8, 3], A_P + 21920)
        PT = at("PT_p", [P, 2, 4, P], A_P + 22016)
        PTc = at("PTc_p", [NC_P, 8, P], A_P + 26112)
        o_row = at("o_row", [P, 2, P], A_P + 30208)
        kc_b = at("kc_b", [P, NC_P], A_P + 31744)
        vc_b = at("vc_b", [NC_P, P], A_P + 31808)
        assert A_P + 32320 <= A_RING + 65088 and A_RING + 67200 <= A_END
        A_S = A_HI
        krow = at("krow", [P, 3, 4, KVW], A_S)
        kT = at("kT", [P, 2, NKV, 512], A_S + 24576)
        vrow = [at(f"vrow{i}", [P, 4, KVW], o) for i, o in enumerate((A_RING, A_RING + 8192, A_KV, A_KV + 8192, A_KV + 16384))]
        k_new_all = at("k_new_all", [P, 16, NSM], A_RING + 16384)
        S_s = at("S_s", [P, PAST + NSTEP], A_RING + 24576)
        W_s = at("W_s", [P, WIN + NSTEP], A_RING + 24576 + 8224)
        C_s = at("C_s", [P, P], A_RING + 24576 + 8224 + 2080)
        PTs = at("PTs", [P, 20, P], A_RING + 35392)
        PTn = at("PTn", [NSTEP, 2, P], A_RING + 45632)
        PTcs = [at("PTcs0", [NC_S, P], A_RING + 46656), at("PTcs1", [NC_S, P], A_KV + 24576)]
        kc_s = at("kc_s", [P, 2, NKV, NC_S], A_RING + 47168)
        vc_s = at("vc_s", [NC_S, 2, NKV, P], A_RING + 51232)
        A_M = A_RING + 55328
        q_s = [at("q_s0", [P, P], A_M), at("q_s1", [P, P], A_KV + 25088)]
        knew = [at("knew0", [P, 16, NSTEP], A_M + 512), at("knew1", [P, 16, NSTEP], A_KV + 25600)]
        vnew = [at("vnew0", [NSTEP, 2, KVW], A_M + 1024), at("vnew1", [NSTEP, 2, KVW], A_RING + 20480)]
        mask_w = at("mask_w", [P, WIN + NSTEP], A_RING + 65088)
        mask_n = at("mask_n", [P, NSTEP], A_RING + 67168)
        selw = at("selw", [P, NSB], A_ROW)
        grp = at("grp", [P, P], A_ROW + 160)
        z_s = at("z_s", [P, NSB], A_M + 7904)
        sc1 = at("sc1", [P, NSB], A_ROW + 672)
        sc2 = at("sc2", [P, NSB], A_M + 8224)
        selb = at("selb", [P, NSB], A_M + 8384)
        top8 = at("top8", [P, 8], A_M + 8544)
        st2 = [at("st0", [P, 12], A_M + 8576), at("st1", [P, 12], A_M + 9152)]
        os_row = at("os_row", [P, P], A_M + 8640)
        rowi = at("rowi", [P, 4], A_ROW + 832, I32)
        rowf = at("rowf", [P, 4], A_ROW + 864)
        coli = at("coli", [P, WIN + NSTEP], A_S + 24576, I32)
        colf = at("colf", [P, WIN + NSTEP], A_S + 26656)
        grpf = at("grpf", [P, P], A_S + 28736)
        assert A_M + 9728 <= A_END, (A_M + 9728, A_END)
        y_rows = at("y_rows", [P, 2, D], A_HI)
        cs_rows = at("cs_rows", [2 * NSEQ, KT, P], A_KV)
        rl = at("rl", [P, 4, NT], A_KV + 10240)
        rl2 = at("rl2", [P, 4, NT], A_KV + 10240 + 5120)

        bank = [ctx.enter_context(nc.psum_tensor(f"bank{i}", [P, 512], F32)) for i in range(8)]

        w_ada = A["w_ada"][0].rearrange("(t p) n -> p t n", p=P)
        w_in = A["w_in"][0].rearrange("(t p) n -> p t n", p=P)
        w_attn = A["w_attn_proj"][0].rearrange("(t p) n -> p t n", p=P)
        w_conv = A["w_conv_proj"][0].rearrange("(t p) n -> p t n", p=P)
        w_out = A["w_out"][0].rearrange("(t p) n -> p t n", p=P)
        w_mlp1 = A["w_mlp1"][0].rearrange("(t p) n -> p t n", p=P)
        w_mlp2 = A["w_mlp2"][0].rearrange("(f t p) n -> f p t n", p=P, t=KT)
        cache = A["cache_nsa_kv"][0].rearrange("g p k h d -> g p k (h d)")
        win = A["state_win_kv"][0].rearrange("b (c p) k h d -> b p c k (h d)", p=P)
        kc_d = dram("kc", [NB, P, NKV, NC_S])
        vc_d = dram("vc", [NB, NC_S, NKV, P])
        x_d = dram("x", [P, KT, NT])
        g_d = dram("gates", [48, NSTEP, NB])

        s_rows = sem("start_rows_loaded")
        s_xrows = sem("x_rows_loaded")
        s_w1 = sem("compress_weights_loaded")
        s_const = sem("constants_made")
        s_tr = sem("start_transposes_done")
        s_prm = sem("start_rows_turned")
        s_x0 = sem("x_feature_major")
        s_ids = sem("page_ids_loaded")
        s_page = [sem("pair0_pages_loaded"), sem("pair1_pages_loaded")]
        s_w1_hi = sem("compress_weights_hi")
        s_w1_lo = sem("compress_weights_lo")
        s_kt_bank = sem("key_bank_filled")
        s_kt_hi = sem("key_bank_hi_copied")
        s_kt_ev = sem("key_bank_split")
        s_cmp_h = sem("compress_hidden_done")
        s_gelu = sem("compress_gelu_done")
        s_cmp_o = sem("compress_out_done")
        s_cmp_ev = sem("compress_out_copied")
        s_cmp_st = [sem("kc_stored"), sem("vc_stored")]
        s_cmp_free = [sem("kc_out_free"), sem("vc_out_free")]
        s_pe_b = sem("pe_bias_summed")
        s_ada = [sem(f"ada_panel_loaded{i}") for i in range(2)]
        s_ada_pe = sem("ada_panel_multiplied")
        s_ada_row = sem("ada_rows_copied")
        s_ada_t = sem("ada_rows_turned")
        s_ada_ev = sem("ada_panel_copied")
        s_silu = sem("silu_of_c_done")
        s_sq = sem("squares_done")
        s_sqp0 = sem("start_squares_summed")
        s_sqt = sem("tile_squares_done")
        s_sqp = sem("tile_squares_summed")
        s_zero = sem("zero_tile_made")
        s_nsum = sem("square_sums_done")
        s_h = sem("operand_split_done")
        s_raw = [sem(f"weight_panel_loaded{i}") for i in range(2)]
        s_hi = sem("weight_hi_ready")
        s_lo = sem("weight_lo_ready")
        s_chunk = sem("chunk_multiplied")
        s_ev = sem("tile_taken_out")
        s_z = sem("z_split_done")
        s_zl = sem("z_lo_ready")
        s_zt = sem("scaled_group_ready")
        s_cpp = sem("prompt_compressed_copied")
        s_m = sem("merge_done")
        s_gate = sem("gate_step")
        s_gld = sem("gate_weights_loaded")
        s_gdma = sem("gates_moved")
        s_pe = sem("tensor_misc")
        s_dv = sem("dve_chain")
        s_xsp = sem("x_spilled")
        s_xadd = sem("x_tile_updated")
        s_xld = sem("x_back")
        s_xld1 = sem("x_back_after_attention")
        s_pool = sem("pool_chain")
        s_out = sem("outputs_written")
        s_win = sem("window_rows_written")
        s_rowdma = sem("kv_rows_written")
        s_rowfree = sem("kv_rows_free")
        s_bun = sem("head_bundle_copied")
        s_vcb = sem("head_values_bundle_copied")
        s_rtr = sem("kv_rows_turned")
        s_rev = sem("kv_rows_copied")
        s_sc = sem("scores_done")
        s_scev = sem("scores_copied")
        s_exp = sem("exps_done")
        s_pt = sem("probs_turned")
        s_ptev = sem("probs_turned_copied")
        s_pv = sem("values_summed")
        s_orow = sem("head_out_mixed")
        s_otr = sem("head_out_turned")
        s_oev = sem("head_out_stored")
        s_kd = [sem(f"sample_keys_loaded{i}") for i in range(3)]
        s_vd = [sem(f"sample_values_loaded{i}") for i in range(5)]
        s_ptr = sem("sample_probs_bank_turned")
        s_cexp = sem("sample_compressed_exps_done")
        s_kall = sem("all_new_rows_copied")
        s_cd = [sem("sample_compressed_loaded0"), sem("sample_compressed_loaded1")]
        s_ktr = sem("sample_keys_turned")
        s_ktev = [sem("sample_bank_copied_act"), sem("sample_bank_copied_dve")]
        s_hidh = sem("hidden_hi_ready")
        s_ssc = sem("sample_scores_done")
        s_sev = sem("sample_scores_copied")
        s_spv = sem("sample_values_summed")
        s_sel = sem("selection_step")
        s_selp = sem("selection_products")
        s_sexp = sem("sample_exps_done")
        s_new = sem("new_rows_copied")
        s_vnt = sem("new_values_turned")
        s_vne = sem("new_values_copied")
        s_so = sem("sample_out_stored")
        s_sm = sem("sample_out_mixed")
        s_sot = sem("sample_out_turned")
        s_hid = sem("hidden_ready")
        s_fin = sem("final_step")
        s_ftr = sem("final_turned")
        s_fev = [sem("final_copied_act"), sem("final_copied_dve")]
        s_pass = [sem("passed_dve"), sem("passed_pe"), sem("passed_pool")]

        block = ctx.enter_context(nc.Block())

        def banks_before(n, pc):
            return 2 * pc if isinstance(n, int) and n == 0 else n * 13 + 2 * pc - (3 if pc < 2 else 0)

        def prob_banks_before(b, last):
            return b * 13 + (10 if last else 14)

        def sample_steps(eng, step):
            step(None, 0, 0, True)
            with eng.Fori(0, NB // 2 - 1) as i:
                step(i * 2, i * 2 + 1, 1, True)
                step(i * 2 + 1, i * 2 + 2, 0, True)
            step(NB - 2, NB - 1, 1, False)
            step(NB - 1, None, 0, False)

        @block.sync
        def _(sp):
            row_src = [
                (rows[0:16, 0, :], A["norm1_g"][0].rearrange("(t p) -> t p", p=P)),
                (rows[16:32, 0, :], A["norm2_g"][0].rearrange("(t p) -> t p", p=P)),
                (rows[32:48, 0, :], A["normf_g"].rearrange("(t p) -> t p", p=P)),
                (rows[48:64, 0, :], A["conv_b"][0].rearrange("(t p) -> t p", p=P)),
                (rows[64:112, 0, :], A["conv_w"][0].rearrange("j (t p) -> (j t) p", p=P)),
                (rows[0:96, 1, :], A["b_ada"][0].rearrange("(t p) -> t p", p=P)),
                (rows[0:16, 2, :], A["c_prompt"].rearrange("b (t p) -> (b t) p", p=P)),
                (rows[:, 3, :], A["c_sample"].rearrange("b (t p) -> (b t) p", p=P)),
                (rows[:, 4, :], A["state_conv"][0, 0:4].rearrange("b j (t p) -> (b j t) p", p=P)),
                (rows[:, 5, :], A["state_conv"][0, 4:8].rearrange("b j (t p) -> (b j t) p", p=P)),
                (rows[0:32, 6, :], A["pe_cmp_k"][0]),
                (rows[0:32, 7, :], A["pe_cmp_v"][0]),
            ]
            sp.dma_start(page_ids[:, :], A["page_table"].rearrange("(a b) n -> a (b n)", a=1)).then_inc(s_ids, 16)
            for dst, src in row_src:
                sp.dma_start(dst, src).then_inc(s_rows, 16)
            sp.dma_start(w1[:, 0], A["w_cmp_k1"][0].rearrange("(r d) f -> d r f", d=P)).then_inc(s_w1, 16)
            sp.dma_start(w1[:, 1], A["w_cmp_v1"][0].rearrange("(r d) f -> d r f", d=P)).then_inc(s_w1, 16)
            sp.dma_start(w2[:, 0, :], A["w_cmp_k2"][0]).then_inc(s_w1, 16)
            sp.dma_start(w2[:, 1, :], A["w_cmp_v2"][0]).then_inc(s_w1, 16)
            sp.dma_start(x_rows[:, 0:2, :], A["x_prompt"][0].rearrange("(t p) n -> p t n", p=P)).then_inc(s_xrows, 16)
            sp.dma_start(x_rows[0:NSM, 2, :], A["x_sample"].rearrange("b s n -> (b s) n")).then_inc(s_xrows, 16)
            def load_pages(b):
                return [sp.value_load(page_ids[0:1, ds(b * NPAGE + pg, 1)], min_val=0, max_val=A["cache_nsa_kv"].shape[1] - 1)
                        for pg in range(NPAGE)]

            def unit_pages(b, u, page):
                kind, pair = u % 4 // 2, u % 2
                sp.wait_ge(s_kt_bank, b * 32 + 8 * u - 8 + 2 * CREDIT)
                for pg in range(NPAGE):
                    sp.dma_start(pages[:, pair, pg, :],
                                 cache[ds(page[pg], 1), :, kind, 256 * pair:256 * pair + 256].rearrange("a p n -> p (a n)")).then_inc(s_page[pair], 16)

            def ada_panel(b, p):
                sp.wait_ge(s_ada_pe, b * 6 + p - 1 + CREDIT)
                sp.dma_start(ada_raw[:, p % 2, :, :], w_ada[:, :, ds(b * 1536 + 256 * p, 256)]).then_inc(s_ada[p % 2], 16)

            def compress_loads(b, last):
                page = load_pages(b)
                for u in range(4):
                    if u == 2 and not last:
                        page = load_pages(b + 1)
                    if u < 2 or not last:
                        unit_pages(b, u + 2, page)
                    for p in ((2 * u + 2, 2 * u + 3) if u < (2 if last else 3) else ()):
                        ada_panel(b, p)

            sp.wait_ge(s_ids, 16)
            first = load_pages(0)
            unit_pages(0, 0, first)
            unit_pages(0, 1, first)
            sp.wait_ge(s_x0, 16)
            sp.dma_start(x_d, mx[:, :, :]).then_inc(s_xsp, 16)
            ada_panel(0, 0)
            ada_panel(0, 1)
            with sp.Fori(0, NB - 1) as b:
                compress_loads(b, False)
            compress_loads(NB - 1, True)
            sp.wait_ge(s_kt_bank, 32 * NB + 2 * CREDIT)
            sp.wait_ge(s_ada_pe, 6 * NB + CREDIT)
            sp.dma_start(raw[:, 0, :, :], w_in[:, :, COL_U:COL_U + 256]).then_inc(s_raw[0], 16)
            sp.dma_start(x0_a[:, :, :], x_d[:, 0:12, :]).then_inc(s_xld, 16)
            sp.dma_start(x0_b[:, :, :], x_d[:, 12:16, :]).then_inc(s_xld, 16)

            def panel(t, src):
                slot = (t // 2) % 2 if isinstance(t, int) else t[1] // 2 % 2
                sp.wait_ge(s_lo, (2 * t if isinstance(t, int) else 2 * t[0] + 2 * t[1]) - 4 + CREDIT)
                sp.dma_start(raw[:, slot, :, :], src).then_inc(s_raw[slot], 16)

            def dense(t0, n, src):
                with sp.Fori(0, n // 4) as i:
                    for j in range(2):
                        panel((i * 4 + t0, 2 * j), src(i * 512 + 256 * j))

            def conv_panels(i):
                for half in range(2):
                    for k, col in enumerate((COL_U, COL_C, COL_B)):
                        if isinstance(i, int) and half + k == 0:
                            continue
                        if isinstance(i, int) and half == 0 and k == 1:
                            sp.wait_ge(s_h, 4)
                        panel((i * 12 + T_CONV, 6 * half + 2 * k), w_in[:, :, ds(i * 512 + col + 256 * half, 256)])

            conv_panels(0)
            with sp.Fori(1, 4) as i:
                conv_panels(i)
            dense(T_MC, 16, lambda c: w_in[:, :, ds(c + COL_MC, 256)])
            dense(T_WC, 16, lambda c: w_conv[:, :, ds(c, 256)])
            dense(T_MA, 16, lambda c: w_in[:, :, ds(c + COL_MA, 256)])
            sp.wait_ge(s_h, 4)
            sp.dma_start(gw[:, :, :], w_in[:, :, COL_G:COL_G + P]).then_inc(s_gld, 16)
            dense(T_Q, 16, lambda c: w_in[:, :, ds(c + COL_Q, 256)])
            dense(T_KV, 24, lambda c: w_in[:, :, ds(c + COL_KV, 256)])

            sp.wait_ge(s_lo, 2 * T_WA + CREDIT)
            sp.dma_start(w1p[:, 0], A["w_cmp_k1"][0].rearrange("(r d) f -> d r f", d=P)).then_inc(s_w1, 16)
            sp.dma_start(w1p[:, 1], A["w_cmp_v1"][0].rearrange("(r d) f -> d r f", d=P)).then_inc(s_w1, 16)
            sp.wait_ge(s_ev, T_WA + CREDIT)
            sp.dma_start(w2p[:, 0, :], A["w_cmp_k2"][0]).then_inc(s_w1, 16)
            sp.dma_start(w2p[:, 1, :], A["w_cmp_v2"][0]).then_inc(s_w1, 16)

            def keys_load(b, c):
                for pg in range(4):
                    page = sp.value_load(page_ids[0:1, ds(b * NPAGE + 4 * c + pg, 1)], min_val=0, max_val=A["cache_nsa_kv"].shape[1] - 1)
                    if pg == 0:
                        sp.wait_ge(s_ktr, b * 20 + (-8, -4, 4, 8)[c] + 2 * CREDIT)
                    sp.dma_start(krow[:, c % 2, pg, :],
                                 cache[ds(page, 1), :, 2, :].rearrange("a p n -> p (a n)")).then_inc(s_kd[c % 2], 16)

            keys_load(0, 0)
            keys_load(0, 1)
            with sp.Fori(0, NKV) as h:
                for tt in range(3):
                    sp.wait_ge(s_rev, h * 6 + 2 * tt + 2 + CREDIT)
                    n = P if tt < 2 else NSM
                    kvo = A["out_kv_prompt"][0, 0, P * tt:P * tt + P] if tt < 2 else A["out_kv_sample"][0].rearrange("b s k h d -> (b s) k h d")
                    sp.dma_start(kvo[:, :, ds(h, 1), :].rearrange("t k a d -> t k (a d)"), rowsb[0:n, tt, 0:4, :]).then_inc(s_rowdma, 16)
                    if tt < 2:
                        wo = A["out_win_prompt"][0, 0, P * tt:P * tt + P]
                        sp.dma_start(wo[:, :, ds(h, 1), :].rearrange("t k a d -> t k (a d)"), rowsb[0:n, tt, 4:6, :]).then_inc(s_rowdma, 16)
                    else:
                        for b in range(NB):
                            wo = A["out_win_sample"][0, b, WIN - NSTEP:WIN]
                            sp.dma_start(wo[:, :, ds(h, 1), :].rearrange("t k a d -> t k (a d)"),
                                         rowsb[NSTEP * b:NSTEP * b + NSTEP, tt, 4:6, :]).then_inc(s_rowdma, 16)
                sp.wait_ge(s_rowdma, h * (16 * (5 + NB)) + 16 * (5 + NB))
                sp.sem_inc(s_rowfree, 1)
            sp.wait_ge(s_sel, 1)

            def window_and_keys(b, more):
                sp.wait_ge(s_ktr, b * 20 + 2 * CREDIT)
                sp.dma_start(krow[:, 2, :, :], win[ds(b, 1), :, :, 0, :].rearrange("a p c n -> p (a c) n")).then_inc(s_kd[2], 16)
                keys_load(b, 2)
                keys_load(b, 3)
                if more:
                    keys_load(b + 1, 0)
                    keys_load(b + 1, 1)

            with sp.Fori(0, NB - 1) as b:
                window_and_keys(b, True)
            window_and_keys(NB - 1, False)
            sp.wait_ge(s_spv, 5 * (NB - 1) + 3 + 2 * CREDIT)
            sp.dma_start(raw[:, 0, :, :], w_attn[:, :, 0:256]).then_inc(s_raw[0], 16)
            sp.wait_ge(s_oev, 32 + CREDIT)
            sp.wait_ge(s_so, NB + CREDIT)
            panel((T_WA, 2), w_attn[:, :, 256:512])
            with sp.Fori(1, 4) as i:
                for j in range(2):
                    panel((i * 4 + T_WA, 2 * j), w_attn[:, :, ds(i * 512 + 256 * j, 256)])
            dense(T_WO, 16, lambda c: w_out[:, :, ds(c, 256)])
            with sp.Fori(0, 4) as f:
                with sp.Fori(0, 4) as i:
                    for j in range(2):
                        panel((f * 32 + i * 4 + T_MLP, 2 * j), w_mlp1[:, :, ds(f * D + i * 512 + 256 * j, 256)])
                with sp.Fori(0, 4) as i:
                    for j in range(2):
                        panel((f * 32 + i * 4 + T_MLP + 16, 2 * j),
                              w_mlp2[ds(f, 1), :, :, ds(i * 512 + 256 * j, 256)].rearrange("a p t n -> p (a t) n"))
            for tt in range(3):
                for done in s_fev:
                    sp.wait_ge(done, 2 * (tt + 1))
                if tt < 2:
                    sp.dma_start(A["out_y_prompt"][0, P * tt:P * tt + P, :], y_rows[:, tt % 2, :]).then_inc(s_out, 16)
                else:
                    sp.dma_start(A["out_y_sample"].rearrange("b s n -> (b s) n"), y_rows[0:NSM, 0, :]).then_inc(s_out, 16)
            sp.wait_ge(s_out, 16 * 3)
            sp.wait_ge(s_rowdma, 16 * NKV * (5 + NB))
            sp.wait_ge(s_win, 16 * (NB + 2))

        @block.gpsimd
        def _(pool):
            chain = Steps(pool, s_pool)
            chain.did(pool.memset(ident[:, :], 0.0))
            pool.memset(ones[:, :], 1.0).then_inc(s_const, 1)
            chain.wait()
            pool.affine_select(out=ident[:, :], in_=ident[:, :], compare_op=ALU.not_equal, fill=1.0, base=0,
                               pattern=[[-1, P]], channel_multiplier=1).then_inc(s_const, 1)
            with pool.Fori(0, NB) as b:
                for kind in range(2):
                    for pair in range(2):
                        pool.wait_ge(s_cmp_ev, b * 4 + 2 * kind + pair + 1 + CREDIT)
                        pool.sem_inc(s_pass[2], 1)
                        if kind == 0:
                            pool.dma_start(kc_d[ds(b, 1), :, 2 * pair:2 * pair + 2, :].rearrange("a p h c -> p (a h) c"),
                                           kc_out[:, :, :]).then_inc(s_cmp_st[0], 16)
                        else:
                            pool.dma_start(vc_d[ds(b, 1), :, 2 * pair:2 * pair + 2, :].rearrange("a p h c -> p (a h) c"),
                                           vc_out[:, :, :]).then_inc(s_cmp_st[1], 16)
                        pool.wait_ge(s_cmp_st[kind], b * 32 + 16 * pair + 16)
                        pool.sem_inc(s_cmp_free[kind], 1)
            for b in range(NB):
                pool.wait_ge(s_ev, 8 + 6 * b + CREDIT)
                pool.dma_start(A["out_win_sample"][0, b, 0:WIN - NSTEP].rearrange("t k h d -> t (k h d)"),
                               A["state_win_kv"][0, b, NSTEP:WIN].rearrange("t k h d -> t (k h d)")).then_inc(s_win, 16)
            pool.wait_ge(s_gate, 5)
            pool.dma_start(g_d, gTs[:, :, :]).then_inc(s_gdma, 16)
            pool.wait_ge(s_gdma, 16)
            pool.dma_start(gate_s[:, :, :], g_d.rearrange("(r h) s b -> (h s) r b", r=3)).then_inc(s_gdma, 16)
            pool.wait_ge(s_ev, T_WA + CREDIT)
            m = Steps(pool, s_pool, chain.value())
            m.did(pool.memset(mask_p[:, :, :], 0.0))
            m.did(pool.memset(mask_c[:, :, :], 0.0))
            m.did(pool.memset(vis[:, :], 1.0))
            m.wait()
            for qt in range(2):
                m.did(pool.affine_select(out=mask_p[:, qt, :], in_=mask_p[:, qt, :], compare_op=ALU.is_ge, fill=NEG,
                                         base=P * qt, pattern=[[-1, NPR]], channel_multiplier=1))
                m.did(pool.affine_select(out=mask_c[:, qt, :], in_=mask_c[:, qt, :], compare_op=ALU.is_ge, fill=NEG,
                                         base=P * qt - CLEN + 1, pattern=[[-CSTR, NC_P]], channel_multiplier=1))
                m.did(pool.affine_select(out=vis[:, qt:qt + 1], in_=vis[:, qt:qt + 1], compare_op=ALU.is_ge, fill=0.0,
                                         base=P * qt - CLEN + 1, pattern=[[0, 1]], channel_multiplier=1))
            m.did(pool.iota(coli[:, :], pattern=[[1, WIN + NSTEP]], base=0, channel_multiplier=0))
            m.did(pool.iota(rowi[:, 0:1], pattern=[[0, 1]], base=0, channel_multiplier=1))
            m.did(pool.memset(selw[:, :], 1.0))
            m.did(pool.memset(sc1[:, :], 1.0))
            m.wait()
            for off, tile in ((0, selw), (1, sc1)):
                m.did(pool.affine_select(out=tile[:, :], in_=tile[:, :], compare_op=ALU.is_ge, fill=0.0, base=off,
                                         pattern=[[-4, NSB]], channel_multiplier=1))
                m.wait()
                m.did(pool.affine_select(out=tile[:, :], in_=tile[:, :], compare_op=ALU.is_ge, fill=0.0, base=3 - off,
                                         pattern=[[4, NSB]], channel_multiplier=-1))
                m.wait()
            assert m.value() == POOL_STEPS, m.value()
            pool.wait_ge(s_pe, 2)
            pool.wait_ge(s_ids, 16)
            for c in range(2):
                for pg in range(4):
                    page = pool.value_load(page_ids[0:1, 4 * c + pg:4 * c + pg + 1], min_val=0, max_val=A["cache_nsa_kv"].shape[1] - 1)
                    pool.dma_start(vrow[c][:, pg, :],
                                   cache[ds(page, 1), :, 3, :].rearrange("a p n -> p (a n)")).then_inc(s_vd[c], 16)
            pool.wait_ge(s_oev, 32 + CREDIT)
            pool.wait_ge(s_ids, 16)
            pool.wait_ge(s_rowdma, 16 * NKV * (5 + NB))
            pool.wait_ge(s_cmp_st[0], 16 * 2 * NB)
            pool.wait_ge(s_cmp_st[1], 16 * 2 * NB)
            pool.wait_ge(s_kall, 1)

            def compressed(b, par):
                pool.dma_start(kc_s[:, par], kc_d[ds(b, 1)].rearrange("a p h c -> p (a h) c")).then_inc(s_cd[par], 16)
                pool.dma_start(vc_s[:, par], vc_d[ds(b, 1)].rearrange("a p h c -> p (a h) c")).then_inc(s_cd[par], 16)

            def values(b, par, more, chunks=range(4)):
                pool.wait_ge(s_spv, b * 5 - 4 + 2 * CREDIT)
                pool.sem_inc(s_pass[2], 1)
                pool.dma_start(vrow[4][:, :, :], win[ds(b, 1), :, :, 1, :].rearrange("a p c n -> p (a c) n")).then_inc(s_vd[4], 16)
                for c in range(4):
                    if c == 0 and c not in chunks:
                        compressed(b + 1, 1 - par)
                    for pg in range(4 if c in chunks else 0):
                        page = pool.value_load(page_ids[0:1, ds(b * NPAGE + 4 * c + pg, 1)], min_val=0, max_val=A["cache_nsa_kv"].shape[1] - 1)
                        if pg == 0:
                            pool.wait_ge(s_spv, b * 5 + c - 3 + 2 * CREDIT)
                            pool.sem_inc(s_pass[2], 1)
                            if c == 0 and more:
                                compressed(b + 1, 1 - par)
                        pool.dma_start(vrow[c][:, pg, :],
                                       cache[ds(page, 1), :, 3, :].rearrange("a p n -> p (a n)")).then_inc(s_vd[c], 16)

            compressed(0, 0)
            values(0, 0, True, chunks=(2, 3))
            values(1, 1, True)
            with pool.Fori(1, NB // 2 - 1) as i:
                for par in range(2):
                    values(i * 2 + par, par, True)
            values(NB - 2, 0, True)
            values(NB - 1, 1, False)
            pool.wait_ge(s_m, 16)
            pool.dma_start(x1[:, :, :], x_d).then_inc(s_xld1, 16)
            pool.wait_ge(s_fin, 4)
            pool.dma_start(A["out_conv_prompt"][0, 0].rearrange("j (t p) -> j t p", p=P), cs_rows[0:2]).then_inc(s_win, 16)
            pool.dma_start(A["out_conv_sample"][0].rearrange("b j (t p) -> (b j) t p", p=P), cs_rows[2:18]).then_inc(s_win, 16)

        @block.scalar
        def _(act):
            fence = lambda: act.wait_ge(s_const, 1)
            act.sem_inc(s_gelu, CREDIT)
            act.sem_inc(s_cmp_o, CREDIT)
            act.sem_inc(s_sqt, CREDIT)
            act.sem_inc(s_rowfree, CREDIT)
            act.sem_inc(s_rev, CREDIT)
            act.sem_inc(s_ptev, CREDIT)
            act.sem_inc(s_ktev[0], CREDIT)
            act.wait_ge(s_w1, 64)
            for kind in range(2):
                act.activation(w1_hi[:, kind], w1[:, kind], ACT.Copy).then_inc(s_w1_hi, 1)
            for k in range(KT):
                act.wait_ge(s_tr, 3 + k)
                act.activation(mx[:, k, :], bank[2 + k % 4][:, 0:NT], ACT.Copy).then_inc(s_x0, 1)
                if k >= 4:
                    act.wait_ge(s_sqp0, k - 3)
                act.activation(sq_start[:, k % 4, :], bank[2 + k % 4][:, 0:NT], ACT.Square).then_inc(s_sq, 1)
            act.wait_ge(s_nsum, 2)
            act.activation(rbc[:, :], rbc[:, :], ACT.Sqrt).then_inc(s_nsum, 1)
            act.wait_ge(s_prm, 11)
            act.activation(cs[:, :, 0:NSEQ], cT[:, :, :], ACT.Silu).then_inc(s_silu, 1)
            act.wait_ge(s_w1_lo, 2)
            act.wait_ge(s_pe_b, 4)
            act.activation(keyT_hi[:, :, 2 * PAST:KEYS], ident[:, 0:2 * CSTR].rearrange("p (a c) -> p a c", a=2), ACT.Copy).then_inc(s_w1_hi, 1)

            def keys_hi(b, u, f):
                act.wait_ge(s_kt_bank, b * 32 + 8 * u + f + 1 + 2 * CREDIT)
                act.wait_ge(s_cmp_h, b * 4 + u - 1 + CREDIT)
                act.activation(keyT_hi[:, u % 2, 512 * f:512 * f + 512], bank[f % 4][:, :], ACT.Copy).then_inc(s_kt_hi, 1)

            def compress_act(b, last):
                for u in range(4):
                    kind, pair = u // 2, u % 2

                    def ada_row_out(p):
                        act.wait_ge(s_ada_pe, b * 6 + p + 1 + CREDIT)
                        act.activation(ada_row[:, :], bank[7][:, 0:256], ACT.Copy).then_inc(s_ada_row, 1)

                    for f in range(8):
                        if f in (0, 4) and u < 3:
                            ada_row_out(2 * u + f // 4)
                        if f == 5:
                            act.wait_ge(s_cmp_h, b * 4 + u + 1 + CREDIT)
                            act.wait_ge(s_cmp_o, b * 4 + u + CREDIT)
                            act.activation(gelu[:, :].rearrange("p (h c) -> p h c", h=2),
                                           bank[4 + pair][:, 0:2 * P].rearrange("p (h c) -> p h c", h=2)[:, :, 0:NC_S], ACT.Gelu_apprx_tanh,
                                           bias=pe_col[:, kind:kind + 1]).then_inc(s_gelu, 1)
                        if not (last and u == 3):
                            keys_hi(b, u + 1, f)

            for f in range(8):
                keys_hi(0, 0, f)
            act.wait_ge(s_xsp, 16)
            with act.Fori(0, NB - 1) as b:
                compress_act(b, False)
            compress_act(NB - 1, True)

            def root(n):
                act.wait_ge(s_nsum, 3 * n + 2)
                act.activation(rbc[:, :], rbc[:, :], ACT.Sqrt).then_inc(s_nsum, 1)

            def modulate_act(shift, n):
                for g in range(4):
                    act.wait_ge(s_zt, 4 * n + g + 1)
                    for k in range(4 * g, 4 * g + 4):
                        act.activation(act_hi[:, k, 0:NPR], sq[:, k, 0:NPR], ACT.Identity, bias=shift[:, k, 0:1])
                    act.activation(act_hi[:, 4 * g:4 * g + 4, NPR:NT], sq[:, 4 * g:4 * g + 4, NPR:NT], ACT.Copy).then_inc(s_z, 1)


            def hi(i, per, t, ch):
                act.wait_ge(s_raw[(t // 2) % 2], i * (4 * per) + 16 * (t // 4 + 1))
                act.wait_ge(s_chunk, i * (2 * per) + 2 * t + ch - 3 + CREDIT)
                act.activation(w_hi[:, (2 * t + ch) % 4], raw[:, (t // 2) % 2, CH * ch:CH * ch + CH, P * (t % 2):P * (t % 2) + P],
                               ACT.Copy).then_inc(s_hi, 1)

            def dense_act(t0, n, evac, per=4, last=False, outer=None):
                def body(i, stop):
                    for j in range(per):
                        t = t0 + j
                        ahead = not (stop and j >= per - 2)
                        step = i if outer is None else outer * 8 + i
                        if ahead:
                            hi(step, 4 if outer is not None else per, t + 2, 0)
                        evac(i, j)
                        if ahead:
                            hi(step, 4 if outer is not None else per, t + 2, 1)
                times = n // per
                with act.Fori(0, times - 1 if last else times) as i:
                    body(i, False)
                if last:
                    body(times - 1, True)

            def tile_done(i, t, per=4):
                act.wait_ge(s_chunk, i * (2 * per) + 2 * t + 2 + CREDIT)

            act.wait_ge(s_ada_pe, 6 * NB + CREDIT)
            for c in range(2):
                hi(0, 4, c // 2, c % 2)
            act.wait_ge(s_cmp_h, 4 * NB + CREDIT)
            modulate_act(ada[:, 0:KT, :], 0)
            act.wait_ge(s_h, 4)
            for c in range(2, 4):
                hi(0, 4, c // 2, c % 2)

            def ev_conv(i, j):
                if j % 6 >= 4:
                    m = 2 * (j // 6) + j % 2
                    act.wait_ge(s_ev, i * 12 + T_CONV + j + 1 + CREDIT)
                    fence()
                    act.activation(z_hi[:, ds(i * 4 + m, 1), :], z_sb[:, j % 2, :].unsqueeze(1), ACT.Copy).then_inc(s_z, 1)

            dense_act(T_CONV, 48, ev_conv, per=12)
            act.wait_ge(s_cmp_st[0], 16 * 2 * NB)
            act.wait_ge(s_cmp_st[1], 16 * 2 * NB)

            def ev_to(dst, t0, func):
                def ev(i, j):
                    tile_done(i, t0 + j)
                    fence()
                    act.activation(dst[:, ds(i * 4 + j, 1), :], bank[j % 4][:, 0:NT].unsqueeze(1), func).then_inc(s_ev, 1)
                return ev

            act.wait_ge(s_zl, 16)
            dense_act(T_MC, 16, ev_to(mx, T_MC, ACT.Sigmoid))
            dense_act(T_WC, 16, lambda i, j: None)
            dense_act(T_MA, 16, ev_to(ga, T_MA, ACT.Sigmoid))
            act.wait_ge(s_gld, 16)
            act.wait_ge(s_ev, T_MA + CREDIT)
            act.activation(gw_hi[:, :, :], gw[:, :, :], ACT.Copy).then_inc(s_gate, 1)
            act.wait_ge(s_gate, 3)
            act.activation(gT[:, :], bank[7][0:48, 0:NT], ACT.Sigmoid).then_inc(s_gate, 1)
            act.wait_ge(s_gate, 4)
            dense_act(T_Q, 16, ev_to(qo, T_Q, ACT.Copy))
            act.wait_ge(s_gate, 7)
            act.wait_ge(s_gdma, 32)
            dense_act(T_KV, 24, ev_to(kv, T_KV, ACT.Copy), last=True)

            for kind in range(2):
                act.wait_ge(s_pe, 1 + kind)
                act.activation(gelu_p[:, kind], bank[6 + kind][:, 0:NKV * NC_P].rearrange("p (h c) -> p h c", h=NKV),
                               ACT.Gelu_apprx_tanh, bias=pe_col[:, kind:kind + 1]).then_inc(s_gelu, 1)
            with act.Fori(0, NKV) as h:
                act.wait_ge(s_scev, h * 18 + 2 + CREDIT)
                for u in range(8):
                    act.activation(S_c[:, u, :], S_c[:, u, :], ACT.Exp, scale=SCALE,
                                   bias=nmp[:, u, 0:1], accum_out=den[:, u, 0:1]).then_inc(s_exp, 1)
                for u in range(8):
                    nk = P * (u % 2 + 1)
                    act.wait_ge(s_scev, h * 18 + 2 * u + 4 + CREDIT)
                    for br in range(2):
                        act.activation(S_p[:, u, br, 0:nk], S_p[:, u, br, 0:nk], ACT.Exp, scale=SCALE,
                                       bias=nmp[:, u, 1 + br:2 + br], accum_out=den[:, u, 1 + br:2 + br]).then_inc(s_exp, 1)
                    n = u - 2
                    if n >= 0:
                        tt, kg = n // 2, n % 2
                        act.wait_ge(s_rtr, h * 6 + n + 1)
                        act.wait_ge(s_rowfree, h + CREDIT)
                        act.wait_ge(s_pv, h * 8 + CREDIT)
                        rows_n = P if tt < 2 else NSM
                        k0, kn = (0, 4) if kg == 0 else (4, 2)
                        act.activation(rowsb[0:rows_n, tt, k0:k0 + kn, :],
                                       bank[n % 2][0:rows_n, 0:kn * P].rearrange("p (k d) -> p k d", d=P), ACT.Copy).then_inc(s_rev, 1)
                for f in range(10):
                    act.wait_ge(s_pt, h * 10 + f + 1)
                    act.wait_ge(s_pv, h * 8 + (f - 3 if f >= 2 else 0) + CREDIT)
                    if f < 2:
                        act.activation(PTc[:, 4 * f:4 * f + 4, :], bank[6][0:NC_P, :].rearrange("p (u q) -> p u q", q=P),
                                       ACT.Copy).then_inc(s_ptev, 1)
                    else:
                        u = f - 2
                        tiles = (0, 2) if u % 2 == 0 else (0, 1, 2, 3)
                        if u % 2 == 0:
                            act.activation(PT[:, u % 2, 0:4:2, :], bank[f % 2][:, :].rearrange("p (k q) -> p k q", q=P)[:, 0:4:2, :],
                                           ACT.Copy).then_inc(s_ptev, 1)
                        else:
                            act.activation(PT[:, u % 2, :, :], bank[f % 2][:, :].rearrange("p (k q) -> p k q", q=P),
                                           ACT.Copy).then_inc(s_ptev, 1)

            def sample_act(b, n, par, more):
                def keys_copy(pc):
                    for hd in range(0, NKV, 2):
                        act.wait_ge(s_ktr, n * 20 + 4 * pc + hd + 1 + 2 * CREDIT)
                        act.wait_ge(s_ssc, n * 6 + (pc if pc >= 2 else 0) + CREDIT)
                        act.activation(kT[:, pc % 2, hd, :], bank[0][:, :], ACT.Copy).then_inc(s_ktev[0], 1)

                def exps(br):
                    act.wait_ge(s_sm, b * 5 + 1 + br)
                    w, st = (S_s, W_s)[br], st2[1 - par]
                    act.activation(w[:, :], w[:, :], ACT.Exp, scale=SCALE, bias=st[:, 4 + br:5 + br],
                                   accum_out=st[:, 7 + br:8 + br]).then_inc(s_sexp, 1)

                if n is not None:
                    keys_copy(0)
                if b is not None:
                    exps(0)
                if n is not None:
                    keys_copy(1)
                if b is not None:
                    exps(1)
                if n is not None:
                    st = st2[par]
                    act.wait_ge(s_sel, n * 12 + 3)
                    act.activation(C_s[:, 0:NC_S], bank[4][:, 0:NC_S], ACT.Exp, scale=SCALE, bias=st[:, 3:4],
                                   accum_out=st[:, 6:7]).then_inc(s_cexp, 1)
                    act.wait_ge(s_selp, n * 3 + 1)
                    act.activation(PTcs[par][:, :], bank[7][0:NC_S, 0:P], ACT.Copy).then_inc(s_cexp, 1)
                if b is not None:
                    for f in range(0, 6, 2):
                        act.wait_ge(s_ptr, b * 6 + f + 1)
                        act.wait_ge(s_spv, b * 5 + 2 * CREDIT)
                        act.activation(PTs[:, 4 * f:4 * f + 4, :], bank[0][:, :].rearrange("p (k q) -> p k q", q=P),
                                       ACT.Copy).then_inc(s_ktev[0], 1)
                if n is not None:
                    for pc in range(2, 5):
                        keys_copy(pc)

            sample_steps(act, sample_act)

            act.wait_ge(s_spv, 5 * NB + 2 * CREDIT)
            act.wait_ge(s_so, NB + CREDIT)
            act.wait_ge(s_oev, 32 + CREDIT)
            for g in range(4):
                if g == 3:
                    for c in range(2):
                        hi(0, 4, T_WA, c)
                act.activation(act_hi[:, 4 * g:4 * g + 4, :], qo[:, 4 * g:4 * g + 4, :], ACT.Copy).then_inc(s_z, 1)
            for c in range(2):
                hi(0, 4, T_WA + 1, c)

            def ev_merged(i, j):
                kt = ds(i * 4 + j, 1)
                act.wait_ge(s_m, i * 4 + j + 1)
                act.wait_ge(s_h, 8)
                fence()
                act.activation(mx_hi[:, kt, :], mx[:, kt, :], ACT.Copy).then_inc(s_z, 1)

            dense_act(T_WA, 16, ev_merged)

            def ev_squares(norm, done):
                def ev(i, j):
                    act.wait_ge(s_xadd, i * 4 + j + 1 + done)
                    act.wait_ge(s_sqp, i * 4 + j - 2 + 17 * norm + CREDIT)
                    fence()
                    act.activation(sqt[:, j, :].unsqueeze(1), x1[:, ds(i * 4 + j, 1), :], ACT.Square).then_inc(s_sqt, 1)
                return ev

            dense_act(T_WO, 16, ev_squares(0, 0))
            root(1)
            modulate_act(ada[:, 3 * KT:4 * KT, :], 1)

            def mlp(f, last):
                def ev_hidden(i, j):
                    n = f * 32 + i * 4
                    act.wait_ge(s_chunk, n * 2 + 2 * (T_MLP + j) + 2 + CREDIT)
                    act.wait_ge(s_hid, f * 16 + i * 4 + j - 3 + CREDIT)
                    act.activation(rl[:, j, :], bank[j][:, 0:NT], ACT.Relu).then_inc(s_ev, 1)
                    act.wait_ge(s_ev, n + T_MLP + j + 1 + CREDIT)
                    fence()
                    act.activation(hid_hi[:, ds(i * 4 + j, 1), :], rl[:, j, :].unsqueeze(1), ACT.Square).then_inc(s_hidh, 1)
                dense_act(T_MLP, 16, ev_hidden, outer=f)
                dense_act(T_MLP + 16, 16, ev_squares(1, 64) if last else lambda i, j: None, outer=f, last=last)

            with act.Fori(0, 3) as f:
                mlp(f, False)
            mlp(3, True)
            root(2)
            for g in range(4):
                act.wait_ge(s_ftr, g + 1)
                act.activation(cs_rows[:, 4 * g:4 * g + 4, :], bank[g % 4][0:2 * NSEQ, :].rearrange("p (k q) -> p k q", q=P),
                               ACT.Copy).then_inc(s_fin, 1)
            for f in range(12):
                tt, g = f // 4, f % 4
                n = P if tt < 2 else NSM
                if f % 2:
                    continue
                act.wait_ge(s_ftr, 4 + f + 1)
                if tt == 2:
                    act.wait_ge(s_out, 32)
                act.activation(y_rows[0:n, tt % 2, 512 * g:512 * g + 512], bank[f % 4][0:n, :], ACT.Copy).then_inc(s_fev[0], 1)

        @block.tensor
        def _(pe):
            mm, tr = nc.tensor.matmul, nc.tensor.transpose
            pe.sem_inc(s_chunk, CREDIT)
            pe.sem_inc(s_kt_bank, 2 * CREDIT)
            pe.sem_inc(s_cmp_h, CREDIT)
            pe.sem_inc(s_ada_pe, CREDIT)
            pe.sem_inc(s_pv, CREDIT)
            pe.sem_inc(s_ktr, 2 * CREDIT)
            pe.sem_inc(s_ssc, CREDIT)
            pe.sem_inc(s_spv, 2 * CREDIT)
            pe.sem_inc(s_sqp, CREDIT)
            pe.wait_ge(s_const, 2)
            pe.wait_ge(s_rows, 16 * 12)
            tr(bank[0][:, 0:112], rows[0:112, 0, :], ident[0:112, 0:112])
            tr(bank[0][:, 128:224], rows[0:96, 1, :], ident[0:96, 0:96])
            tr(bank[0][:, 256:272], rows[0:16, 2, :], ident[0:16, 0:16])
            tr(bank[0][:, 288:320], rows[0:32, 6, :], ident[0:32, 0:32])
            tr(bank[0][:, 320:352], rows[0:32, 7, :], ident[0:32, 0:32]).then_inc(s_tr, 1)
            for k in range(3):
                last = tr(bank[1][:, P * k:P * k + P], rows[:, 3 + k, :], ident[:, :])
            last.then_inc(s_tr, 1)
            pe.wait_ge(s_w1, 64)
            pe.wait_ge(s_prm, 11)
            for kind in range(2):
                for r in range(CLEN):
                    g = r % 4
                    last = mm(bank[6][32 * g:32 * g + 32, P * kind:P * kind + P], peT[:, 32 * kind + r:32 * kind + r + 32], w1[:, kind, r, :],
                              start=(r < 4), stop=(r >= CLEN - 4))
            last.then_inc(s_pe_b, 1)
            pe.wait_ge(s_xrows, 32)

            def start_squares(k):
                pe.wait_ge(s_sq, k + 1)
                mm(bank[7][:, 0:NT], ones[:, :], sq_start[:, k % 4, :], start=(k == 0), stop=(k == KT - 1)).then_inc(s_sqp0, 1)

            for k in range(KT):
                if k >= 4:
                    pe.wait_ge(s_sq, k - 3)
                for tt in range(3):
                    n = P if tt < 2 else NSM
                    last = tr(bank[2 + k % 4][:, P * tt:P * tt + n], x_rows[0:n, tt, P * k:P * k + P], ident[0:n, 0:n])
                last.then_inc(s_tr, 1)
                if k == 2:
                    pe.wait_ge(s_pe_b, 2)
                    for kind in range(2):
                        last = mm(bank[6][:, 256 + kind:257 + kind], pe_rows[:, P * kind:P * kind + P], sel9[:, 0:1], start=True, stop=True)
                    last.then_inc(s_pe_b, 1)
                if k >= 2:
                    start_squares(k - 2)
            start_squares(KT - 2)
            start_squares(KT - 1)
            pe.wait_ge(s_sqp0, KT)
            pe.sem_inc(s_nsum, 1)
            pe.wait_ge(s_nsum, 2)
            pe.wait_ge(s_x0, 16)
            pe.wait_ge(s_silu, 1)
            pe.wait_ge(s_pe_b, 4)

            def keys_bank(b, u, f):
                kind, pair = u // 2, u % 2
                if f == 0:
                    pe.wait_ge(s_page[pair], b * (32 * NPAGE) + 16 * NPAGE * (kind + 1))
                pe.wait_ge(s_kt_ev, b * 32 + 8 * u + f - 3 + CREDIT)
                for pg in range(4):
                    last = tr(bank[f % 4][:, P * pg:P * pg + P], pages[:, pair, 4 * (f % 4) + pg, P * (f // 4):P * (f // 4) + P], ident[:, :])
                last.then_inc(s_kt_bank, 1)

            def compress_pe(b, last_one):

                def ada_prod(p):
                    pe.wait_ge(s_ada[p % 2], b * 48 + 16 * (p // 2) + 16)
                    pe.wait_ge(s_ada_ev, b * 6 + p + CREDIT)
                    for kk in range(4):
                        for g in range(4):
                            last = mm(bank[7][32 * g:32 * g + 32, 0:256], cs[:, 4 * kk + g, :], ada_raw[:, p % 2, 4 * kk + g, :],
                                      start=(kk == 0), stop=(kk == 3))
                    last.then_inc(s_ada_pe, 1)

                def ada_turn(p):
                    pe.wait_ge(s_ada_row, b * 6 + p + 1)
                    for half in range(2):
                        last = mm(bank[7][:, 16 * half:16 * half + NSEQ], ada_row[:, P * half:P * half + P], sel9[:, :], start=True, stop=True)
                    last.then_inc(s_ada_t, 1)

                for u in range(4):
                    kind, pair = u // 2, u % 2
                    if u < 3:
                        ada_prod(2 * u)
                    pe.wait_ge(s_kt_ev, b * 32 + 8 * u + 8 + CREDIT)
                    pe.wait_ge(s_gelu, b * 4 + u - 1 + CREDIT)
                    hout = bank[4 + pair][:, 0:2 * P]
                    for f in range(8):
                        for r in range(6 * f, min(6 * f + 6, CLEN)):
                            k_hi, k_lo = (k[:, pair, r:r + CSTR * (2 * P - 1) + 1:CSTR] for k in (keyT_hi, keyT_lo))
                            mm(hout, w1_hi[:, kind, r, :], k_hi, start=(r == 0), stop=False)
                            mm(hout, w1_lo[:, kind, r, :], k_hi, start=False, stop=False)
                            last = mm(hout, w1_hi[:, kind, r, :], k_lo, start=False, stop=(r == CLEN - 1))
                            if r == CLEN - 1:
                                last.then_inc(s_cmp_h, 1)
                        if not (last_one and u == 3):
                            keys_bank(b, u + 1, f)
                        if u < 3:
                            if f in (1, 5):
                                ada_turn(2 * u + f // 4)
                            elif f == 3:
                                ada_prod(2 * u + 1)
                    pe.wait_ge(s_gelu, b * 4 + u + 1 + CREDIT)
                    pe.wait_ge(s_cmp_ev, b * 4 + u + CREDIT)
                    if kind == 0:
                        last = mm(bank[6][:, 0:2 * NC_S], w2[:, 0, :], gelu[:, :], start=True, stop=True)
                    else:
                        for hh in range(2):
                            last = mm(bank[6][0:NC_S, P * hh:P * hh + P], gelu[:, NC_S * hh:NC_S * hh + NC_S], w2[:, 1, :],
                                      start=True, stop=True)
                    last.then_inc(s_cmp_o, 1)

            for f in range(8):
                keys_bank(0, 0, f)
            pe.wait_ge(s_w1_lo, 3)
            with pe.Fori(0, NB - 1) as b:
                compress_pe(b, False)
            compress_pe(NB - 1, True)

            def dense_pe(t0, n, x_hi, x_lo, per=4, outer=None, groups=None, sem_groups=s_h, after=lambda i, j: None):
                times = n // per
                with pe.Fori(0, times) as i:
                    for j in range(per):
                        t = t0 + j
                        step = i * per if outer is None else outer * 32 + i * 4
                        pe.wait_ge(s_ev, step + t + 1 - 4 + CREDIT)
                        for ch in range(2):
                            pe.wait_ge(s_lo, step * 2 + 2 * t + ch + 1 + CREDIT)
                            if j == 0 and groups:
                                pe.wait_ge(sem_groups, groups[ch])
                            buf = (2 * t + ch) % 4
                            for k in range(CH):
                                kk = CH * ch + k
                                out = bank[t % 4][:, 0:NT]
                                mm(out, w_hi[:, buf, k, :], x_hi[:, kk, :], start=(kk == 0), stop=False)
                                mm(out, w_lo[:, buf, k, :], x_hi[:, kk, :], start=False, stop=False)
                                last = mm(out, w_hi[:, buf, k, :], x_lo[:, kk, :], start=False, stop=(kk == KT - 1))
                            last.then_inc(s_chunk, 1)
                        after(i, j)

            dense_pe(T_CONV, 48, act_hi, act_lo, per=12, groups=(2, 4))
            pe.wait_ge(s_ev, T_MC + CREDIT)
            dense_pe(T_MC, 16, act_hi, act_lo)
            pe.wait_ge(s_ev, T_WC + CREDIT)
            pe.wait_ge(s_zl, 16)
            dense_pe(T_WC, 16, z_hi, z_lo)
            pe.wait_ge(s_ev, T_MA + CREDIT)
            dense_pe(T_MA, 16, act_hi, act_lo)
            pe.wait_ge(s_gate, 2)
            for k in range(KT):
                mm(bank[7][:, 0:NT], gw_hi[:, k, :], act_hi[:, k, :], start=(k == 0), stop=False)
                mm(bank[7][:, 0:NT], gw_lo[:, k, :], act_hi[:, k, :], start=False, stop=False)
                last = mm(bank[7][:, 0:NT], gw_hi[:, k, :], act_lo[:, k, :], start=False, stop=(k == KT - 1))
            last.then_inc(s_gate, 1)
            pe.wait_ge(s_gate, 5)
            for qt in range(2):
                last = tr(bank[6][:, 64 * qt:64 * qt + 48], gT[:, P * qt:P * qt + P], ident[0:48, 0:48])
            last.then_inc(s_gate, 1)
            dense_pe(T_Q, 16, act_hi, act_lo)
            dense_pe(T_KV, 24, act_hi, act_lo)

            pe.wait_ge(s_ev, T_WA + CREDIT)
            pe.wait_ge(s_gate, 7)
            pe.wait_ge(s_w1, 128)
            for kind in range(2):
                hout = bank[6 + kind][:, 0:NKV * NC_P].rearrange("p (h c) -> p h c", h=NKV)
                for r in range(CLEN):
                    last = mm(hout, w1p[:, kind, r, :], kv[:, 4 * kind:4 * kind + 4, r:r + CSTR * (NC_P - 1) + 1:CSTR],
                              start=(r == 0), stop=(r == CLEN - 1))
                last.then_inc(s_pe, 1)
            pe.wait_ge(s_gelu, 4 * NB + 1 + CREDIT)
            mm(bank[4][:, 0:NKV * NC_P], w2p[:, 0, :], gelu_p[:, 0].rearrange("p h c -> p (h c)"), start=True, stop=True).then_inc(s_pe, 1)
            pe.wait_ge(s_gelu, 4 * NB + 2 + CREDIT)
            for h in range(NKV):
                last = mm(bank[5][0:NC_P, P * h:P * h + P], gelu_p[:, 1, h, :], w2p[:, 1, :], start=True, stop=True)
            last.then_inc(s_pe, 1)
            pe.wait_ge(s_cpp, 2)
            with pe.Fori(0, NKV) as h:
                pe.wait_ge(s_bun, h * 3 + 3)

                def rows_turn(n):
                    tt, kg = n // 2, n % 2
                    if n >= 2:
                        pe.wait_ge(s_rev, h * 6 + n - 1 + CREDIT)
                    else:
                        pe.wait_ge(s_ptev, h * 10 + CREDIT)
                    pe.sem_inc(s_pass[1], 1)
                    rows_n = P if tt < 2 else NSM
                    k0, kn = (0, 4) if kg == 0 else (4, 2)
                    for k in range(kn):
                        last = tr(bank[n % 2][0:rows_n, P * k:P * k + P], kv_b[:, k0 + k, P * tt:P * tt + rows_n], ident[:, :])
                    last.then_inc(s_rtr, 1)

                pe.wait_ge(s_oev, h * 8 + CREDIT)
                for u in range(8):
                    g, qt = u // 2, u % 2
                    last = mm(bank[7][:, 16 * u:16 * u + NC_P], q_b[:, g, P * qt:P * qt + P], kc_b[:, :], start=True, stop=True)
                last.then_inc(s_sc, 1)
                for u in range(8):
                    g, qt = u // 2, u % 2
                    nk = P * (qt + 1)
                    if u >= 4:
                        pe.wait_ge(s_scev, h * 18 + 2 * (u - 4) + 3 + CREDIT)
                    mm(bank[2 + u % 4][:, 0:nk], q_b[:, g, P * qt:P * qt + P], kv_b[:, 2, 0:nk], start=True, stop=True)
                    mm(bank[2 + u % 4][:, NPR:NPR + nk], q_b[:, g, P * qt:P * qt + P], kv_b[:, 4, 0:nk],
                       start=True, stop=True).then_inc(s_sc, 1)
                    if u >= 2:
                        rows_turn(u - 2)
                pe.wait_ge(s_rev, h * 6 + 6 + CREDIT)
                for f in range(2):
                    pe.wait_ge(s_exp, h * 24 + 4 * f + 4)
                    if f == 1:
                        pe.wait_ge(s_ptev, h * 10 + 1 + CREDIT)
                    for k in range(4):
                        last = tr(bank[6][0:NC_P, P * k:P * k + P], S_c[:, 4 * f + k, :], ident[:, :])
                    last.then_inc(s_pt, 1)

                def turn(u):
                    pe.wait_ge(s_exp, h * 24 + 2 * u + 10)
                    if u >= 2:
                        pe.wait_ge(s_ptev, h * 10 + u + 1 + CREDIT)
                    for k in ((0, 2) if u % 2 == 0 else (0, 1, 2, 3)):
                        last = tr(bank[u % 2][:, P * k:P * k + P], S_p[:, u, k // 2, P * (k % 2):P * (k % 2) + P], ident[:, :])
                    last.then_inc(s_pt, 1)

                turn(0)
                pe.wait_ge(s_vcb, h * 2 + 2)
                for u in range(8):
                    if u < 7:
                        turn(u + 1)
                    o = bank[2 + u % 4]
                    if u >= 4:
                        pe.wait_ge(s_orow, h * 8 + u - 3)
                    pe.wait_ge(s_ptev, h * 10 + 2 + u + 1 + CREDIT)
                    mm(o[:, 0:P], PTc[:, u, :], vc_b[:, :], start=True, stop=True)
                    for br, kind in ((1, 3), (2, 5)):
                        for t in range(u % 2 + 1):
                            last = mm(o[:, P * br:P * br + P], PT[:, u % 2, 2 * (br - 1) + t, :], rowsb[:, t, kind, :],
                                      start=(t == 0), stop=(t == u % 2))
                    last.then_inc(s_pv, 1)
                    for w in ([u - 1] if u else []) + ([7] if u == 7 else []):
                        pe.wait_ge(s_orow, h * 8 + w + 1)
                        pe.wait_ge(s_oev, h * 8 + w - 1 + CREDIT)
                        tr(bank[7 - w % 2][:, 0:P], o_row[:, w % 2, :], ident[:, :]).then_inc(s_otr, 1)

            pe.wait_ge(s_oev, 32 + CREDIT)
            pe.wait_ge(s_sel, 1)
            def sample_pe(b, n, par, more):

                def keys(pc):
                    slot = pc % 2 if pc < 4 else 2
                    if pc < 4:
                        pe.wait_ge(s_kd[slot], n * 128 + 64 * (pc // 2 + 1))
                    else:
                        pe.wait_ge(s_kd[2], n * 16 + 16)
                    for h in range(NKV):
                        pe.wait_ge(s_ktev[h % 2], banks_before(n, pc) + h // 2 + CREDIT)
                        for k in range(4):
                            last = tr(bank[h % 2][:, P * k:P * k + P], krow[:, slot, k, P * h:P * h + P], ident[:, :])
                        last.then_inc(s_ktr, 1)

                def scores(pc):
                    for eng in range(2):
                        pe.wait_ge(s_ktev[eng], banks_before(n, pc) + 2 + CREDIT)
                    pe.wait_ge(s_sev, n * 5 + (pc - 1 if pc >= 2 else 0) + CREDIT)
                    for h in range(NKV):
                        last = mm(bank[2 + pc % 2][32 * h:32 * h + 32, :], q_s[par][:, 32 * h:32 * h + 32], kT[:, pc % 2, h, :],
                                  start=True, stop=True)
                    last.then_inc(s_ssc, 1)

                if n is not None:
                    pe.wait_ge(s_new, n * 2 + 2)
                    pe.wait_ge(s_cd[par], n * 16 + (32, 16)[par])
                    for keys_of, c0, cn in ([kc_s[:, par, h, :] for h in range(NKV)], 0, NC_S), \
                            ([knew[par][:, h, :] for h in range(NKV)], P, NSTEP), \
                            ([knew[par][:, 8 + h, :] for h in range(NKV)], P + NSTEP, NSTEP):
                        for h in range(NKV):
                            last = mm(bank[4][32 * h:32 * h + 32, c0:c0 + cn], q_s[par][:, 32 * h:32 * h + 32], keys_of[h], start=True, stop=True)
                    last.then_inc(s_ssc, 1)
                    pe.wait_ge(s_so, n - 1 + CREDIT)
                    for br in range(2):
                        for h in range(NKV):
                            last = tr(bank[6 + br][0:NSTEP, P * h:P * h + P], knew[par][:, 8 * br + 4 + h, :], ident[:, :])
                    last.then_inc(s_vnt, 1)
                    keys(0)
                    keys(1)
                    pe.wait_ge(s_cexp, n * 2 + 1)
                    pe.wait_ge(s_vne, n * 2 + 2)
                    tr(bank[7][0:NC_S, 0:P], C_s[:, 0:NC_S], ident[:, :]).then_inc(s_selp, 1)
                    scores(0)
                    pe.wait_ge(s_cexp, n * 2 + 2)
                    mm(bank[7][:, P:P + NSB], PTcs[par][:, :], selw[0:NC_S, :], start=True, stop=True).then_inc(s_selp, 1)
                if b is not None:
                    for f in range(6):
                        pe.wait_ge(s_ktev[f % 2], prob_banks_before(b, n is None) + f // 2 + CREDIT)
                        pe.wait_ge(s_sexp, b * 2 + (1 if f < 4 else 2))
                        for k in range(4 if f < 5 else 0):
                            src = S_s[:, 512 * f + P * k:512 * f + P * k + P] if f < 4 else W_s[:, P * k:P * k + P]
                            last = tr(bank[f % 2][:, P * k:P * k + P], src, ident[:, :])
                        if f == 5:
                            tr(bank[1][0:NSTEP, 0:P], S_s[:, PAST:PAST + NSTEP], ident[:, :])
                            last = tr(bank[1][0:NSTEP, P:2 * P], W_s[:, WIN:WIN + NSTEP], ident[:, :])
                        last.then_inc(s_ptr, 1)
                if n is not None:
                    pe.wait_ge(s_sel, n * 12 + 5)
                    mm(bank[7][:, 192:192 + NSB], grp[:, :], z_s[:, :], start=True, stop=True).then_inc(s_selp, 1)
                if b is not None:
                    bp = 1 - par
                    for eng in range(2):
                        pe.wait_ge(s_ktev[eng], prob_banks_before(b, n is None) + 3 + CREDIT)

                    def weigh(br, probs, values, start, stop):
                        for h in range(NKV):
                            last = mm(bank[5][32 * h:32 * h + 32, P * br:P * br + P], probs[:, 32 * h:32 * h + 32], values[:, P * h:P * h + P],
                                      start=start, stop=stop)
                        return last

                    pe.wait_ge(s_vd[4], b * 16 + 16)
                    for k in range(4):
                        weigh(2, PTs[:, 16 + k, :], vrow[4][:, k, :], k == 0, False)
                    weigh(2, PTn[:, 1, :], vnew[bp][:, 1, :], False, True).then_inc(s_spv, 1)
                    weigh(0, PTcs[bp][:, :], vc_s[:, bp].rearrange("p h d -> p (h d)"), True, True)
                    weigh(1, PTn[:, 0, :], vnew[bp][:, 0, :], True, False)
                    for c in range(4):
                        pe.wait_ge(s_vd[c], b * 64 + 64)
                        for k in range(4):
                            last = weigh(1, PTs[:, 4 * c + k, :], vrow[c][:, k, :], False, c == 3 and k == 3)
                        last.then_inc(s_spv, 1)
                if n is not None:
                    keys(2)
                if b is not None:
                    pe.wait_ge(s_sm, b * 5 + 5)
                    tr(bank[6][:, 0:P], os_row[:, :], ident[:, :]).then_inc(s_sot, 1)
                if n is not None:
                    scores(1)
                    keys(3)
                    scores(2)
                    keys(4)
                    scores(3)
                    scores(4)

            sample_steps(pe, sample_pe)

            dense_pe(T_WA, 16, act_hi, act_lo, groups=(6, 8))

            def square_sums(norm):
                pe.wait_ge(s_zero, norm + 1)
                mm(bank[7][:, 0:NT], ones[:, :], sqt[:, 3, :], start=True, stop=False)

                def after(i, j):
                    pe.wait_ge(s_sqt, i * 4 + j + 16 * norm + CREDIT)
                    mm(bank[7][:, 0:NT], ones[:, :], sqt[:, (j - 1) % 4, :], start=False, stop=False).then_inc(s_sqp, 1)
                return after

            def square_sums_end(norm):
                pe.wait_ge(s_sqt, 16 * norm + 16 + CREDIT)
                mm(bank[7][:, 0:NT], ones[:, :], sqt[:, 3, :], start=False, stop=True).then_inc(s_sqp, 1)
                pe.wait_ge(s_sqp, 17 * norm + 17 + CREDIT)
                pe.sem_inc(s_nsum, 1)

            pe.wait_ge(s_ev, T_WO + CREDIT)
            dense_pe(T_WO, 16, mx_hi, mx_lo, groups=(16, 24), after=square_sums(0))
            square_sums_end(0)

            def mlp(f, last):
                dense_pe(T_MLP, 16, act_hi, act_lo, outer=f, groups=(26, 28))
                pe.wait_ge(s_ev, f * 32 + T_MLP + 16 + CREDIT)
                pe.sem_inc(s_pass[1], 1)
                after = square_sums(1) if last else lambda i, j: None
                dense_pe(T_MLP + 16, 16, hid_hi, hid_lo, outer=f, after=after, sem_groups=s_hid,
                         groups=(f * 16 + 8 + CREDIT, f * 16 + 16 + CREDIT))

            with pe.Fori(0, 3) as f:
                mlp(f, False)
            mlp(3, True)
            square_sums_end(1)
            for g in range(4):
                for k in range(4):
                    last = tr(bank[g][0:2 * NSEQ, P * k:P * k + P], cstate[:, 4 * g + k, :], ident[:, :])
                last.then_inc(s_ftr, 1)
            for f in range(12):
                tt, g = f // 4, f % 4
                n = P if tt < 2 else NSM
                if f < 4:
                    pe.wait_ge(s_fin, f + 1)
                    pe.wait_ge(s_zt, 8 + f + 1)
                else:
                    pe.wait_ge(s_fev[f % 2], (f - 4) // 2 + 1)
                for k in range(4):
                    last = tr(bank[f % 4][0:n, P * k:P * k + P], sq[:, 4 * g + k, P * tt:P * tt + n], ident[:, :])
                last.then_inc(s_ftr, 1)

        @block.vector
        def _(dve):
            for c in (s_kt_ev, s_cmp_free[0], s_cmp_free[1], s_cmp_ev, s_ada_ev, s_lo, s_ev, s_scev, s_oev, s_ktev[1], s_sev, s_so, s_hid):
                dve.sem_inc(c, CREDIT)
            step = Steps(dve, s_dv)
            V = nc.vector

            def seq(ins):
                step.did(ins)
                step.wait()

            dve.wait_ge(s_tr, 2)
            V.tensor_copy(params[:, :], bank[0][:, 0:112]).then_inc(s_prm, 1)
            V.tensor_copy(b_ada[:, :], bank[0][:, 128:224]).then_inc(s_prm, 1)
            V.tensor_copy(cT[:, :, 0], bank[0][:, 256:272]).then_inc(s_prm, 1)
            V.tensor_copy(peT[:, 0:32], bank[0][:, 288:320]).then_inc(s_prm, 1)
            V.tensor_copy(peT[:, 32:64], bank[0][:, 320:352]).then_inc(s_prm, 1)
            V.memset(peT[:, 64:96], 0.0).then_inc(s_prm, 1)
            V.tensor_copy(cT[:, :, 1:NSEQ], bank[1][:, 0:P].rearrange("p (b t) -> p t b", b=NB)).then_inc(s_prm, 1)
            for k in range(2):
                V.tensor_copy(prevT[:, 8 * k:8 * k + 8, :],
                              bank[1][:, P + P * k:2 * P + P * k].rearrange("p (r t) -> p r t", r=8)).then_inc(s_prm, 1)

            V.memset(cs[:, :, :], 0.0).then_inc(s_prm, 1)
            V.tensor_reduce(sel9[:, :], ident[:, :].rearrange("p (g s) -> p s g", g=4)[:, 0:NSEQ, :], AX.X, ALU.add).then_inc(s_prm, 1)
            def rstd(n):
                dve.wait_ge(s_nsum, 3 * n + 1)
                V.tensor_scalar(rbc[:, :], bank[7][:, 0:NT], 1.0 / D, EPS, ALU.mult, ALU.add).then_inc(s_nsum, 1)
                dve.wait_ge(s_nsum, 3 * n + 3)
                seq(V.reciprocal(rbc[:, :], rbc[:, :]))

            dve.wait_ge(s_pe_b, 1)
            V.tensor_copy(pe_rows[:, :], bank[6][:, 0:256]).then_inc(s_pe_b, 1)
            for kind in range(2):
                dve.wait_ge(s_w1_hi, kind + 1)
                V.tensor_tensor(w1_lo[:, kind], w1[:, kind], w1_hi[:, kind].bitcast(F32), ALU.subtract).then_inc(s_w1_lo, 1)
            dve.wait_ge(s_pe_b, 3)
            V.tensor_copy(pe_col[:, :], bank[6][:, 256:258]).then_inc(s_pe_b, 1)
            rstd(0)

            def keys_lo(b, u, f):
                dve.wait_ge(s_kt_hi, b * 32 + 8 * u + f + 1)
                part = (slice(None), u % 2, slice(512 * f, 512 * f + 512))
                V.tensor_tensor(keyT_lo[part], bank[f % 4][:, :], keyT_hi[part].bitcast(F32), ALU.subtract).then_inc(s_kt_ev, 1)

            def compress_dve(b, last):
                for u in range(4):
                    kind, pair = u // 2, u % 2

                    def ada_out(p):
                        dve.wait_ge(s_ada_t, b * 6 + p + 1)
                        V.tensor_tensor(ada[:, ds(b * 12 + 2 * p, 2), :],
                                        bank[7][:, 0:32].rearrange("p (a c) -> p a c", a=2)[:, :, 0:NSEQ],
                                        b_ada[:, ds(b * 12 + 2 * p, 2)].unsqueeze(2).to_broadcast([P, 2, NSEQ]), ALU.add).then_inc(s_ada_ev, 1)

                    for f in range(8):
                        if not (last and u == 3):
                            keys_lo(b, u + 1, f)
                        if f in (2, 5) and u < 3:
                            ada_out(2 * u + f // 4)
                    dve.wait_ge(s_cmp_free[kind], b * 2 + pair + CREDIT)
                    dve.wait_ge(s_cmp_o, b * 4 + u + 1 + CREDIT)
                    if kind == 0:
                        V.tensor_copy(kc_out[:, :, :], bank[6][:, 0:2 * NC_S].rearrange("p (h c) -> p h c", h=2)).then_inc(s_cmp_ev, 1)
                    else:
                        V.tensor_copy(vc_out[:, :, :], bank[6][0:NC_S, 0:2 * P].rearrange("p (h d) -> p h d", h=2)).then_inc(s_cmp_ev, 1)

            for f in range(8):
                if f == 6:
                    dve.wait_ge(s_xsp, 16)
                keys_lo(0, 0, f)
            dve.wait_ge(s_w1_hi, 3)
            V.tensor_tensor(keyT_lo[:, :, 2 * PAST:KEYS], keyT_hi[:, :, 2 * PAST:KEYS].bitcast(F32), keyT_hi[:, :, 2 * PAST:KEYS].bitcast(F32),
                            ALU.subtract).then_inc(s_w1_lo, 1)
            with dve.Fori(0, NB - 1) as b:
                compress_dve(b, False)
            compress_dve(NB - 1, True)
            dve.wait_ge(s_ada_ev, 48 + CREDIT)
            sh1, sc1v, gt1, sh2, sc2v, gt2 = (ada[:, 16 * k:16 * k + 16, :] for k in range(6))

            def per_seq(v, k0, kn):
                return v[:, k0:k0 + kn, 1:NSEQ].unsqueeze(3).to_broadcast([P, kn, NB, NSTEP])

            def by_seq(x):
                return x.rearrange("p k (b s) -> p k b s", b=NB)

            def lo(i, per, t, ch):
                dve.wait_ge(s_hi, i * (2 * per) + 2 * t + ch + 1)
                buf = (2 * t + ch) % 4
                V.tensor_tensor(w_lo[:, buf], raw[:, (t // 2) % 2, CH * ch:CH * ch + CH, P * (t % 2):P * (t % 2) + P],
                                w_hi[:, buf].bitcast(F32), ALU.subtract).then_inc(s_lo, 1)

            def modulate(x, gain, shift, scale, n, z0, ready=None):
                seq(V.scalar_tensor_tensor(out=a_mul[:, :, :], in0=scale, scalar=1.0,
                                           in1=gain.unsqueeze(2).to_broadcast([P, KT, NSEQ]), op0=ALU.add, op1=ALU.mult))
                if ready is not None:
                    ready()

                def scaled(g):
                    k4 = slice(4 * g, 4 * g + 4)
                    h_s = sq[:, k4, NPR:NT]
                    seq(V.tensor_tensor(h_s, x[g][:, :, NPR:NT], rbc[:, NPR:NT].unsqueeze(1).to_broadcast([P, 4, NSM]), ALU.mult))
                    seq(V.tensor_tensor(by_seq(h_s), by_seq(h_s), per_seq(a_mul, 4 * g, 4), ALU.mult))
                    V.tensor_tensor(by_seq(h_s), by_seq(h_s), per_seq(shift, 4 * g, 4), ALU.add)
                    for k in range(4 * g, 4 * g + 4):
                        last = V.scalar_tensor_tensor(out=sq[:, k, 0:NPR], in0=x[g][:, k - 4 * g, 0:NPR], scalar=a_mul[:, k, 0:1],
                                                      in1=rbc[:, 0:NPR], op0=ALU.mult, op1=ALU.mult)
                    last.then_inc(s_zt, 1)

                def low(g):
                    dve.wait_ge(s_z, z0 + g + 1)
                    for k in range(4 * g, 4 * g + 4):
                        V.scalar_tensor_tensor(out=act_lo[:, k, 0:NPR], in0=sq[:, k, 0:NPR], scalar=shift[:, k, 0:1],
                                               in1=act_hi[:, k, 0:NPR].bitcast(F32), op0=ALU.add, op1=ALU.subtract)
                    k4 = slice(4 * g, 4 * g + 4)
                    V.tensor_tensor(act_lo[:, k4, NPR:NT], sq[:, k4, NPR:NT], act_hi[:, k4, NPR:NT].bitcast(F32), ALU.subtract).then_inc(s_h, 1)

                scaled(0)
                scaled(1)
                low(0)
                low(1)
                scaled(2)
                scaled(3)
                low(2)
                low(3)

            for c in range(2):
                lo(0, 4, c // 2, c % 2)
            dve.wait_ge(s_cmp_o, 4 * NB + CREDIT)
            dve.wait_ge(s_xld, 32)
            modulate([x0_a[:, 0:4, :], x0_a[:, 4:8, :], x0_a[:, 8:12, :], x0_b], g1n, sh1, sc1v, 0, 0)

            def dense_dve(t0, n, evac, per=4, last=False, outer=None, chain=0):
                def body(i, stop):
                    for j in range(per):
                        t = t0 + j
                        ahead = not (stop and j >= per - 2)
                        base = i if outer is None else outer * 8 + i
                        if ahead:
                            lo(base, 4 if outer is not None else per, t + 2, 0)
                        evac(i, j)
                        if ahead:
                            lo(base, 4 if outer is not None else per, t + 2, 1)
                times = n // per
                loops = times - 1 if last else times
                with dve.Fori(0, loops) as i:
                    step.enter(i, chain)
                    body(i, False)
                    step.leave(loops)
                if last:
                    body(times - 1, True)

            def tile_done(i, t, per=4):
                dve.wait_ge(s_chunk, i * (2 * per) + 2 * t + 2 + CREDIT)

            for c in range(2, 4):
                lo(0, 4, c // 2, c % 2)
            seq(V.memset(up_p[:, :, 0:2], 0.0))

            def ev_conv(i, j):
                kind, m = (j % 6) // 2, j % 2
                kt = i * 4 + 2 * (j // 6) + m
                ps = bank[j % 4]
                dve.wait_ge(s_ev, i * 12 + T_CONV + j + CREDIT)
                if kind == 0:
                    tile_done(i, T_CONV + j, 12)
                    V.tensor_copy(u_sb[:, m, :], ps[:, 0:NT]).then_inc(s_ev, 1)
                elif kind == 1:
                    seq(V.tensor_scalar(up_s[:, m, :, 0:2], prevT[:, :, ds(kt, 1)].rearrange("p (b j) a -> p b (j a)", j=2), 1.0, None, ALU.mult))
                    tile_done(i, T_CONV + j, 12)
                    seq(V.tensor_tensor(up_p[:, m, 2:NPR + 2], ps[:, 0:NPR], u_sb[:, m, 0:NPR], ALU.mult))
                    V.tensor_tensor(up_s[:, m, :, 2:NSTEP + 2], ps[:, NPR:NT].rearrange("p (b s) -> p b s", b=NB),
                                    u_sb[:, m, NPR:NT].rearrange("p (b s) -> p b s", b=NB), ALU.mult).then_inc(s_ev, 1)
                    dve.wait_ge(s_ev, i * 12 + T_CONV + j + 1 + CREDIT)
                    seq(V.tensor_scalar(cstate[:, ds(kt, 1), 0:2], up_p[:, m, NPR:NPR + 2].unsqueeze(1), 1.0, None, ALU.mult))
                    seq(V.tensor_scalar(cstate[:, ds(kt, 1), 2:2 * NSEQ].rearrange("p a (b j) -> p (a b) j", j=2),
                                        up_s[:, m, :, NSTEP:NSTEP + 2], 1.0, None, ALU.mult))
                else:
                    y_p = y_sb[:, m, 0:NPR]
                    y_s = y_sb[:, m, NPR:NT].rearrange("p (b s) -> p b s", b=NB)
                    w = [v[:, ds(kt, 1)] for v in cvw]
                    seq(V.tensor_scalar(y_p, up_p[:, m, 0:NPR], w[0], cvb[:, ds(kt, 1)], ALU.mult, ALU.add))
                    seq(V.tensor_scalar(y_s, up_s[:, m, :, 0:NSTEP], w[0], cvb[:, ds(kt, 1)], ALU.mult, ALU.add))
                    for r in (1, 2):
                        seq(V.scalar_tensor_tensor(out=y_p, in0=up_p[:, m, r:NPR + r], scalar=w[r], in1=y_p, op0=ALU.mult, op1=ALU.add))
                        seq(V.scalar_tensor_tensor(out=y_s, in0=up_s[:, m, :, r:NSTEP + r], scalar=w[r], in1=y_s, op0=ALU.mult, op1=ALU.add))
                    dve.wait_ge(s_z, i * 4 + 4 + 2 * (j // 6))
                    tile_done(i, T_CONV + j, 12)
                    V.tensor_tensor(z_sb[:, m, :], y_sb[:, m, :], ps[:, 0:NT], ALU.mult).then_inc(s_ev, 1)
                    dve.wait_ge(s_z, i * 4 + 4 + 2 * (j // 6) + m + 1)
                    V.tensor_tensor(z_lo[:, ds(kt, 1), :], z_sb[:, m, :].unsqueeze(1), z_hi[:, ds(kt, 1), :].bitcast(F32), ALU.subtract).then_inc(s_zl, 1)

            dense_dve(T_CONV, 48, ev_conv, per=12, chain=40)
            dense_dve(T_MC, 16, lambda i, j: None)

            def ev_wc(i, j):
                tile_done(i, T_WC + j)
                kt = ds(i * 4 + j, 1)
                V.tensor_tensor(mx[:, kt, :], mx[:, kt, :], bank[j][:, 0:NT].unsqueeze(1), ALU.mult).then_inc(s_ev, 1)

            dve.wait_ge(s_ev, T_WC + CREDIT)
            dense_dve(T_WC, 16, ev_wc)
            dense_dve(T_MA, 16, lambda i, j: None)
            dve.wait_ge(s_gate, 1)
            V.tensor_tensor(gw_lo[:, :, :], gw[:, :, :], gw_hi[:, :, :].bitcast(F32), ALU.subtract).then_inc(s_gate, 1)
            dve.wait_ge(s_gate, 4)
            V.tensor_copy(gTs[:, :, :], gT[:, NPR:NT].rearrange("p (b s) -> p s b", b=NB)).then_inc(s_gate, 1)
            dve.wait_ge(s_gate, 6)
            V.tensor_copy(gate_p[:, :, :], bank[6][:, 0:P].rearrange("p (q c) -> p q c", q=2)[:, :, 0:48]).then_inc(s_gate, 1)
            dense_dve(T_Q, 16, lambda i, j: None)
            dense_dve(T_KV, 24, lambda i, j: None, last=True)

            dve.wait_ge(s_pool, POOL_STEPS)
            seq(V.tensor_tensor(selw[:, :], selw[:, :], sc1[:, :], ALU.add))
            seq(V.tensor_copy(colf[:, :], coli[:, :]))
            seq(V.tensor_scalar(rowi[:, 1:2], rowi[:, 0:1], 7, None, ALU.bitwise_and))
            seq(V.tensor_scalar(rowi[:, 2:3], rowi[:, 0:1], 5, 3, ALU.logical_shift_right, ALU.logical_shift_left))
            seq(V.tensor_copy(rowf[:, 0:3], rowi[:, 0:3]))
            seq(V.tensor_tensor(rowf[:, 3:4], rowf[:, 1:2], rowf[:, 2:3], ALU.add))
            seq(V.tensor_scalar(rowf[:, 2:3], rowf[:, 1:2], float(WIN), None, ALU.add))
            seq(V.tensor_scalar(mask_w[:, :], colf[:, :], rowf[:, 1:2], NEG, ALU.is_le, ALU.mult))
            seq(V.tensor_scalar(mask_n[:, :], colf[:, 0:NSTEP], rowf[:, 1:2], NEG, ALU.is_gt, ALU.mult))
            seq(V.tensor_scalar(coli[:, P:2 * P], coli[:, 0:P], 5, 3, ALU.logical_shift_right, ALU.logical_shift_left))
            seq(V.tensor_scalar(coli[:, 0:P], coli[:, 0:P], 7, None, ALU.bitwise_and))
            seq(V.tensor_copy(grpf[:, :], coli[:, 0:P]))
            seq(V.tensor_copy(grp[:, :], coli[:, P:2 * P]))
            seq(V.tensor_tensor(grpf[:, :], grpf[:, :], grp[:, :], ALU.add))
            seq(V.tensor_scalar(grp[:, :], grpf[:, :], rowf[:, 3:4], None, ALU.is_equal))
            seq(V.tensor_copy(mask_w[:, WIN:WIN + NSTEP], mask_n[:, :]))
            dve.wait_ge(s_pe, 3)
            V.tensor_copy(kc_p[:, :, :], bank[4][:, 0:NKV * NC_P].rearrange("p (h c) -> p h c", h=NKV)).then_inc(s_cpp, 1)
            dve.wait_ge(s_pe, 4)
            V.tensor_copy(vc_p[:, :, :], bank[5][0:NC_P, :].rearrange("p (h d) -> p h d", h=NKV)).then_inc(s_cpp, 1)
            dve.wait_ge(s_cpp, 2)
            dve.wait_ge(s_pool, 10)

            def bundle(h):
                V.tensor_scalar(q_b[:, :, :], qo[:, ds(h * GRP, GRP), 0:NPR], 1.0, None, ALU.mult).then_inc(s_bun, 1)
                V.tensor_scalar(kc_b[:, :], kc_p[:, ds(h, 1), :].rearrange("p a c -> p (a c)"), 1.0, None, ALU.mult).then_inc(s_bun, 1)
                V.tensor_scalar(kv_b[:, :, :], kv[:, :, :].rearrange("p (k h) t -> p k h t", h=NKV)[:, :, ds(h, 1), :].rearrange("p k a t -> p k (a t)"),
                                1.0, None, ALU.mult).then_inc(s_bun, 1)

            bundle(0)

            def prompt_head(h, last):
                dve.wait_ge(s_pv, h * 8 + CREDIT)
                for qt in range(2):
                    gates = V.tensor_scalar(gate_b[:, :, :, qt], gate_p[:, qt, :].rearrange("p (r h) -> p r h", r=3)[:, :, ds(h * GRP, GRP)],
                                            1.0, None, ALU.mult)
                    if qt == 0:
                        seq(gates)
                    else:
                        gates.then_inc(s_vcb, 1)
                V.tensor_scalar(vc_b[:, :], vc_p[:, ds(h, 1), :].rearrange("p a c -> p (a c)"), 1.0, None, ALU.mult).then_inc(s_vcb, 1)
                dve.wait_ge(s_sc, h * 9 + 1)
                V.tensor_tensor(S_c[:, :, :].rearrange("p (g q) c -> p g q c", q=2),
                                bank[7][:, 0:P].rearrange("p (g q c) -> p g q c", g=GRP, q=2)[:, :, :, 0:NC_P],
                                mask_c[:, :, :].unsqueeze(1).to_broadcast([P, GRP, 2, NC_P]), ALU.add).then_inc(s_scev, 1)
                dve.wait_ge(s_scev, h * 18 + 1 + CREDIT)
                seq(V.tensor_reduce(mxp[:, :, 0], S_c[:, :, :], AX.X, ALU.max))
                V.tensor_scalar(nmp[:, :, 0], mxp[:, :, 0], -SCALE, -0.01 * NEG, ALU.mult, ALU.min).then_inc(s_scev, 1)
                for u in range(8):
                    qt = u % 2
                    nk = P * (qt + 1)
                    dve.wait_ge(s_sc, h * 9 + 1 + u + 1)
                    V.tensor_tensor(S_p[:, u, :, 0:nk], bank[2 + u % 4][:, :].rearrange("p (r k) -> p r k", r=2)[:, :, 0:nk],
                                    mask_p[:, qt:qt + 1, 0:nk].to_broadcast([P, 2, nk]), ALU.add).then_inc(s_scev, 1)
                    dve.wait_ge(s_scev, h * 18 + 2 * u + 3 + CREDIT)
                    seq(V.tensor_reduce(mxp[:, u, 1:3], S_p[:, u, :, 0:nk], AX.X, ALU.max))
                    V.tensor_scalar(nmp[:, u, 1:3], mxp[:, u, 1:3], -SCALE, None, ALU.mult).then_inc(s_scev, 1)
                if not last:
                    dve.wait_ge(s_rtr, h * 6 + 6)
                    bundle(h + 1)
                dve.wait_ge(s_exp, h * 24 + 24)
                dve.wait_ge(s_vcb, h * 2 + 2)
                seq(V.tensor_scalar(den[:, :, :], den[:, :, :], 1e-30, None, ALU.max))
                seq(V.reciprocal(rr[:, :, :], den[:, :, :]))
                seq(V.tensor_tensor(rr[:, :, :].rearrange("p (g q) r -> p g q r", q=2), rr[:, :, :].rearrange("p (g q) r -> p g q r", q=2),
                                    gate_b[:, :, :, :].rearrange("p r g q -> p g q r"), ALU.mult))
                seq(V.tensor_tensor(rr[:, :, 0].rearrange("p (g q) -> p g q", q=2), rr[:, :, 0].rearrange("p (g q) -> p g q", q=2),
                                    vis[:, :].unsqueeze(1).to_broadcast([P, GRP, 2]), ALU.mult))

                def store(w):
                    dve.wait_ge(s_otr, h * 8 + w + 1)
                    V.tensor_scalar(qo[:, ds(h * GRP + w // 2, 1), P * (w % 2):P * (w % 2) + P],
                                    bank[7 - w % 2][:, 0:P].unsqueeze(1), 1.0, None, ALU.mult).then_inc(s_oev, 1)

                for u in range(8):
                    o = bank[2 + u % 4]
                    dve.wait_ge(s_pv, h * 8 + u + 1 + CREDIT)
                    if u >= 2:
                        dve.wait_ge(s_otr, h * 8 + u - 1)
                    seq(V.tensor_scalar(o_row[:, u % 2, :], o[:, 0:P], rr[:, u, 0:1], None, ALU.mult))
                    seq(V.scalar_tensor_tensor(out=o_row[:, u % 2, :], in0=o[:, P:2 * P], scalar=rr[:, u, 1:2], in1=o_row[:, u % 2, :],
                                               op0=ALU.mult, op1=ALU.add))
                    V.scalar_tensor_tensor(out=o_row[:, u % 2, :], in0=o[:, 2 * P:3 * P], scalar=rr[:, u, 2:3], in1=o_row[:, u % 2, :],
                                           op0=ALU.mult, op1=ALU.add).then_inc(s_orow, 1)
                    if u >= 1:
                        store(u - 1)
                store(7)

            with dve.Fori(0, NKV - 1) as h:
                step.enter(h, 30)
                prompt_head(h, False)
                step.leave(NKV - 1)
            prompt_head(NKV - 1, True)

            dve.wait_ge(s_gdma, 32)
            V.tensor_copy(rowf[:, 0:1], rowf[:, 1:2]).then_inc(s_sel, 1)
            dve.wait_ge(s_sel, 1)
            dve.wait_ge(s_rowdma, 16 * NKV * (5 + NB))
            V.tensor_copy(k_new_all[:, :, :], kv[:, 8:24, NPR:NT]).then_inc(s_kall, 1)
            dve.wait_ge(s_kall, 1)

            def new_rows(n, par):
                V.tensor_scalar(q_s[par][:, :].rearrange("p (h s) -> p h s", h=NH), qo[:, :, ds(n * NSTEP + NPR, NSTEP)], 1.0, None, ALU.mult).then_inc(s_new, 1)
                V.tensor_scalar(knew[par][:, :, :], k_new_all[:, :, ds(n * NSTEP, NSTEP)], 1.0, None, ALU.mult).then_inc(s_new, 1)

            new_rows(0, 0)

            def sample_dve(b, n, par, more):
                bst, nst = st2[1 - par], st2[par]

                def keys_out(pc):
                    for hd in range(1, NKV, 2):
                        dve.wait_ge(s_ktr, n * 20 + 4 * pc + hd + 1 + 2 * CREDIT)
                        dve.wait_ge(s_ssc, n * 6 + (pc if pc >= 2 else 0) + CREDIT)
                        V.tensor_copy(kT[:, pc % 2, hd, :], bank[1][:, :]).then_inc(s_ktev[1], 1)

                def scores_out(pc):
                    dve.wait_ge(s_ssc, n * 6 + 1 + pc + 1 + CREDIT)
                    if pc < 4:
                        V.tensor_tensor(S_s[:, 512 * pc:512 * pc + 512].rearrange("p (n k) -> p n k", k=SLC),
                                        bank[2 + pc % 2][:, :].rearrange("p (n k) -> p n k", k=SLC),
                                        selb[:, 8 * pc:8 * pc + 8].unsqueeze(2).to_broadcast([P, 8, SLC]), ALU.add).then_inc(s_sev, 1)
                    else:
                        V.tensor_tensor(W_s[:, 0:WIN], bank[2][:, :], mask_w[:, 0:WIN], ALU.add).then_inc(s_sev, 1)

                def bias(br):
                    w = (S_s, W_s)[br]
                    seq(V.tensor_reduce(bst[:, 1 + br:2 + br], w[:, :], AX.X, ALU.max))
                    V.tensor_scalar(bst[:, 4 + br:5 + br], bst[:, 1 + br:2 + br], -SCALE, None, ALU.mult).then_inc(s_sm, 1)

                if b is not None:
                    dve.wait_ge(s_sev, b * 5 + 5 + CREDIT)
                    bias(0)
                if n is not None:
                    keys_out(0)
                    dve.wait_ge(s_ssc, n * 6 + 1 + CREDIT)
                    V.tensor_reduce(nst[:, 0:1], bank[4][:, 0:NC_S], AX.X, ALU.max).then_inc(s_sel, 1)
                    dve.wait_ge(s_sel, n * 12 + 2)
                    V.tensor_scalar(nst[:, 3:4], nst[:, 0:1], -SCALE, None, ALU.mult).then_inc(s_sel, 1)
                if b is not None:
                    bias(1)
                if n is not None:
                    keys_out(1)
                    dve.wait_ge(s_vnt, n + 1)
                    for br in range(2):
                        V.tensor_copy(vnew[par][:, br, :], bank[6 + br][0:NSTEP, :]).then_inc(s_vne, 1)
                    dve.wait_ge(s_cexp, n * 2 + 1)
                    V.reciprocal(nst[:, 9:10], nst[:, 6:7]).then_inc(s_sel, 1)
                    dve.wait_ge(s_sel, n * 12 + 4)
                    dve.wait_ge(s_selp, n * 3 + 2)
                    V.tensor_scalar(z_s[:, :], bank[7][:, P:P + NSB], nst[:, 9:10], None, ALU.mult).then_inc(s_sel, 1)
                if b is not None:
                    for f in range(1, 6, 2):
                        dve.wait_ge(s_ptr, b * 6 + f + 1)
                        if f < 5:
                            V.tensor_copy(PTs[:, 4 * f:4 * f + 4, :], bank[1][:, :].rearrange("p (k q) -> p k q", q=P)).then_inc(s_ktev[1], 1)
                        else:
                            V.tensor_copy(PTn[:, :, :], bank[1][0:NSTEP, 0:2 * P].rearrange("p (k q) -> p k q", q=P)).then_inc(s_ktev[1], 1)
                if n is not None:
                    seq(V.tensor_tensor(S_s[:, PAST:PAST + NSTEP], bank[4][:, P:P + NSTEP], mask_n[:, :], ALU.add))
                    seq(V.tensor_tensor(W_s[:, WIN:WIN + NSTEP], bank[4][:, P + NSTEP:P + 2 * NSTEP], mask_n[:, :], ALU.add))
                    dve.wait_ge(s_selp, n * 3 + 3)
                    picks = [
                        lambda: V.tensor_copy(sc1[:, :], bank[7][:, 192:192 + NSB]),
                        lambda: V.memset(sc1[:, 0:1], -NEG),
                        lambda: V.memset(sc1[:, NSB - 2:NSB], -NEG),
                        lambda: V.max(top8[:, :], sc1[:, :]),
                        lambda: V.match_replace(sc2[:, :], top8[:, :], sc1[:, :], NEG),
                        lambda: V.max(top8[:, :], sc2[:, :]),
                        lambda: V.match_replace(sc1[:, :], top8[:, :], sc2[:, :], NEG),
                        lambda: V.tensor_scalar(selb[:, :], sc1[:, :], 0.5 * NEG, NEG, ALU.is_gt, ALU.mult),
                    ]
                    for k, pick in enumerate(picks):
                        dve.wait_ge(s_sel, n * 12 + 5 + k)
                        dve.sem_inc(s_pass[0], 1)
                        pick().then_inc(s_sel, 1)
                    dve.wait_ge(s_sel, n * 12 + 13)
                if b is not None:
                    dve.wait_ge(s_sexp, b * 2 + 2)
                    seq(V.reciprocal(bst[:, 9:12], bst[:, 6:9]))
                    seq(V.tensor_tensor(bst[:, 9:12], bst[:, 9:12], gate_s[:, :, ds(b, 1)].rearrange("p r a -> p (r a)"), ALU.mult))
                    dve.wait_ge(s_spv, b * 5 + 5 + 2 * CREDIT)
                    V.tensor_scalar(os_row[:, :], bank[5][:, 0:P], bst[:, 9:10], None, ALU.mult).then_inc(s_sm, 1)
                    for br in (1, 2):
                        dve.wait_ge(s_sm, b * 5 + 2 + br)
                        V.scalar_tensor_tensor(out=os_row[:, :], in0=bank[5][:, P * br:P * br + P], scalar=bst[:, 9 + br:10 + br], in1=os_row[:, :],
                                               op0=ALU.mult, op1=ALU.add).then_inc(s_sm, 1)
                if n is not None:
                    keys_out(2)
                    scores_out(0)
                if b is not None:
                    dve.wait_ge(s_sot, b + 1)
                    V.tensor_scalar(qo[:, :, ds(b * NSTEP + NPR, NSTEP)], bank[6][:, 0:P].rearrange("p (h s) -> p h s", h=NH), 1.0, None,
                                    ALU.mult).then_inc(s_so, 1)
                if n is not None:
                    keys_out(3)
                    scores_out(1)
                    keys_out(4)
                    scores_out(2)
                    if more:
                        new_rows(n + 1, 1 - par)
                    scores_out(3)
                    scores_out(4)

            def sample_dve_steps():
                sample_dve(None, 0, 0, True)
                with dve.Fori(0, NB // 2 - 1) as i:
                    step.enter(i, 12)
                    sample_dve(i * 2, i * 2 + 1, 1, True)
                    sample_dve(i * 2 + 1, i * 2 + 2, 0, True)
                    step.leave(NB // 2 - 1)
                sample_dve(NB - 2, NB - 1, 1, False)
                sample_dve(NB - 1, None, 0, False)

            sample_dve_steps()

            for g in range(4):
                if g == 3:
                    for c in range(2):
                        lo(0, 4, T_WA, c)
                dve.wait_ge(s_z, 20 + g + 1)
                k4 = slice(4 * g, 4 * g + 4)
                V.tensor_tensor(act_lo[:, k4, :], qo[:, k4, :], act_hi[:, k4, :].bitcast(F32), ALU.subtract).then_inc(s_h, 1)
            for c in range(2):
                lo(0, 4, T_WA + 1, c)

            def ev_wa(i, j):
                kt = ds(i * 4 + j, 1)
                tile_done(i, T_WA + j)
                V.tensor_tensor(ga[:, kt, :], ga[:, kt, :], bank[j][:, 0:NT].unsqueeze(1), ALU.mult).then_inc(s_ev, 1)
                dve.wait_ge(s_ev, i * 4 + T_WA + j + 1 + CREDIT)
                V.tensor_tensor(mx[:, kt, :], mx[:, kt, :], ga[:, kt, :], ALU.add).then_inc(s_m, 1)
                dve.wait_ge(s_z, i * 4 + j + 25)
                V.tensor_tensor(mx_lo[:, kt, :], mx[:, kt, :], mx_hi[:, kt, :].bitcast(F32), ALU.subtract).then_inc(s_h, 1)

            dense_dve(T_WA, 16, ev_wa)
            dve.wait_ge(s_m, 16)

            def ev_add(gate, t0, outer=None):
                def ev(i, j):
                    kt = ds(i * 4 + j, 1)
                    if outer is None:
                        tile_done(i, t0 + j)
                    else:
                        dve.wait_ge(s_chunk, outer * 64 + i * 8 + 2 * (t0 + j) + 2 + CREDIT)
                    seq(V.tensor_tensor(tmp_s[:, :].rearrange("p (b s) -> p b s", b=NB), bank[j][:, NPR:NT].rearrange("p (b s) -> p b s", b=NB),
                                        gate[:, kt, 1:NSEQ].rearrange("p a b -> p (a b)").unsqueeze(2).to_broadcast([P, NB, NSTEP]), ALU.mult))
                    V.scalar_tensor_tensor(out=x1[:, kt, 0:NPR], in0=bank[j][:, 0:NPR].unsqueeze(1), scalar=gate[:, kt, 0:1].rearrange("p a c -> p (a c)"),
                                           in1=x1[:, kt, 0:NPR], op0=ALU.mult, op1=ALU.add).then_inc(s_ev, 1)
                    V.tensor_tensor(x1[:, kt, NPR:NT], x1[:, kt, NPR:NT], tmp_s[:, :].unsqueeze(1), ALU.add).then_inc(s_xadd, 1)
                    dve.wait_ge(s_xadd, (i * 4 if outer is None else outer * 16 + i * 4 + 16) + j + 1)
                return ev

            V.memset(sqt[:, 3, :], 0.0).then_inc(s_zero, 1)
            dve.wait_ge(s_xld1, 16)
            dense_dve(T_WO, 16, ev_add(gt1, T_WO), chain=4)
            modulate([x1[:, 4 * g:4 * g + 4, :] for g in range(4)], g2n, sh2, sc2v, 1, 40, ready=lambda: rstd(1))

            def mlp(f, last):
                def ev_hidden(i, j):
                    n = f * 16 + i * 4 + j + 1
                    dve.wait_ge(s_hidh, n)
                    seq(V.tensor_tensor(rl2[:, j, :], rl[:, j, :], rl[:, j, :], ALU.mult))
                    V.tensor_tensor(hid_lo[:, ds(i * 4 + j, 1), :], rl2[:, j, :].unsqueeze(1), hid_hi[:, ds(i * 4 + j, 1), :].bitcast(F32),
                                    ALU.subtract).then_inc(s_hid, 1)
                dense_dve(T_MLP, 16, ev_hidden, outer=f, chain=4)
                if last:
                    V.memset(sqt[:, 3, :], 0.0).then_inc(s_zero, 1)
                dense_dve(T_MLP + 16, 16, ev_add(gt2, T_MLP + 16, outer=f), outer=f, last=last, chain=4)

            with dve.Fori(0, 3) as f:
                step.enter(f, 32)
                mlp(f, False)
                step.leave(3)
            mlp(3, True)
            rstd(2)
            for g in range(4):
                for k in range(4 * g, 4 * g + 4):
                    last = V.scalar_tensor_tensor(out=sq[:, k, :], in0=x1[:, k, :], scalar=gfn[:, k:k + 1], in1=rbc[:, :],
                                                  op0=ALU.mult, op1=ALU.mult)
                last.then_inc(s_zt, 1)
            for f in range(1, 12, 2):
                tt, g = f // 4, f % 4
                n = P if tt < 2 else NSM
                dve.wait_ge(s_ftr, 4 + f + 1)
                if tt == 2:
                    dve.wait_ge(s_out, 32)
                V.tensor_copy(y_rows[0:n, tt % 2, 512 * g:512 * g + 512], bank[f % 4][0:n, :]).then_inc(s_fev[1], 1)


_INS = ["x_prompt", "x_sample", "c_prompt", "c_sample", "cache_nsa_kv", "page_table", "state_win_kv", "state_conv",
        "w_ada", "b_ada", "norm1_g", "norm2_g", "w_in", "w_cmp_k1", "w_cmp_k2", "pe_cmp_k", "w_cmp_v1", "w_cmp_v2", "pe_cmp_v",
        "conv_w", "conv_b", "w_attn_proj", "w_conv_proj", "w_out", "w_mlp1", "w_mlp2", "normf_g"]
_OUTS = [("y_prompt", (1, 256, 2048)), ("y_sample", (8, 8, 2048)), ("kv_prompt", (1, 1, 256, 4, 4, 128)),
         ("kv_sample", (1, 8, 8, 4, 4, 128)), ("win_prompt", (1, 1, 256, 2, 4, 128)), ("win_sample", (1, 8, 512, 2, 4, 128)),
         ("conv_prompt", (1, 1, 2, 2048)), ("conv_sample", (1, 8, 2, 2048))]


def kernel(**inputs):
    import numpy as _np
    import concourse.bacc as _bacc
    from concourse import mybir as _mybir
    from concourse.bass_utils import run_bass_kernel_spmd as _run

    nc = _bacc.Bacc("TRN2", target_bir_lowering=False, num_devices=1)
    arrays, A = {}, {}
    for name in _INS:
        a = _np.ascontiguousarray(inputs[name])
        arrays[f"in_{name}"] = a
        A[name] = nc.dram_tensor(f"in_{name}", a.shape, _mybir.dt.from_np(a.dtype), kind="ExternalInput").ap()
    for name, shape in _OUTS:
        A[f"out_{name}"] = nc.dram_tensor(f"res_{name}", shape, _mybir.dt.float32, kind="ExternalOutput").ap()
    build_step(nc, A)
    r = _run(nc, [arrays], core_ids=[0])
    return tuple(r.results[0][f"res_{name}"] for name, _ in _OUTS)
```
